# Optimizing a Trainium2 kernel written in Bass

```python
import math
import jax, jax.numpy as jnp
from jax import lax
import numpy as np

D_MODEL = 1024
BATCH = 1
SEQ = 2048
DEPTH = 1
DEC_BATCH = 8
DEC_SEQ = 4
PAST_LEN = 8192
PAGE_SIZE = 128

HEAD_DIM = 64
N_HEADS_A = (D_MODEL // 2) // HEAD_DIM
N_HEADS_B = (D_MODEL // 2) // (2 * HEAD_DIM)
DILATED_BRANCHES = ((128, 1), (512, 4), (2048, 16))
MAX_WINDOW = max(w for w, _ in DILATED_BRANCHES)
ROT_DIM = HEAD_DIM // 4
ROPE_THETA = 500000.0
D_FF = 4 * D_MODEL
Q_BLOCK = 128
RMS_EPS = 1e-6
SUBLN_EPS = 1e-5
WIDTH_A = N_HEADS_A * HEAD_DIM
WIDTH_B_QK = N_HEADS_B * 2 * HEAD_DIM
WIDTH_B_V = N_HEADS_B * 2 * HEAD_DIM
D_IN = 3 * WIDTH_A + 2 * WIDTH_B_QK + WIDTH_B_V
D_MIX = WIDTH_A + WIDTH_B_V

kernel_name = "hybrid_dilated_diff_attn_decoder_step"

def rmsnorm(x, g, eps=RMS_EPS):
    xf = x.astype(jnp.float32)
    y = xf * lax.rsqrt(jnp.mean(xf * xf, axis=-1, keepdims=True) + eps)
    return (y * g.astype(jnp.float32)).astype(x.dtype)

def rope(x, pos):
    half = ROT_DIM // 2
    inv = ROPE_THETA ** (-jnp.arange(half, dtype=jnp.float32) * 2.0 / ROT_DIM)
    ang = pos.astype(jnp.float32)[:, None] * inv[None, :]
    shape = (1, pos.shape[0]) + (1,) * (x.ndim - 3) + (half,)
    cos = jnp.cos(ang).reshape(shape)
    sin = jnp.sin(ang).reshape(shape)
    xr = x[..., :ROT_DIM].astype(jnp.float32)
    x1, x2 = xr[..., :half], xr[..., half:]
    rot = jnp.concatenate([x1 * cos - x2 * sin, x2 * cos + x1 * sin], axis=-1).astype(x.dtype)
    return jnp.concatenate([rot, x[..., ROT_DIM:]], axis=-1)

def project_qkv(hn, w_in, pos):
    n, t, _ = hn.shape
    z = hn @ w_in
    cuts = [WIDTH_A, 2 * WIDTH_A, 3 * WIDTH_A, 3 * WIDTH_A + WIDTH_B_QK, 3 * WIDTH_A + 2 * WIDTH_B_QK]
    qa, ka, va, qb, kb, vb = jnp.split(z, cuts, axis=-1)
    qa = rope(qa.reshape(n, t, N_HEADS_A, HEAD_DIM), pos)
    ka = rope(ka.reshape(n, t, N_HEADS_A, HEAD_DIM), pos)
    va = va.reshape(n, t, N_HEADS_A, HEAD_DIM)
    qb = rope(qb.reshape(n, t, N_HEADS_B, 2, HEAD_DIM), pos)
    kb = rope(kb.reshape(n, t, N_HEADS_B, 2, HEAD_DIM), pos)
    vb = vb.reshape(n, t, N_HEADS_B, 2 * HEAD_DIM)
    return qa, ka, va, qb, kb, vb

def softmax_parts(s, valid):
    s = jnp.where(valid, s, -jnp.inf)
    m = jnp.max(s, axis=-1, keepdims=True)
    p = jnp.exp(s - m)
    return p, m, jnp.sum(p, axis=-1, keepdims=True)

def dilated_branch_prompt(q, k, v, window, dil):
    b, s_len, h, e = q.shape
    w = window // dil
    length = s_len // dil
    nb = -(-length // w)
    lp = nb * w

    def to_blocks(a):
        a = a.reshape(b, length, dil, h, e).transpose(0, 2, 1, 3, 4)
        a = jnp.pad(a, ((0, 0), (0, 0), (0, lp - length), (0, 0), (0, 0)))
        return a.reshape(b, dil, nb, w, h, e)

    def with_prev(a):
        prev = jnp.pad(a[:, :, :-1], ((0, 0), (0, 0), (1, 0), (0, 0), (0, 0), (0, 0)))
        return jnp.concatenate([prev, a], axis=3)

    qb = to_blocks(q)
    kk = with_prev(to_blocks(k))
    vv = with_prev(to_blocks(v))
    sc = jnp.einsum('brnqhe,brnkhe->brnhqk', qb, kk).astype(jnp.float32) * (e ** -0.5)
    i = jnp.arange(w)[:, None]
    j = jnp.arange(2 * w)[None, :]
    dist = w + i - j
    blk = jnp.arange(nb)[:, None, None]
    valid = (dist >= 0) & (dist <= w) & ((blk > 0) | (j >= w))
    p, m, l = softmax_parts(sc, valid[:, None])
    o = jnp.einsum('brnhqk,brnkhe->brnqhe', p, vv.astype(jnp.float32)) / jnp.swapaxes(l, 3, 4)
    m = jnp.swapaxes(m[..., 0], 3, 4)
    l = jnp.swapaxes(l[..., 0], 3, 4)

    def from_blocks(a):
        rest = a.shape[5:]
        a = a.reshape((b, dil, lp, h) + rest)[:, :, :length]
        return jnp.swapaxes(a, 1, 2).reshape((b, s_len, h) + rest)

    return from_blocks(o), from_blocks(m), from_blocks(l)

def dilated_branch_sample(q, k_all, v_all, window, dil):
    n, t, h, e = q.shape
    lb = k_all.shape[1] - t
    n_keys = window // dil + 1
    idx = (lb + jnp.arange(t))[:, None] - dil * jnp.arange(n_keys)[None, :]
    valid = idx >= 0
    idx = jnp.maximum(idx, 0)
    kg = k_all[:, idx]
    vg = v_all[:, idx]
    sc = jnp.einsum('nthe,ntjhe->nthj', q, kg).astype(jnp.float32) * (e ** -0.5)
    p, m, l = softmax_parts(sc, valid[None, :, None, :])
    o = jnp.einsum('nthj,ntjhe->nthe', p, vg.astype(jnp.float32)) / l
    return o, m[..., 0], l[..., 0]

def combine_branches(parts):
    mx = parts[0][1]
    for _, m, _ in parts[1:]:
        mx = jnp.maximum(mx, m)
    num = None
    den = None
    for o, m, l in parts:
        c = jnp.exp(m - mx) * l
        num = c[..., None] * o if num is None else num + c[..., None] * o
        den = c if den is None else den + c
    return num / den[..., None]

def diff_attention_core(q, k, v, valid, lam):
    e = q.shape[-1]
    sc = jnp.einsum('nqhce,nkhce->nhcqk', q, k).astype(jnp.float32) * (e ** -0.5)
    a = jax.nn.softmax(jnp.where(valid, sc, -jnp.inf), axis=-1)
    wts = a[:, :, 0] - lam * a[:, :, 1]
    return jnp.einsum('nhqk,nkhe->nqhe', wts, v.astype(jnp.float32))

def diff_attention_prompt(q, k, v, lam):
    b, s_len = q.shape[:2]
    nb = s_len // Q_BLOCK
    kpos = jnp.arange(s_len)

    def block(n):
        qn = lax.dynamic_slice_in_dim(q, n * Q_BLOCK, Q_BLOCK, axis=1)
        qpos = n * Q_BLOCK + jnp.arange(Q_BLOCK)
        return diff_attention_core(qn, k, v, kpos[None, :] <= qpos[:, None], lam)

    o = lax.map(block, jnp.arange(nb))
    return jnp.swapaxes(o, 0, 1).reshape(b, s_len, N_HEADS_B, 2 * HEAD_DIM)

def diff_attention_sample(q, k_new, v_new, cache_k, cache_v, page_table, lam):
    n, t = q.shape[:2]
    kp = cache_k[page_table].reshape(n, -1, N_HEADS_B, 2, HEAD_DIM).astype(k_new.dtype)
    vp = cache_v[page_table].reshape(n, -1, N_HEADS_B, 2 * HEAD_DIM).astype(v_new.dtype)
    past = kp.shape[1]
    k_all = jnp.concatenate([kp, k_new], axis=1)
    v_all = jnp.concatenate([vp, v_new], axis=1)
    kidx = jnp.arange(past + t)[None, :]
    valid = (kidx < past) | ((kidx - past) <= jnp.arange(t)[:, None])
    return diff_attention_core(q, k_all, v_all, valid, lam)

def diff_head_norm(o, g, lambda_init):
    return rmsnorm(o, g, SUBLN_EPS) * (1.0 - lambda_init)

def mlp_sublayer(h, g, w_up, w_down):
    u = rmsnorm(h, g) @ w_up
    return h + jnp.square(jax.nn.relu(u)) @ w_down

def setup_inputs(seed: int = 0) -> dict:
    key = jax.random.key(seed)
    ks = jax.random.split(key, 24)
    f32 = jnp.float32
    n_pages = PAST_LEN // PAGE_SIZE
    n_phys = (5 * DEC_BATCH * n_pages + 3) // 4
    win_buf = min(MAX_WINDOW, PAST_LEN)

    def nrm(k, shape, scale=1.0):
        return jax.random.normal(k, shape, f32) * scale

    page_table = jax.random.permutation(ks[6], n_phys)[:DEC_BATCH * n_pages]
    page_table = page_table.reshape(DEC_BATCH, n_pages).astype(jnp.int32)
    return {
        "x_prompt": nrm(ks[0], (BATCH, SEQ, D_MODEL)),
        "x_sample": nrm(ks[1], (DEC_BATCH, DEC_SEQ, D_MODEL)),
        "state_win_k": nrm(ks[2], (DEPTH, DEC_BATCH, win_buf, N_HEADS_A, HEAD_DIM)),
        "state_win_v": nrm(ks[3], (DEPTH, DEC_BATCH, win_buf, N_HEADS_A, HEAD_DIM)),
        "cache_diff_k": nrm(ks[4], (DEPTH, n_phys, PAGE_SIZE, N_HEADS_B, 2 * HEAD_DIM)),
        "cache_diff_v": nrm(ks[5], (DEPTH, n_phys, PAGE_SIZE, N_HEADS_B, 2 * HEAD_DIM)),
        "page_table": page_table,
        "norm_attn": 1.0 + nrm(ks[7], (DEPTH, D_MODEL), 0.01),
        "w_in": nrm(ks[8], (DEPTH, D_MODEL, D_IN), D_MODEL ** -0.5),
        "lambda_q1": nrm(ks[9], (DEPTH, HEAD_DIM), 0.1),
        "lambda_k1": nrm(ks[10], (DEPTH, HEAD_DIM), 0.1),
        "lambda_q2": nrm(ks[11], (DEPTH, HEAD_DIM), 0.1),
        "lambda_k2": nrm(ks[12], (DEPTH, HEAD_DIM), 0.1),
        "subln_gain": 1.0 + nrm(ks[13], (DEPTH, 2 * HEAD_DIM), 0.01),
        "w_out": nrm(ks[14], (DEPTH, D_MIX, D_MODEL), D_MIX ** -0.5),
        "norm_mlp": 1.0 + nrm(ks[15], (DEPTH, D_MODEL), 0.01),
        "w_up": nrm(ks[16], (DEPTH, D_MODEL, D_FF), D_MODEL ** -0.5),
        "w_down": nrm(ks[17], (DEPTH, D_FF, D_MODEL), D_FF ** -0.5),
        "final_norm": 1.0 + nrm(ks[18], (D_MODEL,), 0.01),
    }

def reference(x_prompt, x_sample, state_win_k, state_win_v, cache_diff_k, cache_diff_v, page_table,
              norm_attn, w_in, lambda_q1, lambda_k1, lambda_q2, lambda_k2, subln_gain, w_out,
              norm_mlp, w_up, w_down, final_norm):
    b, s_len, _ = x_prompt.shape
    nd, t, _ = x_sample.shape
    past = page_table.shape[1] * PAGE_SIZE
    pos_p = jnp.arange(s_len)
    pos_s = past + jnp.arange(t)
    keep_p = min(MAX_WINDOW, s_len)
    hp, hs = x_prompt, x_sample
    dk_p, dv_p, wk_p, wv_p = [], [], [], []
    dk_s, dv_s, wk_s, wv_s = [], [], [], []
    for l in range(DEPTH):
        lambda_init = 0.8 - 0.6 * math.exp(-0.3 * l)
        lam = (jnp.exp(jnp.sum((lambda_q1[l] * lambda_k1[l]).astype(jnp.float32)))
               - jnp.exp(jnp.sum((lambda_q2[l] * lambda_k2[l]).astype(jnp.float32))) + lambda_init)

        qa, ka, va, qb, kb, vb = project_qkv(rmsnorm(hp, norm_attn[l]), w_in[l], pos_p)
        oa = combine_branches([dilated_branch_prompt(qa, ka, va, w, d) for w, d in DILATED_BRANCHES])
        ob = diff_head_norm(diff_attention_prompt(qb, kb, vb, lam), subln_gain[l], lambda_init)
        mix = jnp.concatenate([oa.reshape(b, s_len, WIDTH_A), ob.reshape(b, s_len, WIDTH_B_V)], axis=-1)
        hp = hp + mix.astype(hp.dtype) @ w_out[l]
        hp = mlp_sublayer(hp, norm_mlp[l], w_up[l], w_down[l])
        dk_p.append(kb.reshape(b, s_len, N_HEADS_B, 2 * HEAD_DIM))
        dv_p.append(vb)
        wk_p.append(ka[:, s_len - keep_p:])
        wv_p.append(va[:, s_len - keep_p:])

        qa, ka, va, qb, kb, vb = project_qkv(rmsnorm(hs, norm_attn[l]), w_in[l], pos_s)
        lb = state_win_k.shape[2]
        k_all = jnp.concatenate([state_win_k[l].astype(ka.dtype), ka], axis=1)
        v_all = jnp.concatenate([state_win_v[l].astype(va.dtype), va], axis=1)
        oa = combine_branches([dilated_branch_sample(qa, k_all, v_all, w, d) for w, d in DILATED_BRANCHES])
        ob = diff_head_norm(diff_attention_sample(qb, kb, vb, cache_diff_k[l], cache_diff_v[l], page_table, lam),
                            subln_gain[l], lambda_init)
        mix = jnp.concatenate([oa.reshape(nd, t, WIDTH_A), ob.reshape(nd, t, WIDTH_B_V)], axis=-1)
        hs = hs + mix.astype(hs.dtype) @ w_out[l]
        hs = mlp_sublayer(hs, norm_mlp[l], w_up[l], w_down[l])
        dk_s.append(kb.reshape(nd, t, N_HEADS_B, 2 * HEAD_DIM))
        dv_s.append(vb)
        wk_s.append(k_all[:, t:t + lb])
        wv_s.append(v_all[:, t:t + lb])

    y_prompt = rmsnorm(hp, final_norm)
    y_sample = rmsnorm(hs, final_norm)
    return (y_prompt, y_sample,
            jnp.stack(dk_p), jnp.stack(dv_p), jnp.stack(wk_p), jnp.stack(wv_p),
            jnp.stack(dk_s), jnp.stack(dv_s), jnp.stack(wk_s), jnp.stack(wv_s))


_drawn_inputs = setup_inputs


def setup_inputs(seed=0):
    import zlib

    import numpy as np

    out = dict(_drawn_inputs(seed))
    spreads = {}
    factors = {'norm_attn': 5.375,
     'lambda_q1': 6.792,
     'lambda_k1': 8.0,
     'subln_gain': 45.31,
     'norm_mlp': 33.471,
     'final_norm': 33.779,
     'lambda_q2': 8.0,
     'lambda_k2': 8.0}
    for name, (base, spread) in spreads.items():
        noise = np.random.default_rng([zlib.crc32(name.encode()), seed]).standard_normal(out[name].shape)
        drawn = base * np.exp(spread * noise) if base else spread * noise
        out[name] = __import__('jax').numpy.asarray(drawn.astype(out[name].dtype))
    for name, factor in factors.items():
        out[name] = (out[name] * factor).astype(out[name].dtype)
    return out
```

```python
import math
from contextlib import ExitStack

import numpy as np

import concourse.bass as bass
import concourse.mybir as mybir

F32 = mybir.dt.float32
I32 = mybir.dt.int32
ALU = mybir.AluOpType
ACT = mybir.ActivationFunctionType
AX = mybir.AxisListType

P = 128
D = 1024
S = 2048
ND, TD = 8, 4
NS = ND * TD
HD = 64
GW = 512
NP = GW // P
FF = 4096
WIN = 2048
PAGES, PAGE = 64, 128
NPHYS = 640
BRANCHES = ((128, 1), (512, 4), (2048, 16))
KC = D // P
NT = S // P
ROT = HD // 4
THETA = 500000.0
SCALE = HD ** -0.5
LAMBDA_INIT = 0.8 - 0.6 * math.exp(0.0)
NEG = -1.0e30
BIG = 3.0e38
EPS, SUB_EPS = 1e-6, 1e-5
FG = FF // 512


class Count:

    def __init__(self, base=0):
        self.base, self.n = base, 0

    def up(self, k=1):
        self.n += k
        return self.base + self.n


def linker(eng, sem, count):
    def link(ins):
        ins.then_inc(sem, 1)
        eng.wait_ge(sem, count.up())
    return link


def project(nc, io, keep):
    GROUPS = ("qa", "ka", "qb", "kb", "va", "vb")
    COLS = {"qa": 0, "ka": 1, "va": 2, "qb": 3, "kb": 4, "vb": 5}
    NG, NR = 6, 4
    ZB = 4
    with ExitStack() as ctx:
        sb = lambda n, s, d=F32: ctx.enter_context(nc.sbuf_tensor(n, s, d))
        ps = lambda n: ctx.enter_context(nc.psum_tensor(n, [P, 512], F32))
        sem = lambda n: ctx.enter_context(nc.semaphore(n))
        w_in = sb("a_w_in", [P, KC, NG * GW])
        gain = sb("a_gain", [P, KC])
        cos = sb("a_cos", [P, NT + 1, ROT])
        sin = sb("a_sin", [P, NT + 1, ROT])
        x = [sb(f"a_x{b}", [P, D]) for b in range(2)]
        xs = sb("a_xs", [P, D])
        xT = [sb(f"a_xT{b}", [P, KC, P]) for b in range(2)]
        stat = sb("a_stat", [P, 4])
        z = [sb(f"a_z{b}", [P, NG, GW]) for b in range(2)]
        rot = sb("a_rot", [P, 2, GW // HD, ROT])
        zT = [sb(f"a_zT{b}", [P, NR, NP, P]) for b in range(2)]
        x_turn = [ps(f"a_turn{i}") for i in range(2)]
        z_ps = [ps(f"a_zps{i}") for i in range(ZB)]
        z_turn = [ps(f"a_zturn{i}") for i in range(2)]

        const_in = sem("a_const_in")
        w_landed = [sem(f"a_w_landed{i}") for i in range(NG)]
        x_landed = [sem(f"a_x_landed{b}") for b in range(2)]
        squared = sem("a_squared")
        var_ready = sem("a_var_ready")
        root_ready = sem("a_root_ready")
        xs_ready = sem("a_xs_ready")
        x_turned = sem("a_x_turned")
        xT_ready = sem("a_xT_ready")
        z_summed = sem("a_z_summed")
        z_free = sem("a_z_free")
        rotated = sem("a_rotated")
        z_turned = sem("a_z_turned")
        zT_ready = sem("a_zT_ready")
        stored = [sem(f"a_stored{b}") for b in range(2)]
        vec = sem("a_vec")
        VEC = NR + 1
        copied = sem("a_copied")

        w_cols = io["w_in"].rearrange("(c p) (g n) -> g p c n", p=P, g=NG)
        order = [GROUPS[i] for i in range(NG)]

        def rows_of(it):
            return NS if isinstance(it, int) and it == NT else P

        def phase(prologue, step):
            def run(eng):
                prologue()
                with eng.Fori(0, (NT - 2) // 2) as p:
                    for b in range(2):
                        step(p * 2 + b, b)
                for it in range(NT - 2, NT + 1):
                    step(it, it % 2)
            return run

        with nc.Block() as block:
            @block.sync
            def _(sp):
                def load(it, b):
                    src = io["x_sample"] if rows_of(it) == NS else io["x_prompt"].rearrange(
                        "(t p) d -> t p d", p=P)[bass.ds(it, 1)].rearrange("o p d -> (o p) d")
                    sp.dma_start(x[b][0:rows_of(it)], src).then_inc(x_landed[b], 16)

                def prologue():
                    load(0, 0)
                    load(1, 1)
                    for name, dst in (("norm_attn", gain), ("cos", cos), ("sin", sin), ("ident", keep["ident"])):
                        sp.dma_start(dst[:], io[name]).then_inc(const_in, 16)
                    for i, g in enumerate(order):
                        sp.dma_start(w_in[:, :, COLS[g] * GW:(COLS[g] + 1) * GW],
                                     w_cols[COLS[g]]).then_inc(w_landed[i], 16)

                def step(it, b):
                    r = rows_of(it)
                    if not isinstance(it, int) or it < NT - 1:
                        sp.wait_ge(xs_ready, it + 1)
                        load(it + 2, b)
                    if r == NS:
                        for i, g in enumerate(order):
                            if i < NR:
                                sp.wait_ge(rotated, it * NR + i + 1)
                            else:
                                sp.wait_ge(z_free, it * NG + (ZB + i + 1))
                            if g in ("kb", "vb"):
                                sp.dma_start(io[g + "_s"], z[b][0:NS, i, :]).then_inc(stored[b], 16)
                            elif g in ("ka", "va"):
                                for n in range(ND):
                                    sp.dma_start(io[g + "_win"][n, WIN - TD:WIN, :],
                                                 z[b][n * TD:(n + 1) * TD, i, :]).then_inc(stored[b], 16)
                        for n in range(2):
                            sp.wait_ge(stored[n], 16 * 8 * (NT // 2) + (16 * (2 + 2 * ND) if n == b else 0))
                        return
                    for i, g in enumerate(order):
                        if g[0] == "q":
                            continue
                        if i < NR:
                            sp.wait_ge(rotated, it * NR + (i + 1))
                        else:
                            sp.wait_ge(z_free, it * NG + (ZB + i + 1))
                        dst = io[g + "_p"].rearrange("(t p) n -> t p n", p=P)[bass.ds(it, 1)]
                        sp.dma_start(dst.rearrange("o p n -> (o p) n"), z[b][:, i, :]).then_inc(stored[b], 16)
                    for i, g in enumerate(order[:NR]):
                        sp.wait_ge(zT_ready, it * NR + (2 + i + 1))
                        dst = io[g[0] + "T"].rearrange("g p (t n) -> t p g n", n=P)[bass.ds(it, 1)]
                        at = 0 if g[1] == "a" else NP
                        sp.dma_start(dst[:, :, at:at + NP].rearrange("o p g n -> (o p) g n"),
                                     zT[b][:, i]).then_inc(stored[b], 16)

                phase(prologue, step)(sp)

            @block.gpsimd
            def _(pool):
                body = (WIN - TD) // 16 * 16
                for landed in w_landed:
                    pool.wait_ge(landed, 16)
                with pool.Fori(0, ND) as n:
                    pool.wait_ge(xs_ready, n * 2 + 1)
                    for k in ("ka", "va"):
                        src = io[k + "_state"][bass.ds(n, 1)].rearrange("o t n -> (o t) n")
                        dst = io[k + "_win"][bass.ds(n, 1)].rearrange("o t n -> (o t) n")
                        pool.dma_start(dst[0:body].rearrange("(a b) n -> a b n", a=16),
                                       src[TD:TD + body].rearrange("(a b) n -> a b n", a=16)).then_inc(copied, 16)
                        pool.dma_start(dst[body:WIN - TD], src[TD + body:WIN]).then_inc(copied, 16)
                pool.wait_ge(copied, 16 * 4 * ND)

            @block.scalar
            def _(act):
                def norm(it, b):
                    r = rows_of(it)
                    act.wait_ge(x_landed[b], (it - b) * 8 + 16)
                    act.wait_ge(x_turned, it * 2)
                    nc.scalar.activation(xs[0:r], x[b][0:r], ACT.Square,
                                         accum_out=stat[0:r, 0:1]).then_inc(squared, 1)
                    act.wait_ge(var_ready, it + 1)
                    nc.scalar.activation(stat[0:r, 2:3], stat[0:r, 1:2], ACT.Sqrt).then_inc(root_ready, 1)

                def prologue():
                    act.sem_inc(z_free, ZB)
                    act.sem_inc(zT_ready, 2)
                    norm(0, 0)

                def step(it, b):
                    r = rows_of(it)
                    act.wait_ge(stored[b], (it - b) * 64)
                    for i in range(NG):
                        act.wait_ge(z_summed, it * NG + i + 1)
                        nc.scalar.copy(z[b][0:r, i, :], z_ps[ring(b, i)][0:r, :]).then_inc(z_free, 1)
                        if i == 1 and r == P:
                            norm(it + 1, 1 - b)
                    for i in range(NR):
                        act.wait_ge(z_turned, it * NR + i + 1)
                        dst = zT[b][:, i, :, 0:r] if r == P else keep[GROUPS[i][0] + "sT"][
                            :, 0 if GROUPS[i][1] == "a" else NP:(0 if GROUPS[i][1] == "a" else NP) + NP, :]
                        src = z_turn[i % 2][:, :].rearrange("p (g n) -> p g n", g=NP)[:, :, 0:r]
                        nc.scalar.copy(dst, src).then_inc(zT_ready, 1)

                phase(prologue, step)(act)

            @block.vector
            def _(dve):
                def norm(it, b, link):
                    r = rows_of(it)
                    dve.wait_ge(squared, it + 1)
                    nc.vector.tensor_scalar(stat[0:r, 1:2], stat[0:r, 0:1], 1.0 / D, EPS,
                                            ALU.mult, ALU.add).then_inc(var_ready, 1)
                    dve.wait_ge(root_ready, it + 1)
                    link(nc.vector.reciprocal(stat[0:r, 3:4], stat[0:r, 2:3]))
                    nc.vector.tensor_scalar(xs[0:r], x[b][0:r], stat[0:r, 3:4], None,
                                            ALU.mult).then_inc(xs_ready, 1)

                def spread(it, b):
                    r = rows_of(it)
                    if not (isinstance(it, int) and it < 2):
                        dve.wait_ge(z_summed, (it - 1) * NG)
                    for h in range(2):
                        dve.wait_ge(x_turned, it * 2 + h + 1)
                        dst = xT[b][:, 4 * h:4 * h + 4, 0:r]
                        src = x_turn[h][:, :].rearrange("p (c n) -> p c n", c=4)[:, :, 0:r]
                        g = gain[:, 4 * h:4 * h + 4].unsqueeze(2).broadcast_to([P, 4, r])
                        nc.vector.tensor_tensor(dst, src, g, ALU.mult).then_inc(xT_ready, 1)

                def prologue():
                    dve.wait_ge(const_in, 64)
                    norm(0, 0, linker(dve, vec, Count(0)))
                    spread(0, 0)

                def step(it, b):
                    r = rows_of(it)
                    link = linker(dve, vec, Count(it * VEC + 1))
                    for i in range(NR):
                        if i == 2 and r == P:
                            norm(it + 1, 1 - b, link)
                        dve.wait_ge(z_free, it * NG + (ZB + i + 1))
                        head = z[b][0:r, i, :].rearrange("p (u e) -> p u e", e=HD)[:, :, 0:ROT]
                        u = GW // HD
                        tab = lambda t: t[0:r, bass.ds(it, 1), :].broadcast_to([r, u, ROT])
                        nc.vector.tensor_tensor(rot[0:r, 0], head, tab(cos), ALU.mult)
                        swap = head.rearrange("p u (h e) -> p u h e", h=2)[:, :, ::-1, :]
                        link(nc.vector.tensor_tensor(
                            rot[0:r, 1].rearrange("p u (h e) -> p u h e", h=2), swap,
                            tab(sin).rearrange("p u (h e) -> p u h e", h=2), ALU.mult))
                        nc.vector.tensor_tensor(head, rot[0:r, 0], rot[0:r, 1], ALU.add).then_inc(rotated, 1)
                        dve.wait_ge(rotated, it * NR + (i + 1))
                    if r == P:
                        spread(it + 1, 1 - b)

                phase(prologue, step)(dve)

            @block.tensor
            def _(pe):
                def turn(it, b):
                    r = rows_of(it)
                    if isinstance(it, int) and it == 0:
                        pe.wait_ge(const_in, 64)
                    pe.wait_ge(xs_ready, it + 1)
                    for h in range(2):
                        if not (isinstance(it, int) and it == 0):
                            pe.wait_ge(xT_ready, it * 2 - 1 + h)
                        for c in range(4):
                            m = nc.tensor.transpose(x_turn[h][:, c * P:c * P + r],
                                                    xs[0:r, (4 * h + c) * P:(4 * h + c + 1) * P],
                                                    keep["ident"][0:r, 0:r])
                        m.then_inc(x_turned, 1)

                def prologue():
                    turn(0, 0)

                def step(it, b):
                    r = rows_of(it)
                    pe.wait_ge(xT_ready, it * 2 + 2)
                    for i, g in enumerate(order):
                        if not isinstance(it, int):
                            pe.wait_ge(w_landed[i], 16)
                        pe.wait_ge(z_free, it * NG + (i + 1))
                        for c in range(KC):
                            m = nc.tensor.matmul(z_ps[ring(b, i)][0:r, :], xT[b][:, c, 0:r],
                                                 w_in[:, c, COLS[g] * GW:(COLS[g] + 1) * GW],
                                                 start=(c == 0), stop=(c == KC - 1))
                        m.then_inc(z_summed, 1)
                        if i == NR and r == P:
                            turn(it + 1, 1 - b)
                    for i in range(NR):
                        pe.wait_ge(rotated, it * NR + (i + 1))
                        pe.wait_ge(zT_ready, it * NR + (i + 1))
                        for g in range(NP):
                            m = nc.tensor.transpose(z_turn[i % 2][:, g * P:g * P + r],
                                                    z[b][0:r, i, g * P:(g + 1) * P], keep["ident"][0:r, 0:r])
                        m.then_inc(z_turned, 1)

                phase(prologue, step)(pe)


def ring(b, i):
    return (6 * b + i) % 4


def reuse(base, n, slots):
    return base if n < slots else base + (n - slots + 1)


def attend_prompt(nc, io, keep):
    NQ = 4
    NU = NT // NQ
    PASSES = NP // 2
    SS, WS = 4, 4
    with ExitStack() as ctx:
        sb = lambda n, s, d=F32: ctx.enter_context(nc.sbuf_tensor(n, s, d))
        ps = lambda n: ctx.enter_context(nc.psum_tensor(n, [P, 512], F32))
        sem = lambda n: ctx.enter_context(nc.semaphore(n))
        q = [sb(f"b_q{i}", [P, 2, S]) for i in range(2)]
        k = [sb(f"b_k{i}", [P, S]) for i in range(2)]
        v = [sb(f"b_v{i}", [P, NT, P]) for i in range(2)]
        bias = [sb("b_bias_dilated", [P, S]), sb("b_bias_causal", [P, S])]
        w = [[sb(f"b_w{i}_{t}", [P, S]) for t in range(NQ)] for i in range(2)]
        w1 = [sb(f"b_second{t}", [P, S]) for t in range(2)]
        wT = [sb(f"b_wT{i}", [P, 512]) for i in range(WS)]
        o = [sb(f"b_o{i}", [P, 512]) for i in range(2)]
        part = sb("b_part", [P, 2, NU])
        top = sb("b_top", [P, 2])
        shift = sb("b_shift", [P, 2, 2 * NQ])
        total = sb("b_total", [P, 2, 2 * NQ])
        inv = sb("b_inv", [P, 2, 2 * NQ])
        lam_rows = sb("b_lam_rows", [P, 4 * HD])
        lam_prod = sb("b_lam_prod", [P, 2, HD])
        lam_sum = sb("b_lam_sum", [P, 2])
        lam_exp = sb("b_lam_exp", [P, 2])
        s_ps = [ps(f"b_s{i}") for i in range(SS)]
        turn = [ps(f"b_turn{i}") for i in range(2)]
        o_ps = [ps(f"b_ops{i}") for i in range(2)]

        const_in = sem("b_const_in")
        lam_summed = sem("b_lam_summed")
        lam_exped = sem("b_lam_exped")
        lam_ready = sem("b_lam_ready")
        zeroed = sem("b_zeroed")
        pair_in = [sem(f"b_pair_in{i}") for i in range(2)]
        s_full = sem("b_s_full")
        s_used = sem("b_s_used")
        shift_ready = sem("b_shift_ready")
        exp_done = sem("b_exp_done")
        inv_ready = sem("b_inv_ready")
        w_ready = sem("b_w_ready")
        turned = sem("b_turned")
        copied = [sem("b_copied_scalar"), sem("b_copied_vector")]
        wT_used = sem("b_wT_used")
        o_copied = sem("b_o_copied")
        o_out = [sem(f"b_o_out{i}") for i in range(2)]
        vec = sem("b_vec")
        vec_gate, pool_gate = sem("b_vec_gate"), sem("b_pool_gate")

        class Pass:
            def __init__(self, diff):
                self.diff = diff
                self.maps = (0, 1) if diff else (0,)
                self.units = [(i, m, g) for i in range(2) for m in ((0,) if diff else (0, 1)) for g in range(NU)]
                self.n = len(self.units)
                self.part0 = [sum(NQ * (g + 1) * len(self.maps) for _, _, g in self.units[:n]) for n in range(self.n + 1)]
                self.key0 = [sum(NQ * (g + 1) for _, _, g in self.units[:n]) for n in range(self.n + 1)]
                self.rows = NQ * len(self.maps)
                self.links = sum(self.rows * (g > 0) + 3 * NQ * diff for _, _, g in self.units)

        kinds = (Pass(False), Pass(True))
        COUNTS = ("units", "parts", "keys", "rows", "tiles", "vec")

        def size(kd):
            return dict(units=kd.n, parts=kd.part0[-1], keys=kd.key0[-1], rows=kd.n * kd.rows, tiles=kd.n * NQ, vec=kd.links)

        def passes(eng, body):
            done = dict.fromkeys(COUNTS, 0)
            for kd in kinds:
                n = size(kd)
                with eng.Fori(0, PASSES) as r:
                    body(kd, r, {c: r * n[c] + done[c] for c in COUNTS})
                for c in COUNTS:
                    done[c] += PASSES * n[c]

        with nc.Block() as block:
            @block.sync
            def _(sp):
                for dst, name in ((bias[0], "bias_dilated"), (bias[1], "bias_causal")):
                    sp.dma_start(dst[:], io[name]).then_inc(const_in, 16)
                sp.dma_start(lam_rows[:], io["lambdas"].broadcast_to([P, 4 * HD])).then_inc(const_in, 16)
                sp.wait_ge(zeroed, 2)
                ends = []
                for pair in range(2 * NP):
                    i, kd = pair % 2, kinds[pair // NP]
                    if pair >= 2:
                        sp.wait_ge(wT_used, ends[pair - 2])
                    sp.dma_start(k[i][:], io["kT"][pair]).then_inc(pair_in[i], 16)
                    for m in range(2):
                        h = slice(m * HD, (m + 1) * HD)
                        sp.dma_start(q[i][h, m, :], io["qT"][pair, h]).then_inc(pair_in[i], 16)
                    vs = io["vb_p" if kd.diff else "va_p"].rearrange("(t p) (g n) -> g p t n", p=P, g=NP)
                    sp.dma_start(v[i][:], vs[pair % NP]).then_inc(pair_in[i], 16)
                    ends.append((ends[-1] if ends else 0) + kd.key0[-1] // 2)

            @block.gpsimd
            def _(pool):
                for i in range(2):
                    nc.gpsimd.memset(q[i][:], 0.0).then_inc(zeroed, 1)
                kd = kinds[0]
                with pool.Fori(0, PASSES) as r:
                    for n, (i, m, g) in enumerate(kd.units):
                        for t in range(NQ):
                            pool.wait_ge(inv_ready, r * (kd.n * NQ) + (n * NQ + t + 1))
                            pool.sem_inc(pool_gate, 1)
                            row = w[n % 2][t][:, 0:(NQ * g + t + 1) * P]
                            nc.gpsimd.tensor_scalar(row, row, inv[:, n % 2, 2 * t:2 * t + 1], None,
                                                    ALU.mult).then_inc(w_ready, 1)

            @block.tensor
            def _(pe):
                def body(kd, r, base):
                    def scores(n):
                        i, m, g = kd.units[n]
                        if n % (kd.n // 2) == 0:
                            pe.wait_ge(pair_in[i], r * 64 + (64 * (1 + PASSES * kd.diff)))
                        j = kd.part0[n]
                        for t in range(NQ):
                            for mm in kd.maps:
                                for b in range(g + 1):
                                    pe.wait_ge(s_used, reuse(base["parts"], j, SS))
                                    lo, hi = b * 512, min((b + 1) * 512, (NQ * g + t + 1) * P)
                                    nc.tensor.matmul(s_ps[j % SS][:, 0:hi - lo],
                                                     q[i][:, m + mm, (NQ * g + t) * P:(NQ * g + t + 1) * P],
                                                     k[i][:, lo:hi], start=True, stop=True).then_inc(s_full, 1)
                                    j += 1

                    def weigh(n):
                        i, m, g = kd.units[n]
                        nk = NQ * (g + 1)
                        pe.wait_ge(w_ready, base["tiles"] + NQ * (n + 1))

                        def turn_keys(kt):
                            e = kd.key0[n] + kt
                            pe.wait_ge(copied[e % 2], base["keys/2"] + e // 2)
                            for t in range(max(0, kt - NQ * g), NQ):
                                last = nc.tensor.transpose(turn[e % 2][:, t * P:(t + 1) * P],
                                                           w[n % 2][t][:, kt * P:(kt + 1) * P], keep["ident"][:])
                            last.then_inc(turned, 1)

                        turn_keys(0)
                        turn_keys(1)
                        pe.wait_ge(o_copied, reuse(base["units"], n, 2))
                        rows, lo = (P, 0) if kd.diff else (HD, m * HD)
                        for kt in range(nk):
                            e = kd.key0[n] + kt
                            c0 = max(0, kt - NQ * g) * P
                            pe.wait_ge(copied[e % 2], base["keys/2"] + (e // 2 + 1))
                            nc.tensor.matmul(o_ps[n % 2][0:rows, c0:512], v[i][:, kt, lo:lo + rows],
                                             wT[e % WS][:, c0:512], start=(kt == 0),
                                             stop=(kt == nk - 1)).then_inc(wT_used, 1)
                            if kt + 2 < nk:
                                turn_keys(kt + 2)

                    base["keys/2"] = r * (kd.key0[-1] // 2) + (PASSES * kinds[0].key0[-1] // 2 * kd.diff)
                    scores(0)
                    for n in range(kd.n):
                        if n + 1 < kd.n:
                            scores(n + 1)
                        weigh(n)

                passes(pe, body)

            def copy_turned(eng, copy, kd, base, n, which):
                i, m, g = kd.units[n]
                for kt in range(NQ * (g + 1)):
                    e = kd.key0[n] + kt
                    if e % 2 != which:
                        continue
                    c0 = max(0, kt - NQ * g) * P
                    eng.wait_ge(turned, base["keys"] + (e + 1))
                    eng.wait_ge(wT_used, reuse(base["keys"], e, WS))
                    copy(wT[e % WS][:, c0:512], turn[e % 2][:, c0:512]).then_inc(copied[which], 1)

            @block.scalar
            def _(act):
                act.wait_ge(lam_summed, 1)
                nc.scalar.activation(lam_exp[:], lam_sum[:], ACT.Exp).then_inc(lam_exped, 1)

                def body(kd, r, base):
                    def exps(n):
                        i, m, g = kd.units[n]
                        for t in range(NQ):
                            for mm in kd.maps:
                                act.wait_ge(shift_ready, base["rows"] + (n * kd.rows + t * len(kd.maps) + mm + 1))
                                row = (w1[t % 2] if mm else w[n % 2][t])[:, 0:(NQ * g + t + 1) * P]
                                c = 2 * t + mm
                                nc.scalar.activation(row, row, ACT.Exp, bias=shift[:, n % 2, c:c + 1], scale=SCALE,
                                                     accum_out=total[:, n % 2, c:c + 1]).then_inc(exp_done, 1)

                    def put(n):
                        i, m, g = kd.units[n]
                        rows, lo = (P, 0) if kd.diff else (HD, m * HD)
                        act.wait_ge(wT_used, base["keys"] + kd.key0[n + 1])
                        act.wait_ge(o_out[n % 2], base["units"] * 8 + n // 2 * 16)
                        nc.scalar.copy(o[n % 2][0:rows], o_ps[n % 2][0:rows]).then_inc(o_copied, 1)
                        pair = r * 2 + (NP * kd.diff + i)
                        act.wait_ge(o_copied, base["units"] + (n + 1))
                        dst = io["mixT"][bass.ds(pair, 1), lo:lo + rows, g * 512:(g + 1) * 512]
                        act.dma_start(dst.rearrange("o p n -> (o p) n"), o[n % 2][0:rows]).then_inc(o_out[n % 2], 16)

                    exps(0)
                    for n in range(kd.n):
                        if n + 1 < kd.n:
                            exps(n + 1)
                        copy_turned(act, nc.scalar.copy, kd, base, n, 0)
                        put(n)

                passes(act, body)
                for i in range(2):
                    act.wait_ge(o_out[i], 8 * PASSES * (kinds[0].n + kinds[1].n))

            @block.vector
            def _(dve):
                link = linker(dve, vec, Count(0))
                dve.wait_ge(const_in, 48)
                link(nc.vector.tensor_tensor(lam_prod[:].rearrange("p a n -> p (a n)"), lam_rows[:, 0:2 * HD],
                                             lam_rows[:, 2 * HD:4 * HD], ALU.mult))
                nc.vector.tensor_reduce(lam_sum[:], lam_prod[:], AX.X, ALU.add).then_inc(lam_summed, 1)
                dve.wait_ge(lam_exped, 1)
                link(nc.vector.tensor_scalar(keep["neg_lam"][:], lam_exp[:, 1:2], -LAMBDA_INIT, None, ALU.add))
                link(nc.vector.tensor_tensor(keep["neg_lam"][:], keep["neg_lam"][:], lam_exp[:, 0:1], ALU.subtract))

                def body(kd, r, base):
                    link = linker(dve, vec, Count(base["vec"] + 3))

                    def biased(n, t, mm, j):
                        i, m, g = kd.units[n]
                        tile = NQ * g + t
                        row = w1[t % 2] if mm else w[n % 2][t]
                        rb = n * kd.rows + t * len(kd.maps) + mm
                        for b in range(g + 1):
                            lo, hi = b * 512, min((b + 1) * 512, (tile + 1) * P)
                            at = (NT - 1 - tile) * P + lo
                            dve.wait_ge(s_full, base["parts"] + (j + 1))
                            dve.sem_inc(vec_gate, 1)
                            nc.vector.tensor_tensor_reduce(
                                out=row[:, lo:hi], in0=s_ps[j % SS][:, 0:hi - lo],
                                in1=bias[kd.diff][:, at:at + hi - lo], scale=1.0, scalar=-BIG, op0=ALU.add,
                                op1=ALU.max, accum_out=(part[:, rb % 2, b:b + 1])).then_inc(s_used, 1)
                            j += 1
                        dve.wait_ge(s_used, base["parts"] + j)
                        src = part[:, rb % 2, 0:1]
                        if g:
                            link(nc.vector.tensor_reduce(top[:, rb % 2:rb % 2 + 1], part[:, rb % 2, 0:g + 1],
                                                         AX.X, ALU.max))
                            src = top[:, rb % 2:rb % 2 + 1]
                        c = 2 * t + mm
                        nc.vector.tensor_scalar(shift[:, n % 2, c:c + 1], src, -SCALE, None,
                                                ALU.mult).then_inc(shift_ready, 1)
                        return j

                    def normed(n, t):
                        i, m, g = kd.units[n]
                        c = 2 * t
                        dve.wait_ge(exp_done, base["rows"] + (n * kd.rows + (t + 1) * len(kd.maps)))
                        rec = nc.vector.reciprocal(inv[:, n % 2, c:c + len(kd.maps)],
                                                   total[:, n % 2, c:c + len(kd.maps)])
                        if not kd.diff:
                            rec.then_inc(inv_ready, 1)
                            return
                        link(rec)
                        cols = (NQ * g + t + 1) * P
                        link(nc.vector.tensor_scalar(inv[:, n % 2, c + 1:c + 2], inv[:, n % 2, c + 1:c + 2],
                                                     keep["neg_lam"][:, 0:1], None, ALU.mult))
                        row = w[n % 2][t][:, 0:cols]
                        link(nc.vector.tensor_scalar(row, row, inv[:, n % 2, c:c + 1], None, ALU.mult))
                        nc.vector.scalar_tensor_tensor(out=row, in0=w1[t % 2][:, 0:cols],
                                                       scalar=inv[:, n % 2, c + 1:c + 2], in1=row,
                                                       op0=ALU.mult, op1=ALU.add).then_inc(w_ready, 1)

                    def score_rows(n):
                        dve.wait_ge(turned, base["keys"] + (kd.key0[n - 1] if n >= 2 else 0))
                        j = kd.part0[n]
                        for t in range(NQ):
                            for mm in kd.maps:
                                j = biased(n, t, mm, j)
                            if t >= 1:
                                normed(n, t - 1)

                    score_rows(0)
                    normed(0, NQ - 1)
                    for n in range(kd.n):
                        if n + 1 < kd.n:
                            score_rows(n + 1)
                        copy_turned(dve, nc.vector.tensor_copy, kd, base, n, 1)
                        if n + 1 < kd.n:
                            normed(n + 1, NQ - 1)

                passes(dve, body)


CH = 8
SL = 4
ROWS = 32
NC = PAGES // CH + 1


def attend_decode(nc, io, keep):
    RG = 3
    with ExitStack() as ctx:
        sb = lambda n, s, d=F32: ctx.enter_context(nc.sbuf_tensor(n, s, d))
        ps = lambda n: ctx.enter_context(nc.psum_tensor(n, [P, 512], F32))
        sem = lambda n: ctx.enter_context(nc.semaphore(n))
        table = sb("c_table", [1, ND * PAGES], I32)
        k = [sb(f"c_k{i}", [P, CH, GW]) for i in range(RG)]
        v = [sb(f"c_v{i}", [P, CH, GW]) for i in range(RG)]
        kT = [sb(f"c_kT{i}", [P, NP, CH * P]) for i in range(RG)]
        q_rows = sb("c_q_rows", [P, 2, NP, SL * ROWS])
        v_new = sb("c_v_new", [TD, 2, ND, GW])
        bias_new = sb("c_bias_new", [P, 2, TD])
        bias_win = sb("c_bias_win", [P, 2 * P])
        own_head = sb("c_own_head", [P, 2, GW])
        same_row = sb("c_same_row", [P, P])
        token = sb("c_token", [P, TD])
        map_of = sb("c_map_of", [P, 2])
        sign = sb("c_sign", [P, 2])
        s_new = sb("c_s_new", [P, 2, TD])
        p_new = sb("c_p_new", [P, 2, TD])
        pT_new = sb("c_pT_new", [TD, 2, P])
        s_win = sb("c_s_win", [P, 2 * P])
        m = sb("c_m", [P, 2, 2])
        chunk_max = sb("c_chunk_max", [P, 1])
        shift = sb("c_shift", [P, RG])
        shift_new = sb("c_shift_new", [P, 2])
        alpha = sb("c_alpha", [P, RG])
        l_new = sb("c_l_new", [P, 2])
        l_chunk = sb("c_l_chunk", [P, RG])
        l = sb("c_l", [P, 2])
        prob = [sb(f"c_prob{i}", [P, 2 * P]) for i in range(RG)]
        pT = [sb(f"c_pT{i}", [P, 2 * P]) for i in range(RG)]
        acc = sb("c_acc", [P, 2, GW])
        m_row = sb("c_m_row", [2, ROWS])
        m_rows = sb("c_m_rows", [2, SL, ROWS])
        below = sb("c_below", [P, 2])
        weight = sb("c_weight", [P, 2])
        lw = sb("c_lw", [P, 2])
        coef = sb("c_coef", [P, 2])
        comb = sb("c_comb", [P, 2, TD])
        turn = [ps(f"c_turn{i}") for i in range(2)]
        s_ps = [ps(f"c_s{i}") for i in range(RG)]
        pT_ps, o_ps, x_ps = ps("c_pT_ps"), ps("c_o_ps"), ps("c_x_ps")

        const_in, table_in = sem("c_const_in"), sem("c_table_in")
        q_zero, q_ready = sem("c_q_zero"), sem("c_q_ready")
        k_in = [sem(f"c_k_in{i}") for i in range(RG)]
        v_in = [sem(f"c_v_in{i}") for i in range(RG)]
        turned = sem("c_turned")
        copied = [sem("c_copied_scalar"), sem("c_copied_vector")]
        s_full, shift_ready, exp_done = sem("c_s_full"), sem("c_shift_ready"), sem("c_exp_done")
        p_turned, pT_ready = sem("c_p_turned"), sem("c_pT_ready")
        o_full, o_added, l_added = sem("c_o_full"), sem("c_o_added"), sem("c_l_added")
        new_scored, new_shifted, new_exped = sem("c_new_scored"), sem("c_new_shifted"), sem("c_new_exped")
        new_turned, new_pT, new_full, new_taken = (sem("c_new_turned"), sem("c_new_pT"), sem("c_new_full"),
                                                   sem("c_new_taken"))
        m_turned, m_spread_ready, m_spread = sem("c_m_turned"), sem("c_m_spread_ready"), sem("c_m_spread")
        below_ready, weight_ready = sem("c_below_ready"), sem("c_weight_ready")
        lw_ready, l_summed, comb_ready = sem("c_lw_ready"), sem("c_l_summed"), sem("c_comb_ready")
        mixed, mix_kept = sem("c_mixed"), sem("c_mix_kept")
        vec = sem("c_vec")
        vec_gate, sp_gate = sem("c_vec_gate"), sem("c_sp_gate")

        kind = lambda c: 1 if c < NC - 1 else 0
        EV = NP * CH // 4
        LINKS = 3 + 2 * NC + 4

        with nc.Block() as block:
            @block.sync
            def _(sp):
                sp.dma_start(table[:], io["page_table"]).then_inc(table_in, 16)
                consts = (("bias_new", bias_new), ("bias_win", bias_win), ("own_head", own_head),
                          ("same_row", same_row), ("token", token), ("map_of", map_of))
                for name, dst in consts:
                    sp.dma_start(dst[:], io[name]).then_inc(const_in, 16)
                sp.dma_start(v_new[:, 0], io["va_win"][:, WIN - TD:WIN, :].rearrange("n t d -> t n d")).then_inc(const_in, 16)
                sp.dma_start(v_new[:, 1], io["vb_s"].rearrange("(n t) d -> t n d", t=TD)).then_inc(const_in, 16)
                sp.wait_ge(table_in, 16)
                with sp.Fori(0, ND) as n:
                    for c in range(NC):
                        i = c % RG
                        sp.wait_ge(turned, n * (NC * EV) + max(0, c - RG + 1) * EV)
                        sp.sem_inc(sp_gate, 1)
                        sp.wait_ge(o_full, n * NC + max(0, c - RG + 1))
                        sp.sem_inc(sp_gate, 1)
                        if kind(c):
                            for g in range(CH):
                                page = sp.value_load(table[0:1, bass.ds(n * PAGES + (c * CH + g), 1)],
                                                     min_val=0, max_val=NPHYS - 1)
                                for dst, src, landed in ((k, "k_cache", k_in), (v, "v_cache", v_in)):
                                    sp.dma_start(dst[i][:, g, :], io[src][bass.ds(page, 1)].rearrange(
                                        "o p d -> (o p) d")).then_inc(landed[i], 16)
                        else:
                            for dst, src, landed in ((k, "ka_state", k_in), (v, "va_state", v_in)):
                                rows = io[src][bass.ds(n, 1)].rearrange("o t d -> (o t) d")
                                for g in range(3):
                                    by = rows[g * 512:(g + 1) * 512].rearrange("(a r) d -> a r d", r=16)[:, 0:TD, :]
                                    sp.dma_start(dst[i][:, g, :], by).then_inc(landed[i], 16)
                                near = rows[1536:2048].rearrange("(g p) d -> p g d", p=P)
                                sp.dma_start(dst[i][:, 3:7, :], near).then_inc(landed[i], 16)
                                sp.dma_start(dst[i][:, 7, :], rows[1920:2048]).then_inc(landed[i], 16)

            def landed(c, n):
                count = lambda cc: 16 * (CH if kind(cc) else 5)
                mine = [cc for cc in range(NC) if cc % RG == c % RG]
                return n * sum(map(count, mine)) + sum(count(cc) for cc in mine if cc <= c)

            @block.tensor
            def _(pe):
                pe.wait_ge(const_in, 16 * 8)
                with pe.Fori(0, ND) as n:
                    def turn_keys(c):
                        i = c % RG
                        pe.wait_ge(k_in[i], landed(c, n))
                        for e in range(EV):
                            p, half = e // 2, e % 2
                            pe.wait_ge(copied[e % 2], n * (NC * EV // 2) + (c * EV + e) // 2)
                            for g in range(4):
                                last = nc.tensor.transpose(turn[e % 2][:, g * P:(g + 1) * P],
                                                           k[i][:, half * 4 + g, p * P:(p + 1) * P], keep["ident"][:])
                            last.then_inc(turned, 1)

                    def scores(c):
                        i = c % RG
                        for e in range(2):
                            pe.wait_ge(copied[e], n * (NC * EV // 2) + (c + 1) * EV // 2)
                        pe.wait_ge(exp_done, n * NC + max(0, c - RG + 1))
                        for p in range(NP):
                            for j in range(SL):
                                last = nc.tensor.matmul(
                                    s_ps[i][ROWS * j:ROWS * (j + 1), 0:2 * P],
                                    q_rows[:, kind(c), p, ROWS * j:ROWS * (j + 1)],
                                    kT[i][:, p, j * 2 * P:(j + 1) * 2 * P], start=(p == 0), stop=(p == NP - 1))
                        last.then_inc(s_full, 1)

                    def weigh(c):
                        i = c % RG
                        pe.wait_ge(exp_done, n * NC + (c + 1))
                        pe.wait_ge(pT_ready, n * NC + c)
                        for a in range(2):
                            last = nc.tensor.transpose(pT_ps[:, a * P:(a + 1) * P],
                                                       prob[i][:, a * P:(a + 1) * P], keep["ident"][:])
                        last.then_inc(p_turned, 1)
                        pe.wait_ge(v_in[i], landed(c, n))
                        pe.wait_ge(pT_ready, n * NC + (c + 1))
                        if c:
                            pe.wait_ge(o_added, n * NC + c)
                        else:
                            pe.wait_ge(new_taken, n * 2 + 2)
                        for a in range(2):
                            for j in range(SL):
                                last = nc.tensor.matmul(
                                    o_ps[ROWS * j:ROWS * (j + 1), :],
                                    pT[i][:, a * P + ROWS * j:a * P + ROWS * (j + 1)],
                                    v[i][:, 2 * j + a, :], start=(a == 0), stop=(a == 1))
                        last.then_inc(o_full, 1)

                    def new_scores():
                        pe.wait_ge(q_ready, n * 2 + 2)
                        for kd in range(2):
                            for p in range(NP):
                                rhs = keep["ksT"][:, kd * NP + p, bass.ds(n * TD, TD)]
                                last = nc.tensor.matmul(x_ps[:, kd * TD:(kd + 1) * TD], q_rows[:, kd, p, :],
                                                        rhs, start=(p == 0), stop=(p == NP - 1))
                        last.then_inc(new_scored, 1)

                    def new_values():
                        pe.wait_ge(new_exped, n * 2 + 2)
                        for kd in range(2):
                            last = nc.tensor.transpose(x_ps[0:TD, P + kd * P:P + (kd + 1) * P], p_new[:, kd, :],
                                                       keep["ident"][:])
                        last.then_inc(new_turned, 1)
                        pe.wait_ge(new_pT, n + 1)
                        for kd in range(2):
                            pe.wait_ge(new_taken, n * 2 + kd)
                            nc.tensor.matmul(o_ps[:, :], pT_new[:, kd, :],
                                             v_new[:, kd, bass.ds(n, 1), :].rearrange("t o d -> t (o d)"),
                                             start=True, stop=True).then_inc(new_full, 1)

                    turn_keys(0)
                    new_scores()
                    turn_keys(1)
                    new_values()
                    for c in range(NC):
                        if 1 <= c < NC - 1:
                            turn_keys(c + 1)
                        scores(c)
                        if c:
                            weigh(c - 1)
                    weigh(NC - 1)
                    nc.tensor.transpose(x_ps[0:2, 0:P], m[:, 0, :], keep["ident"][:]).then_inc(m_turned, 1)
                    pe.wait_ge(m_spread_ready, n + 1)
                    nc.tensor.matmul(x_ps[:, 128:130], m_rows[:, :, :].rearrange("k j r -> k (j r)"),
                                     keep["ident"][0:2, 0:2], start=True, stop=True).then_inc(m_spread, 1)
                    pe.wait_ge(lw_ready, n + 1)
                    nc.tensor.matmul(x_ps[:, 132:134], same_row[:], lw[:], start=True, stop=True).then_inc(l_summed, 1)
                    pe.wait_ge(comb_ready, n + 1)
                    for kd in range(2):
                        for p in range(NP):
                            at = 136 + (kd * NP + p) * TD
                            last = nc.tensor.matmul(x_ps[:, at:at + TD], acc[:, kd, p * P:(p + 1) * P],
                                                    comb[:, kd, :], start=True, stop=True)
                    last.then_inc(mixed, 1)
                    pe.wait_ge(mix_kept, n + 1)

            @block.scalar
            def _(act):
                with act.Fori(0, ND) as n:
                    def copy_keys(c):
                        i = c % RG
                        for e in range(0, EV, 2):
                            act.wait_ge(turned, n * (NC * EV) + (c * EV + e + 1))
                            act.wait_ge(s_full, n * NC + max(0, c - RG + 1))
                            nc.scalar.copy(kT[i][:, e // 2, 0:512], turn[0][:]).then_inc(copied[0], 1)

                    def exps(c):
                        i = c % RG
                        act.wait_ge(shift_ready, n * NC + (c + 1))
                        old = m[:, c % 2 if kind(c) else 1, kind(c):kind(c) + 1]
                        nc.scalar.activation(alpha[:, i:i + 1], old, ACT.Exp, bias=shift[:, i:i + 1], scale=SCALE)
                        src = s_ps[i][:, 0:2 * P] if kind(c) else s_win[:]
                        nc.scalar.activation(prob[i][:], src, ACT.Exp, bias=shift[:, i:i + 1], scale=SCALE,
                                             accum_out=l_chunk[:, i:i + 1]).then_inc(exp_done, 1)

                    def copy_pT(c):
                        act.wait_ge(p_turned, n * NC + (c + 1))
                        nc.scalar.copy(pT[c % RG][:], pT_ps[:, 0:2 * P]).then_inc(pT_ready, 1)

                    copy_keys(0)
                    act.wait_ge(new_shifted, n + 1)
                    for kd in range(2):
                        nc.scalar.activation(p_new[:, kd, :], s_new[:, kd, :], ACT.Exp, bias=shift_new[:, kd:kd + 1],
                                             scale=SCALE, accum_out=l_new[:, kd:kd + 1]).then_inc(new_exped, 1)
                    copy_keys(1)
                    for c in range(NC):
                        if 1 <= c < NC - 1:
                            copy_keys(c + 1)
                        if c:
                            copy_pT(c - 1)
                        exps(c)
                    copy_pT(NC - 1)
                    act.wait_ge(below_ready, n + 1)
                    nc.scalar.activation(weight[:], below[:], ACT.Exp, scale=SCALE).then_inc(weight_ready, 1)

            @block.vector
            def _(dve):
                dve.wait_ge(const_in, 16 * 8)
                nc.vector.memset(q_rows[:].rearrange("p a b c -> p (a b c)"), 0.0).then_inc(q_zero, 1)
                nc.vector.tensor_scalar(sign[:], map_of[:], keep["neg_lam"][:, 0:1], None, ALU.mult).then_inc(q_zero, 1)
                dve.wait_ge(q_zero, 2)
                nc.vector.tensor_tensor(sign[:, 0:1], sign[:, 0:1], map_of[:, 1:2], ALU.add).then_inc(q_zero, 1)
                dve.wait_ge(q_zero, 3)
                with dve.Fori(0, ND) as n:
                    count = Count(n * LINKS)
                    link = linker(dve, vec, count)

                    def copy_keys(c):
                        i = c % RG
                        for e in range(1, EV, 2):
                            dve.wait_ge(turned, n * (NC * EV) + (c * EV + e + 1))
                            dve.wait_ge(s_full, n * NC + max(0, c - RG + 1))
                            nc.vector.tensor_copy(kT[i][:, e // 2, 512:1024], turn[1][:]).then_inc(copied[1], 1)

                    def maxima(c):
                        i, kd = c % RG, kind(c)
                        dve.wait_ge(s_full, n * NC + (c + 1))
                        if kd:
                            link(nc.vector.tensor_reduce(chunk_max[:], s_ps[i][:, 0:2 * P], AX.X, ALU.max))
                        else:
                            dve.sem_inc(vec_gate, 1)
                            link(nc.vector.tensor_tensor_reduce(
                                out=s_win[:], in0=s_ps[i][:, 0:2 * P], in1=bias_win[:], scale=1.0, scalar=-BIG,
                                op0=ALU.add, op1=ALU.max, accum_out=chunk_max[:]))
                        old, new = (c % 2, (c + 1) % 2) if kd else (1, 0)
                        link(nc.vector.tensor_tensor(m[:, new, kd:kd + 1], m[:, old, kd:kd + 1], chunk_max[:], ALU.max))
                        nc.vector.tensor_scalar(shift[:, i:i + 1], m[:, new, kd:kd + 1], -SCALE, None,
                                                ALU.mult).then_inc(shift_ready, 1)

                    def add(c):
                        i, kd = c % RG, kind(c)
                        dve.wait_ge(exp_done, n * NC + (c + 1))
                        dve.wait_ge(l_added, n * NC + c)
                        nc.vector.scalar_tensor_tensor(out=l[:, kd:kd + 1], in0=l[:, kd:kd + 1],
                                                       scalar=alpha[:, i:i + 1], in1=l_chunk[:, i:i + 1],
                                                       op0=ALU.mult, op1=ALU.add).then_inc(l_added, 1)
                        dve.wait_ge(o_full, n * NC + (c + 1))
                        nc.vector.scalar_tensor_tensor(out=acc[:, kd, :], in0=acc[:, kd, :],
                                                       scalar=alpha[:, i:i + 1], in1=o_ps[:, :],
                                                       op0=ALU.mult, op1=ALU.add).then_inc(o_added, 1)

                    for c in range(2):
                        h = slice(c * HD, (c + 1) * HD)
                        for kd in range(2):
                            for g in range(NP):
                                src = keep["qsT"][h, kd * NP + g, bass.ds(n * TD, TD)]
                                at = g * 2 * TD + c * TD
                                dst = q_rows[h, kd, g, :].rearrange("p (j r) -> p j r", j=SL)[:, :, at:at + TD]
                                last = nc.vector.tensor_copy(dst, src.unsqueeze(1).broadcast_to([HD, SL, TD]))
                        last.then_inc(q_ready, 1)
                    copy_keys(0)
                    dve.wait_ge(new_scored, n + 1)
                    link(nc.vector.tensor_tensor(s_new[:], x_ps[:, 0:2 * TD].rearrange("p (a b) -> p a b", a=2),
                                                 bias_new[:], ALU.add))
                    nc.vector.tensor_reduce(m[:, 1, 0:1], s_new[:, 0, :], AX.X, ALU.max)
                    link(nc.vector.tensor_reduce(m[:, 0, 1:2], s_new[:, 1, :], AX.X, ALU.max))
                    nc.vector.tensor_scalar(shift_new[:, 0:1], m[:, 1, 0:1], -SCALE, None, ALU.mult)
                    nc.vector.tensor_scalar(shift_new[:, 1:2], m[:, 0, 1:2], -SCALE, None,
                                            ALU.mult).then_inc(new_shifted, 1)
                    copy_keys(1)
                    dve.wait_ge(new_exped, n * 2 + 2)
                    link(nc.vector.tensor_scalar(l[:], l_new[:], 1.0 / SL, None, ALU.mult))
                    dve.wait_ge(new_turned, n + 1)
                    nc.vector.tensor_scalar(pT_new[:], x_ps[0:TD, P:3 * P].rearrange("t (a b) -> t a b", a=2),
                                            1.0 / SL, None, ALU.mult).then_inc(new_pT, 1)
                    for kd in range(2):
                        dve.wait_ge(new_full, n * 2 + kd + 1)
                        nc.vector.tensor_copy(acc[:, kd, :], o_ps[:, :]).then_inc(new_taken, 1)
                    dve.wait_ge(new_taken, n * 2 + 2)
                    for c in range(NC):
                        if 1 <= c < NC - 1:
                            copy_keys(c + 1)
                        maxima(c)
                        if c:
                            add(c - 1)
                    add(NC - 1)
                    dve.wait_ge(m_turned, n + 1)
                    link(nc.vector.tensor_reduce(m_row[:], x_ps[0:2, 0:P].rearrange("k (j r) -> k r j", j=SL),
                                                 AX.X, ALU.max))
                    nc.vector.tensor_copy(m_rows[:], m_row[:].unsqueeze(1).broadcast_to([2, SL, ROWS])).then_inc(
                        m_spread_ready, 1)
                    dve.wait_ge(m_spread, n + 1)
                    nc.vector.tensor_tensor(below[:], m[:, 0, :], x_ps[:, 128:130], ALU.subtract).then_inc(below_ready, 1)
                    dve.wait_ge(o_added, n * NC + NC)
                    nc.vector.tensor_tensor(acc[:], acc[:], own_head[:], ALU.mult)
                    dve.wait_ge(weight_ready, n + 1)
                    dve.wait_ge(l_added, n * NC + NC)
                    nc.vector.tensor_tensor(lw[:], l[:], weight[:], ALU.mult).then_inc(lw_ready, 1)
                    dve.wait_ge(l_summed, n + 1)
                    link(nc.vector.reciprocal(coef[:], x_ps[:, 132:134]))
                    link(nc.vector.tensor_tensor(coef[:], coef[:], weight[:], ALU.mult))
                    link(nc.vector.tensor_tensor(coef[:, 1:2], coef[:, 1:2], sign[:, 0:1], ALU.mult))
                    for kd in range(2):
                        ins = nc.vector.tensor_scalar(comb[:, kd, :], token[:], coef[:, kd:kd + 1], None, ALU.mult)
                    ins.then_inc(comb_ready, 1)
                    dve.wait_ge(mixed, n + 1)
                    nc.vector.tensor_copy(keep["mixsT"][:, :, bass.ds(n * TD, TD)],
                                          x_ps[:, 136:136 + 2 * NP * TD].rearrange("p (g t) -> p g t", t=TD)).then_inc(
                                              mix_kept, 1)
                    assert count.n == LINKS, count.n


def mlp(nc, io, keep):
    TB = 4
    NB = NT // TB
    DB = 4
    DP = 2 * TB
    NF = 4
    NH = NP
    with ExitStack() as ctx:
        sb = lambda n, s, d=F32: ctx.enter_context(nc.sbuf_tensor(n, s, d))
        ps = lambda n: ctx.enter_context(nc.psum_tensor(n, [P, 512], F32))
        sem = lambda n: ctx.enter_context(nc.semaphore(n))
        w_out = sb("d_w_out", [P, KC, D])
        w_up = [sb(f"d_w_up{i}", [P, KC, 512]) for i in range(2)]
        w_down = [sb(f"d_w_down{i}", [P, NF, D]) for i in range(2)]
        mix = sb("d_mix", [P, KC, 512])
        y = [sb(f"d_y{i}", [P, TB, D]) for i in range(2)]
        hs = [sb(f"d_hs{i}", [P, D]) for i in range(2)]
        hT = sb("d_hT", [P, KC, 512])
        uT = [sb(f"d_uT{i}", [P, NF, 512]) for i in range(2)]
        square = sb("d_square", [P, 512])
        root = sb("d_root", [P, 512])
        gain_mlp = sb("d_gain_mlp", [P, KC])
        gain_head = sb("d_gain_head", [P, 1])
        gain_last = sb("d_gain_last", [P, D])
        ones = sb("d_ones", [P, P])
        fold = sb("d_fold", [P, P])
        stat = sb("d_stat", [P, 4])
        d_ps = [ps(f"d_dps{i}") for i in range(DB)]
        u_ps = [ps(f"d_ups{i}") for i in range(2)]
        t_ps = [ps(f"d_tps{i}") for i in range(2)]

        const_in, out_in = sem("d_const_in"), sem("d_out_in")
        up_in = [sem(f"d_up_in{i}") for i in range(2)]
        down_in = [sem(f"d_down_in{i}") for i in range(2)]
        mix_in, y_in = sem("d_mix_in"), sem("d_y_in")
        ones_ready, gain_ready = sem("d_ones_ready"), sem("d_gain_ready")
        squared, summed = sem("d_squared"), sem("d_summed")
        var_ready, rooted = sem("d_var_ready"), sem("d_rooted")
        mix_ready = sem("d_mix_ready")
        d_full, d_used = sem("d_d_full"), sem("d_d_used")
        u_full, u_relued, u_used = sem("d_u_full"), sem("d_u_relued"), sem("d_u_used")
        row_squared, row_var, row_rooted = sem("d_row_squared"), sem("d_row_var"), sem("d_row_rooted")
        hs_ready, h_turned, hT_ready = sem("d_hs_ready"), sem("d_h_turned"), sem("d_hT_ready")
        y_ready = sem("d_y_ready")
        stored = [sem(f"d_stored{i}") for i in range(2)]
        vec = sem("d_vec")
        sp_gate = sem("d_sp_gate")
        u4_ready, f_full, f_used = sem("d_u4_ready"), sem("d_f_full"), sem("d_f_used")

        BLOCK_D = DP * (1 + FG)
        BLOCK_U = NF * FG

        with nc.Block() as block:
            def load_up(sp, g, i):
                src = io["w_up"].rearrange("(c p) (g n) -> g p c n", p=P, g=FG)[bass.ds(g, 1)]
                sp.dma_start(w_up[i][:], src.rearrange("o p c n -> (o p) c n")).then_inc(up_in[i], 16)

            def load_down(sp, g, i):
                src = io["w_down"].rearrange("(g f p) n -> g p f n", p=P, f=NF)[bass.ds(g, 1)]
                sp.dma_start(w_down[i][:], src.rearrange("o p f n -> (o p) f n")).then_inc(down_in[i], 16)

            @block.sync
            def _(sp):
                def load_mix(blk):
                    src = io["mixT"].rearrange("c p n -> p c n")[:, :, blk * 512:(blk + 1) * 512]
                    sp.dma_start(mix[:], src).then_inc(mix_in, 16)

                def load_x(blk):
                    if blk < NB:
                        src = io["x_prompt"].rearrange("(b t p) d -> b p t d", p=P, t=TB)[blk]
                        sp.dma_start(y[blk % 2][:], src).then_inc(y_in, 16)
                    else:
                        sp.dma_start(y[blk % 2][0:NS, 0, :], io["x_sample"]).then_inc(y_in, 16)

                load_mix(0)
                sp.dma_start(gain_mlp[:], io["norm_mlp"]).then_inc(const_in, 16)
                sp.dma_start(gain_head[:], io["subln_gain"]).then_inc(const_in, 16)
                sp.dma_start(gain_last[:], io["final_norm"].broadcast_to([P, D])).then_inc(const_in, 16)
                sp.dma_start(fold[:], io["same_row"]).then_inc(const_in, 16)
                sp.dma_start(w_out[:], io["w_out"].rearrange("(c p) n -> p c n", p=P)).then_inc(out_in, 16)
                load_x(0)
                for g in range(2):
                    load_up(sp, g, g)
                    load_down(sp, g, g)
                for blk in range(NB + 1):
                    if blk < NB:
                        sp.wait_ge(d_full, blk * BLOCK_D + DP)
                        if blk + 1 < NB:
                            load_mix(blk + 1)
                        if blk >= 1:
                            sp.wait_ge(stored[(blk + 1) % 2], 16 * TB * ((blk + 1) // 2))
                        load_x(blk + 1)
                    group_u, group_d = (NF, DP) if blk < NB else (1, 2)
                    base_d = blk * BLOCK_D + (DP if blk < NB else 2)

                    def reload(gg, i):
                        sp.wait_ge(u_full, gg * (2 * group_u) + (blk * BLOCK_U + (i + 1) * group_u))
                        sp.sem_inc(sp_gate, 1)
                        g = (2 * gg + 2 + i) % FG if isinstance(gg, int) else gg * 2 + (2 + i)
                        load_up(sp, g, i)
                        sp.wait_ge(d_full, gg * (2 * group_d) + (base_d + (i + 1) * group_d))
                        sp.sem_inc(sp_gate, 1)
                        load_down(sp, g, i)

                    with sp.Fori(0, FG // 2 - 1) as gg:
                        for i in range(2):
                            reload(gg, i)
                    if blk < NB:
                        for i in range(2):
                            reload(FG // 2 - 1, i)

            @block.gpsimd
            def _(pool):
                for blk in range(NB):
                    for t in range(TB):
                        pool.wait_ge(y_ready, blk * TB + t + 1)
                        dst = io["y_p"].rearrange("(b t p) d -> b t p d", p=P, t=TB)[blk, t]
                        pool.dma_start(dst, y[blk % 2][:, t, :]).then_inc(stored[blk % 2], 16)
                pool.wait_ge(y_ready, NB * TB + 1)
                pool.dma_start(io["y_s"], y[NB % 2][0:NS, 0, :]).then_inc(stored[NB % 2], 16)
                for i in range(2):
                    pool.wait_ge(stored[i], 16 * TB * (NB // 2) + 16 * (NB % 2 == i))

            @block.tensor
            def _(pe):
                pe.wait_ge(const_in, 64)
                pe.wait_ge(ones_ready, 1)
                turns = Count()

                def bank():
                    n = turns.n
                    turns.up()
                    if n >= 2:
                        pe.wait_ge(hT_ready, n - 1)
                    return t_ps[n % 2]

                def head_sums(blk):
                    heads, cols = (NH, 512) if blk < NB else (1, NH * NS)
                    for h in range(heads):
                        pe.wait_ge(squared, blk * NH + h + 1)
                        dst = bank()
                        nc.tensor.matmul(dst[:, 0:cols], ones[:], square[:, 0:cols], start=True,
                                         stop=True).then_inc(summed, 1)

                def project_out(blk, t):
                    rows = P if blk < NB else NS
                    if t == 0:
                        pe.wait_ge(mix_ready, min(blk, NB) * NH + (NH if blk < NB else 1))
                    for half in range(2):
                        n = blk * BLOCK_D + 2 * t + half
                        if n >= DB:
                            pe.wait_ge(d_used, n - DB + 1)
                        for c in range(KC):
                            lhs = mix[:, c, t * P:(t + 1) * P] if blk < NB else keep["mixsT"][:, c, :]
                            last = nc.tensor.matmul(d_ps[n % DB][0:rows, :], lhs,
                                                    w_out[:, c, half * 512:(half + 1) * 512],
                                                    start=(c == 0), stop=(c == KC - 1))
                        last.then_inc(d_full, 1)

                def turn_h(blk, t):
                    rows = P if blk < NB else NS
                    pe.wait_ge(hs_ready, blk * TB + t + 1)
                    for half in range(2):
                        dst = bank()
                        for c in range(4):
                            last = nc.tensor.transpose(dst[:, c * P:c * P + rows],
                                                       hs[t % 2][0:rows, (4 * half + c) * P:(4 * half + c + 1) * P],
                                                       keep["ident"][0:rows, 0:rows])
                        last.then_inc(h_turned, 1)

                pe.wait_ge(mix_in, 16)
                head_sums(0)
                pe.wait_ge(out_in, 16)
                for blk in range(NB):
                    project_out(blk, 0)
                    for t in range(TB):
                        if t + 1 < TB:
                            project_out(blk, t + 1)
                        turn_h(blk, t)
                    pe.wait_ge(hT_ready, turns.n)
                    with pe.Fori(0, FG // 2) as gg:
                        for i in range(2):
                            pe.wait_ge(up_in[i], gg * 16 + (blk * (FG // 2) + 1) * 16)
                            for f in range(NF):
                                n = blk * BLOCK_U + i * NF + f
                                if blk == 0 and i == 0 and f < 2:
                                    pe.wait_ge(u_used, gg * (2 * NF))
                                else:
                                    pe.wait_ge(u_used, gg * (2 * NF) + (n - 1))
                                for c in range(KC):
                                    last = nc.tensor.matmul(u_ps[f % 2][:, :], w_up[i][:, c, f * P:(f + 1) * P],
                                                            hT[:, c, :], start=(c == 0), stop=(c == KC - 1))
                                last.then_inc(u_full, 1)
                            pe.wait_ge(down_in[i], gg * 16 + (blk * (FG // 2) + 1) * 16)
                            for t in range(TB):
                                for half in range(2):
                                    n = blk * BLOCK_D + DP + i * DP + 2 * t + half
                                    pe.wait_ge(d_used, gg * (2 * DP) + (n - DB + 1))
                                    for f in range(NF):
                                        if t == 0 and half == 0:
                                            pe.wait_ge(u_used, gg * (2 * NF) + (blk * BLOCK_U + i * NF + f + 1))
                                        last = nc.tensor.matmul(d_ps[n % DB][:, :], uT[i][:, f, t * P:(t + 1) * P],
                                                                w_down[i][:, f, half * 512:(half + 1) * 512],
                                                                start=(f == 0), stop=(f == NF - 1))
                                    last.then_inc(d_full, 1)
                    head_sums(blk + 1)
                d0 = NB * BLOCK_D
                project_out(NB, 0)
                turn_h(NB, 0)
                pe.wait_ge(hT_ready, turns.n)
                with pe.Fori(0, FG // 2) as gg:
                    for i in range(2):
                        pe.wait_ge(up_in[i], gg * 16 + (NB * (FG // 2) + 1) * 16)
                        n = NB * BLOCK_U + i
                        pe.wait_ge(u_used, gg * 2 + n)
                        for c in range(KC):
                            j = c % 4
                            last = nc.tensor.matmul(u_ps[0][NS * j:NS * (j + 1), :], hT[:, c, 0:NS], w_up[i][:, c, :],
                                                    start=(c < 4), stop=(c >= 4))
                        last.then_inc(u_full, 1)
                        pe.wait_ge(u4_ready, gg * 2 + (i + 1))
                        for f in range(NF):
                            last = nc.tensor.matmul(u_ps[1][:, f * NS:(f + 1) * NS], square[:, f * P:(f + 1) * P],
                                                    fold[:, 0:NS], start=True, stop=True)
                        last.then_inc(f_full, 1)
                        pe.wait_ge(u_used, gg * 2 + (n + 1))
                        pe.wait_ge(down_in[i], gg * 16 + (NB * (FG // 2) + 1) * 16)
                        pe.wait_ge(d_used, gg * 4 + (d0 + 2 + 2 * i))
                        for f in range(NF):
                            for half in range(2):
                                last = nc.tensor.matmul(d_ps[half][NS * f:NS * (f + 1), :], uT[i][:, f, 0:NS],
                                                        w_down[i][:, f, half * 512:(half + 1) * 512],
                                                        start=True, stop=True)
                            if f >= NF - 1:
                                last.then_inc(d_full, 2)
                pe.wait_ge(d_used, d0 + 2 + 2 * FG)
                for half in range(2):
                    nc.tensor.matmul(d_ps[2 + half][0:NS, :], fold[:, 0:NS], hs[1][:, half * 512:(half + 1) * 512],
                                     start=True, stop=True).then_inc(d_full, 1)

            @block.scalar
            def _(act):
                row_events = Count()

                def head_roots(blk):
                    if blk < NB:
                        act.wait_ge(mix_in, 16 * (blk + 1))
                    heads, cols = (NH, 512) if blk < NB else (1, NH * NS)
                    for h in range(heads):
                        n = blk * NH + h
                        src = mix[:, NP + h, :] if blk < NB else keep["mixsT"][:, NP:2 * NP, :]
                        dst = square[:, 0:cols] if blk < NB else square[:, 0:cols].rearrange("p (a b) -> p a b", a=NH)
                        if n:
                            act.wait_ge(summed, n)
                        nc.scalar.activation(dst, src, ACT.Square).then_inc(squared, 1)
                        act.wait_ge(var_ready, n + 1)
                        nc.scalar.activation(root[:, 0:cols], root[:, 0:cols], ACT.Sqrt).then_inc(rooted, 1)

                def row_root(rows, src, junk, ready):
                    ready()
                    nc.scalar.activation(junk, src, ACT.Square, accum_out=stat[0:rows, 0:1]).then_inc(row_squared, 1)
                    act.wait_ge(row_var, row_events.up())
                    nc.scalar.activation(stat[0:rows, 2:3], stat[0:rows, 1:2], ACT.Sqrt).then_inc(row_rooted, 1)

                def early(blk, t):
                    rows = P if blk < NB else NS

                    def ready():
                        act.wait_ge(d_used, blk * BLOCK_D + 2 * (t + 1))
                        if blk * TB + t >= 2:
                            act.wait_ge(h_turned, 2 * (blk * TB + t - 1))

                    row_root(rows, y[blk % 2][0:rows, t, :], hs[t % 2][0:rows], ready)

                def late(blk, t):
                    rows = P if blk < NB else NS

                    def ready():
                        act.wait_ge(d_used, (blk + 1) * BLOCK_D if blk < NB else NB * BLOCK_D + 2 + 2 * FG + 2)
                        if blk < NB:
                            act.wait_ge(h_turned, 2 * TB * (blk + 1))

                    row_root(rows, y[blk % 2][0:rows, t, :], hs[0][0:rows], ready)

                head_roots(0)
                for blk in range(NB):
                    for t in range(TB):
                        early(blk, t)
                    with act.Fori(0, FG // 2) as gg:
                        for i in range(2):
                            for f in range(NF):
                                n = blk * BLOCK_U + i * NF + f
                                act.wait_ge(u_full, gg * (2 * NF) + (n + 1))
                                act.wait_ge(d_full, gg * (2 * DP) + (blk * BLOCK_D + i * DP))
                                nc.scalar.activation(uT[i][:, f, :], u_ps[f % 2][:], ACT.Relu).then_inc(u_relued, 1)
                    head_roots(blk + 1)
                    for t in range(TB):
                        late(blk, t)
                early(NB, 0)
                with act.Fori(0, FG // 2) as gg:
                    for i in range(2):
                        act.wait_ge(u_full, gg * 2 + (NB * BLOCK_U + i + 1))
                        act.wait_ge(f_full, gg * 2 + i)
                        nc.scalar.copy(square[:], u_ps[0][:]).then_inc(u4_ready, 1)
                        act.wait_ge(f_full, gg * 2 + (i + 1))
                        act.wait_ge(d_full, gg * 4 + (NB * BLOCK_D + 2 * i))
                        nc.scalar.activation(uT[i][:, :, 0:NS], u_ps[1][:, 0:NF * NS].rearrange(
                            "p (f n) -> p f n", f=NF), ACT.Relu).then_inc(u_relued, 1)
                late(NB, 0)

            @block.vector
            def _(dve):
                link = linker(dve, vec, Count())
                row_events = Count()
                dve.wait_ge(const_in, 64)
                nc.vector.memset(ones[:], 1.0).then_inc(ones_ready, 1)
                link(nc.vector.tensor_scalar(gain_head[:], gain_head[:], 1.0 - LAMBDA_INIT, None, ALU.mult))

                def head_norms(blk):
                    heads, cols = (NH, 512) if blk < NB else (1, NH * NS)
                    for h in range(heads):
                        n = blk * NH + h
                        dve.wait_ge(summed, n + 1)
                        nc.vector.tensor_scalar(root[:, 0:cols], t_ps[sum_bank[n] % 2][:, 0:cols], 1.0 / P, SUB_EPS,
                                                ALU.mult, ALU.add).then_inc(var_ready, 1)
                        dve.wait_ge(var_ready, n + 1)
                        dve.sem_inc(hT_ready, 1)
                        dve.wait_ge(rooted, n + 1)
                        link(nc.vector.reciprocal(root[:, 0:cols], root[:, 0:cols]))
                        if blk < NB:
                            m, r = mix[:, NP + h, :], root[:, 0:cols]
                        else:
                            m, r = keep["mixsT"][:, NP:2 * NP, :], root[:, 0:cols].rearrange("p (a b) -> p a b", a=NH)
                        nc.vector.scalar_tensor_tensor(out=m, in0=m, scalar=gain_head[:, 0:1], in1=r,
                                                       op0=ALU.mult, op1=ALU.mult).then_inc(mix_ready, 1)
                        dve.wait_ge(mix_ready, n + 1)

                def row_norm(rows):
                    n = row_events.up()
                    dve.wait_ge(row_squared, n)
                    nc.vector.tensor_scalar(stat[0:rows, 1:2], stat[0:rows, 0:1], 1.0 / D, EPS,
                                            ALU.mult, ALU.add).then_inc(row_var, 1)
                    dve.wait_ge(row_rooted, n)
                    link(nc.vector.reciprocal(stat[0:rows, 3:4], stat[0:rows, 2:3]))

                def residual(blk, t):
                    rows = P if blk < NB else NS
                    if t == 0:
                        dve.wait_ge(y_in, 16 * (blk + 1))
                    for half in range(2):
                        n = blk * BLOCK_D + 2 * t + half
                        part = y[blk % 2][0:rows, t, half * 512:(half + 1) * 512]
                        dve.wait_ge(d_full, n + 1)
                        nc.vector.tensor_tensor(part, part, d_ps[n % DB][0:rows, :], ALU.add).then_inc(d_used, 1)

                def normed(blk, t):
                    rows = P if blk < NB else NS
                    row_norm(rows)
                    nc.vector.tensor_scalar(hs[t % 2][0:rows], y[blk % 2][0:rows, t, :], stat[0:rows, 3:4], None,
                                            ALU.mult).then_inc(hs_ready, 1)

                def spread(blk, t):
                    rows = P if blk < NB else NS
                    if t == 0 and blk:
                        dve.wait_ge(u_full, blk * BLOCK_U)
                    for half in range(2):
                        dve.wait_ge(h_turned, 2 * (blk * TB + t) + half + 1)
                        src = t_ps[turn_bank[blk * TB + t] % 2 ^ half][:].rearrange("p (c n) -> p c n", c=4)[:, :, 0:rows]
                        g = gain_mlp[:, 4 * half:4 * half + 4].unsqueeze(2).broadcast_to([P, 4, rows])
                        nc.vector.tensor_tensor(hT[:, 4 * half:4 * half + 4, t * P:t * P + rows], src, g,
                                                ALU.mult).then_inc(hT_ready, 1)

                def last_norm(blk, t):
                    rows = P if blk < NB else NS
                    row_norm(rows)
                    part = y[blk % 2][0:rows, t, :]
                    nc.vector.scalar_tensor_tensor(out=part, in0=part, scalar=stat[0:rows, 3:4],
                                                   in1=gain_last[0:rows], op0=ALU.mult,
                                                   op1=ALU.mult).then_inc(y_ready, 1)

                sum_bank, turn_bank, at = {}, {}, 0
                for blk in range(NB + 1):
                    for h in range(NH if blk < NB else 1):
                        sum_bank[blk * NH + h] = at
                        at += 1
                    for t in range(TB if blk < NB else 1):
                        turn_bank[blk * TB + t] = at
                        at += 2

                head_norms(0)
                for blk in range(NB):
                    residual(blk, 0)
                    for t in range(TB):
                        normed(blk, t)
                        if t + 1 < TB:
                            residual(blk, t + 1)
                        spread(blk, t)
                    with dve.Fori(0, FG // 2) as gg:
                        for i in range(2):
                            for f in range(NF):
                                n = blk * BLOCK_U + i * NF + f
                                dve.wait_ge(u_relued, gg * (2 * NF) + (n + 1))
                                nc.vector.tensor_tensor(uT[i][:, f, :], uT[i][:, f, :], u_ps[f % 2][:],
                                                        ALU.mult).then_inc(u_used, 1)
                            for t in range(TB):
                                for half in range(2):
                                    n = blk * BLOCK_D + DP + i * DP + 2 * t + half
                                    part = y[blk % 2][:, t, half * 512:(half + 1) * 512]
                                    dve.wait_ge(d_full, gg * (2 * DP) + (n + 1))
                                    nc.vector.tensor_tensor(part, part, d_ps[n % DB][:], ALU.add).then_inc(d_used, 1)
                    head_norms(blk + 1)
                    for t in range(TB):
                        last_norm(blk, t)
                d0 = NB * BLOCK_D
                residual(NB, 0)
                normed(NB, 0)
                spread(NB, 0)
                link(nc.vector.memset(hs[1][:], 0.0))
                with dve.Fori(0, FG // 2) as gg:
                    for i in range(2):
                        dve.wait_ge(u_relued, gg * 2 + (NB * BLOCK_U + i + 1))
                        nc.vector.tensor_tensor(uT[i][:, :, 0:NS], uT[i][:, :, 0:NS],
                                                u_ps[1][:, 0:NF * NS].rearrange("p (f n) -> p f n", f=NF),
                                                ALU.mult).then_inc(u_used, 1)
                        dve.wait_ge(d_full, gg * 4 + (d0 + 2 + 2 * (i + 1)))
                        for half in range(2):
                            part = hs[1][:, half * 512:(half + 1) * 512]
                            nc.vector.tensor_tensor(part, part, d_ps[half][:], ALU.add).then_inc(d_used, 1)
                for half in range(2):
                    dve.wait_ge(d_full, d0 + 2 + 2 * FG + half + 1)
                    part = y[NB % 2][0:NS, 0, half * 512:(half + 1) * 512]
                    nc.vector.tensor_tensor(part, part, d_ps[2 + half][0:NS, :], ALU.add).then_inc(d_used, 1)
                last_norm(NB, 0)


def build(nc, io):
    with ExitStack() as ctx:
        sb = lambda n, s: ctx.enter_context(nc.sbuf_tensor(n, s, F32))
        keep = {"ident": sb("ident", [P, P]), "qsT": sb("qsT", [P, 2 * NP, NS]), "ksT": sb("ksT", [P, 2 * NP, NS]),
                "mixsT": sb("mixsT", [P, 2 * NP, NS]), "neg_lam": sb("neg_lam", [P, 1])}
        for name, dt in (("qT", F32), ("kT", F32), ("mixT", F32)):
            io[name] = nc.dram_tensor(name, [2 * NP, P, S], dt, kind="Internal").ap()
        project(nc, io, keep)
        attend_prompt(nc, io, keep)
        attend_decode(nc, io, keep)
        mlp(nc, io, keep)


def rope_tables():
    half = ROT // 2
    inv = np.float32(THETA) ** (-np.arange(half, dtype=np.float32) * np.float32(2.0) / np.float32(ROT))
    pos = np.zeros((NT + 1, P), np.float32)
    pos[:NT] = np.arange(S).reshape(NT, P)
    pos[NT, :NS] = PAGES * PAGE + np.arange(NS) % TD
    ang = (pos[:, :, None] * inv).astype(np.float32).astype(np.float64)
    cos, sin = np.cos(ang), np.sin(ang)
    lay = lambda a: np.ascontiguousarray(a.transpose(1, 0, 2).astype(np.float32))
    return lay(np.concatenate([cos, cos], -1)), lay(np.concatenate([-sin, sin], -1))


def log_reads(dist):
    reads = sum(((dist >= 0) & (dist <= w) & (dist % d == 0)).astype(np.float64) for w, d in BRANCHES)
    return np.where(reads > 0, np.log(np.maximum(reads, 1)) / SCALE, NEG).astype(np.float32)


def decode_constants():
    row = np.arange(SL * ROWS)
    slot, pair, which, t = row // ROWS, row % ROWS // (2 * TD), row % (2 * TD) // TD, row % TD
    key = np.arange(P)
    pos = np.stack([16 * (g * 32 + key // TD) + key % TD for g in range(3)]
                   + [1536 + g * P + key for g in range(4)] + [np.full(P, 2 * WIN)])
    pos = pos.reshape(SL, 2 * P)[slot]
    win = log_reads(np.where(pos < WIN, WIN + t[:, None] - pos, -1))
    ago = t[:, None] - np.arange(TD)[None, :]
    new = np.stack([log_reads(ago), np.where(ago >= 0, 0, NEG).astype(np.float32)], 1)
    col = np.arange(GW)
    same_pair = pair[:, None] == col[None, :] // P
    own = np.stack([same_pair & (which[:, None] == col[None, :] % P // HD), same_pair], 1)
    f = lambda a: np.ascontiguousarray(a.astype(np.float32))
    return {"bias_win": f(win), "bias_new": f(new), "own_head": f(own),
            "same_row": f(row[:, None] % ROWS == row[None, :] % ROWS),
            "token": f(t[:, None] == np.arange(TD)[None, :]), "map_of": f(np.stack([which == 1, which == 0], 1))}


def constants():
    cos, sin = rope_tables()
    dist = (NT - 1) * P + np.arange(P)[:, None] - np.arange(S)[None, :]
    return {"ident": np.eye(P, dtype=np.float32), "cos": cos, "sin": sin,
            "bias_dilated": log_reads(dist), "bias_causal": np.where(dist >= 0, 0, NEG).astype(np.float32),
            **decode_constants()}


OUTPUTS = (("y_p", (1, S, D)), ("y_s", (ND, TD, D)), ("kb_p", (1, 1, S, 4, 2 * HD)), ("vb_p", (1, 1, S, 4, 2 * HD)),
           ("ka_p", (1, 1, S, 8, HD)), ("va_p", (1, 1, S, 8, HD)),
           ("kb_s", (1, ND, TD, 4, 2 * HD)), ("vb_s", (1, ND, TD, 4, 2 * HD)),
           ("ka_win", (1, ND, WIN, 8, HD)), ("va_win", (1, ND, WIN, 8, HD)))
SHAPES = {"y_p": (S, D), "y_s": (NS, D), "kb_p": (S, GW), "vb_p": (S, GW), "ka_p": (S, GW), "va_p": (S, GW),
          "kb_s": (NS, GW), "vb_s": (NS, GW), "ka_win": (ND, WIN, GW), "va_win": (ND, WIN, GW)}


def lay_out(inputs):
    a = {k: np.asarray(v) for k, v in inputs.items()}
    by_chunk = lambda v: np.ascontiguousarray(v.reshape(-1, P).T)
    out = {
        "x_prompt": a["x_prompt"].reshape(S, D), "x_sample": a["x_sample"].reshape(NS, D),
        "ka_state": a["state_win_k"].reshape(ND, WIN, GW), "va_state": a["state_win_v"].reshape(ND, WIN, GW),
        "k_cache": a["cache_diff_k"].reshape(NPHYS, PAGE, GW), "v_cache": a["cache_diff_v"].reshape(NPHYS, PAGE, GW),
        "page_table": a["page_table"].reshape(1, ND * PAGES),
        "norm_attn": by_chunk(a["norm_attn"]), "norm_mlp": by_chunk(a["norm_mlp"]),
        "final_norm": a["final_norm"].reshape(1, D), "subln_gain": a["subln_gain"].reshape(P, 1),
        "lambdas": np.stack([a[k].reshape(HD) for k in ("lambda_q1", "lambda_q2", "lambda_k1", "lambda_k2")]).reshape(1, 4 * HD),
        "w_in": a["w_in"][0], "w_out": a["w_out"][0], "w_up": a["w_up"][0], "w_down": a["w_down"][0],
    }
    out.update(constants())
    return {k: np.ascontiguousarray(v) for k, v in out.items()}


def kernel(**inputs):
    import concourse.bacc as bacc
    from concourse.bass_utils import run_bass_kernel_spmd

    nc = bacc.Bacc("TRN2", target_bir_lowering=False, num_devices=1)
    arrays = lay_out(inputs)
    io = {k: nc.dram_tensor("in_" + k, v.shape, mybir.dt.from_np(v.dtype), kind="ExternalInput").ap()
          for k, v in arrays.items()}
    for k, _ in OUTPUTS:
        io[k] = nc.dram_tensor("out_" + k, SHAPES[k], F32, kind="ExternalOutput").ap()
    build(nc, io)
    r = run_bass_kernel_spmd(nc, [{"in_" + k: v for k, v in arrays.items()}], core_ids=[0])
    return tuple(np.asarray(r.results[0]["out_" + k]).reshape(s) for k, s in OUTPUTS)
```

```python
import math
from contextlib import ExitStack

import numpy as np

import concourse.bass as bass
import concourse.mybir as mybir

F32 = mybir.dt.float32
I32 = mybir.dt.int32
ALU = mybir.AluOpType
ACT = mybir.ActivationFunctionType
AX = mybir.AxisListType

P = 128
D = 1024
S = 2048
ND, TD = 8, 4
NS = ND * TD
HD = 64
GW = 512
NP = GW // P
FF = 4096
WIN = 2048
PAGES, PAGE = 64, 128
NPHYS = 640
BRANCHES = ((128, 1), (512, 4), (2048, 16))
KC = D // P
NT = S // P
ROT = HD // 4
THETA = 500000.0
SCALE = HD ** -0.5
LAMBDA_INIT = 0.8 - 0.6 * math.exp(0.0)
NEG = -1.0e30
BIG = 3.0e38
EPS, SUB_EPS = 1e-6, 1e-5
FG = FF // 512


class Count:

    def __init__(self, base=0):
        self.base, self.n = base, 0

    def up(self, k=1):
        self.n += k
        return self.base + self.n


def linker(eng, sem, count):
    def link(ins):
        ins.then_inc(sem, 1)
        eng.wait_ge(sem, count.up())
    return link


def project(nc, io, keep):
    GROUPS = ("qa", "ka", "qb", "kb", "va", "vb")
    COLS = {"qa": 0, "ka": 1, "va": 2, "qb": 3, "kb": 4, "vb": 5}
    NG, NR = 6, 4
    ZB = 4
    with ExitStack() as ctx:
        sb = lambda n, s, d=F32: ctx.enter_context(nc.sbuf_tensor(n, s, d))
        ps = lambda n: ctx.enter_context(nc.psum_tensor(n, [P, 512], F32))
        sem = lambda n: ctx.enter_context(nc.semaphore(n))
        w_in = sb("a_w_in", [P, KC, NG * GW])
        gain = sb("a_gain", [P, KC])
        cos = sb("a_cos", [P, NT + 1, ROT])
        sin = sb("a_sin", [P, NT + 1, ROT])
        x = [sb(f"a_x{b}", [P, D]) for b in range(2)]
        xs = sb("a_xs", [P, D])
        xT = [sb(f"a_xT{b}", [P, KC, P]) for b in range(2)]
        stat = sb("a_stat", [P, 4])
        z = [sb(f"a_z{b}", [P, NG, GW]) for b in range(2)]
        rot = sb("a_rot", [P, 2, GW // HD, ROT])
        zT = [sb(f"a_zT{b}", [P, NR, NP, P]) for b in range(2)]
        x_turn = [ps(f"a_turn{i}") for i in range(2)]
        z_ps = [ps(f"a_zps{i}") for i in range(ZB)]
        z_turn = [ps(f"a_zturn{i}") for i in range(2)]

        const_in = sem("a_const_in")
        w_landed = [sem(f"a_w_landed{i}") for i in range(NG)]
        x_landed = [sem(f"a_x_landed{b}") for b in range(2)]
        squared = sem("a_squared")
        var_ready = sem("a_var_ready")
        root_ready = sem("a_root_ready")
        xs_ready = sem("a_xs_ready")
        x_turned = sem("a_x_turned")
        xT_ready = sem("a_xT_ready")
        z_summed = sem("a_z_summed")
        z_free = sem("a_z_free")
        rotated = sem("a_rotated")
        z_turned = sem("a_z_turned")
        zT_ready = sem("a_zT_ready")
        stored = [sem(f"a_stored{b}") for b in range(2)]
        vec = sem("a_vec")
        VEC = NR + 1
        copied = sem("a_copied")

        w_cols = io["w_in"].rearrange("(c p) (g n) -> g p c n", p=P, g=NG)
        order = [GROUPS[i] for i in range(NG)]

        def rows_of(it):
            return NS if isinstance(it, int) and it == NT else P

        def phase(prologue, step):
            def run(eng):
                prologue()
                with eng.Fori(0, (NT - 2) // 2) as p:
                    for b in range(2):
                        step(p * 2 + b, b)
                for it in range(NT - 2, NT + 1):
                    step(it, it % 2)
            return run

        with nc.Block() as block:
            @block.sync
            def _(sp):
                def load(it, b):
                    src = io["x_sample"] if rows_of(it) == NS else io["x_prompt"].rearrange(
                        "(t p) d -> t p d", p=P)[bass.ds(it, 1)].rearrange("o p d -> (o p) d")
                    sp.dma_start(x[b][0:rows_of(it)], src).then_inc(x_landed[b], 16)

                def prologue():
                    for b in range(2):
                        sp.sem_inc(stored[b], 1)
                    load(0, 0)
                    load(1, 1)
                    for name, dst in (("norm_attn", gain), ("cos", cos), ("sin", sin), ("ident", keep["ident"])):
                        sp.dma_start(dst[:], io[name]).then_inc(const_in, 16)
                    for i, g in enumerate(order):
                        sp.dma_start(w_in[:, :, COLS[g] * GW:(COLS[g] + 1) * GW],
                                     w_cols[COLS[g]]).then_inc(w_landed[i], 16)

                def step(it, b):
                    r = rows_of(it)
                    if not isinstance(it, int) or it < NT - 1:
                        sp.wait_ge(xs_ready, it + 1)
                        load(it + 2, b)
                    if r == NS:
                        for i, g in enumerate(order):
                            if i < NR:
                                sp.wait_ge(rotated, it * NR + i + 1)
                            else:
                                sp.wait_ge(z_free, it * NG + (ZB + i + 1))
                            if g in ("kb", "vb"):
                                sp.dma_start(io[g + "_s"], z[b][0:NS, i, :]).then_inc(stored[b], 16)
                            elif g in ("ka", "va"):
                                for n in range(ND):
                                    sp.dma_start(io[g + "_win"][n, WIN - TD:WIN, :],
                                                 z[b][n * TD:(n + 1) * TD, i, :]).then_inc(stored[b], 16)
                        for n in range(2):
                            sp.wait_ge(stored[n], 1 + 16 * 8 * (NT // 2) + (16 * (2 + 2 * ND) if n == b else 0))
                        return
                    for i, g in enumerate(order):
                        if g[0] == "q":
                            continue
                        if i < NR:
                            sp.wait_ge(rotated, it * NR + (i + 1))
                        else:
                            sp.wait_ge(z_free, it * NG + (ZB + i + 1))
                        dst = io[g + "_p"].rearrange("(t p) n -> t p n", p=P)[bass.ds(it, 1)]
                        sp.dma_start(dst.rearrange("o p n -> (o p) n"), z[b][:, i, :]).then_inc(stored[b], 16)
                    for i, g in enumerate(order[:NR]):
                        sp.wait_ge(zT_ready, it * NR + (2 + i + 1))
                        dst = io[g[0] + "T"].rearrange("g p (t n) -> t p g n", n=P)[bass.ds(it, 1)]
                        at = 0 if g[1] == "a" else NP
                        sp.dma_start(dst[:, :, at:at + NP].rearrange("o p g n -> (o p) g n"),
                                     zT[b][:, i]).then_inc(stored[b], 16)

                phase(prologue, step)(sp)

            @block.gpsimd
            def _(pool):
                body = (WIN - TD) // 16 * 16
                for landed in w_landed:
                    pool.wait_ge(landed, 16)
                with pool.Fori(0, ND) as n:
                    pool.wait_ge(xs_ready, n * 2 + 1)
                    for k in ("ka", "va"):
                        src = io[k + "_state"][bass.ds(n, 1)].rearrange("o t n -> (o t) n")
                        dst = io[k + "_win"][bass.ds(n, 1)].rearrange("o t n -> (o t) n")
                        pool.dma_start(dst[0:body].rearrange("(a b) n -> a b n", a=16),
                                       src[TD:TD + body].rearrange("(a b) n -> a b n", a=16)).then_inc(copied, 16)
                        pool.dma_start(dst[body:WIN - TD], src[TD + body:WIN]).then_inc(copied, 16)
                pool.wait_ge(copied, 16 * 4 * ND)

            @block.scalar
            def _(act):
                def norm(it, b):
                    r = rows_of(it)
                    act.wait_ge(x_landed[b], (it - b) * 8 + 16)
                    if not isinstance(it, int) or it:
                        act.wait_ge(x_turned, it * 2)
                    nc.scalar.activation(xs[0:r], x[b][0:r], ACT.Square,
                                         accum_out=stat[0:r, 0:1]).then_inc(squared, 1)
                    act.wait_ge(var_ready, it + 1)
                    nc.scalar.activation(stat[0:r, 2:3], stat[0:r, 1:2], ACT.Sqrt).then_inc(root_ready, 1)

                def prologue():
                    act.sem_inc(z_free, ZB)
                    act.sem_inc(zT_ready, 2)
                    norm(0, 0)

                def step(it, b):
                    r = rows_of(it)
                    act.wait_ge(stored[b], (it - b) * 64 + 1)
                    for i in range(NG):
                        act.wait_ge(z_summed, it * NG + (i + 2))
                        nc.scalar.copy(z[b][0:r, i, :], z_ps[ring(b, i)][0:r, :]).then_inc(z_free, 1)
                        if i == 1 and r == P:
                            norm(it + 1, 1 - b)
                    for i in range(NR):
                        act.wait_ge(z_turned, it * NR + i + 1)
                        dst = zT[b][:, i, :, 0:r] if r == P else keep[GROUPS[i][0] + "sT"][
                            :, 0 if GROUPS[i][1] == "a" else NP:(0 if GROUPS[i][1] == "a" else NP) + NP, :]
                        src = z_turn[i % 2][:, :].rearrange("p (g n) -> p g n", g=NP)[:, :, 0:r]
                        nc.scalar.copy(dst, src).then_inc(zT_ready, 1)

                phase(prologue, step)(act)

            @block.vector
            def _(dve):
                def norm(it, b, link):
                    r = rows_of(it)
                    dve.wait_ge(squared, it + 1)
                    nc.vector.tensor_scalar(stat[0:r, 1:2], stat[0:r, 0:1], 1.0 / D, EPS,
                                            ALU.mult, ALU.add).then_inc(var_ready, 1)
                    dve.wait_ge(root_ready, it + 1)
                    link(nc.vector.reciprocal(stat[0:r, 3:4], stat[0:r, 2:3]))
                    nc.vector.tensor_scalar(xs[0:r], x[b][0:r], stat[0:r, 3:4], None,
                                            ALU.mult).then_inc(xs_ready, 1)

                def spread(it, b):
                    r = rows_of(it)
                    if not (isinstance(it, int) and it < 2):
                        dve.wait_ge(z_summed, (it - 1) * NG + 1)
                    for h in range(2):
                        dve.wait_ge(x_turned, it * 2 + h + 1)
                        dst = xT[b][:, 4 * h:4 * h + 4, 0:r]
                        src = x_turn[h][:, :].rearrange("p (c n) -> p c n", c=4)[:, :, 0:r]
                        g = gain[:, 4 * h:4 * h + 4].unsqueeze(2).broadcast_to([P, 4, r])
                        nc.vector.tensor_tensor(dst, src, g, ALU.mult).then_inc(xT_ready, 1)

                def prologue():
                    dve.wait_ge(const_in, 64)
                    norm(0, 0, linker(dve, vec, Count(0)))
                    spread(0, 0)

                def step(it, b):
                    r = rows_of(it)
                    link = linker(dve, vec, Count(it * VEC + 1))
                    for i in range(NR):
                        if i == 2 and r == P:
                            norm(it + 1, 1 - b, link)
                        dve.wait_ge(z_free, it * NG + (ZB + i + 1))
                        head = z[b][0:r, i, :].rearrange("p (u e) -> p u e", e=HD)[:, :, 0:ROT]
                        u = GW // HD
                        tab = lambda t: t[0:r, bass.ds(it, 1), :].broadcast_to([r, u, ROT])
                        nc.vector.tensor_tensor(rot[0:r, 0], head, tab(cos), ALU.mult)
                        swap = head.rearrange("p u (h e) -> p u h e", h=2)[:, :, ::-1, :]
                        link(nc.vector.tensor_tensor(
                            rot[0:r, 1].rearrange("p u (h e) -> p u h e", h=2), swap,
                            tab(sin).rearrange("p u (h e) -> p u h e", h=2), ALU.mult))
                        nc.vector.tensor_tensor(head, rot[0:r, 0], rot[0:r, 1], ALU.add).then_inc(rotated, 1)
                        dve.wait_ge(rotated, it * NR + (i + 1))
                    if r == P:
                        spread(it + 1, 1 - b)

                phase(prologue, step)(dve)

            @block.tensor
            def _(pe):
                def turn(it, b):
                    r = rows_of(it)
                    if isinstance(it, int) and it == 0:
                        pe.wait_ge(const_in, 64)
                    pe.wait_ge(xs_ready, it + 1)
                    for h in range(2):
                        if not (isinstance(it, int) and it == 0):
                            pe.wait_ge(xT_ready, it * 2 - 1 + h)
                        for c in range(4):
                            m = nc.tensor.transpose(x_turn[h][:, c * P:c * P + r],
                                                    xs[0:r, (4 * h + c) * P:(4 * h + c + 1) * P],
                                                    keep["ident"][0:r, 0:r])
                        m.then_inc(x_turned, 1)

                def prologue():
                    pe.sem_inc(z_summed, 1)
                    turn(0, 0)

                def step(it, b):
                    r = rows_of(it)
                    pe.wait_ge(xT_ready, it * 2 + 2)
                    for i, g in enumerate(order):
                        if not isinstance(it, int):
                            pe.wait_ge(w_landed[i], 16)
                        pe.wait_ge(z_free, it * NG + (i + 1))
                        for c in range(KC):
                            m = nc.tensor.matmul(z_ps[ring(b, i)][0:r, :], xT[b][:, c, 0:r],
                                                 w_in[:, c, COLS[g] * GW:(COLS[g] + 1) * GW],
                                                 start=(c == 0), stop=(c == KC - 1))
                        m.then_inc(z_summed, 1)
                        if i == NR and r == P:
                            turn(it + 1, 1 - b)
                    for i in range(NR):
                        pe.wait_ge(rotated, it * NR + (i + 1))
                        pe.wait_ge(zT_ready, it * NR + (i + 1))
                        for g in range(NP):
                            m = nc.tensor.transpose(z_turn[i % 2][:, g * P:g * P + r],
                                                    z[b][0:r, i, g * P:(g + 1) * P], keep["ident"][0:r, 0:r])
                        m.then_inc(z_turned, 1)

                phase(prologue, step)(pe)


def ring(b, i):
    return (6 * b + i) % 4


def attend_prompt(nc, io, keep):
    NQ = 4
    NU = NT // NQ
    PASSES = NP // 2
    SS, WS, OS = 4, 4, 2
    with ExitStack() as ctx:
        sb = lambda n, s, d=F32: ctx.enter_context(nc.sbuf_tensor(n, s, d))
        ps = lambda n: ctx.enter_context(nc.psum_tensor(n, [P, 512], F32))
        sem = lambda n: ctx.enter_context(nc.semaphore(n))
        q = [sb(f"b_q{i}", [P, 2, S]) for i in range(2)]
        k = [sb(f"b_k{i}", [P, S]) for i in range(2)]
        v = [sb(f"b_v{i}", [P, NT, P]) for i in range(2)]
        bias = [sb("b_bias_dilated", [P, S]), sb("b_bias_causal", [P, S])]
        w = [[sb(f"b_w{i}_{t}", [P, S]) for t in range(NQ)] for i in range(2)]
        w1 = [sb(f"b_second{t}", [P, S]) for t in range(2)]
        wT = [sb(f"b_wT{i}", [P, 512]) for i in range(WS)]
        o = [sb(f"b_o{i}", [P, 512]) for i in range(2)]
        part = sb("b_part", [P, 2, NU])
        top = sb("b_top", [P, 2])
        shift = sb("b_shift", [P, 2, 2 * NQ])
        total = sb("b_total", [P, 2, 2 * NQ])
        inv = sb("b_inv", [P, 2, 2 * NQ])
        lam_rows = sb("b_lam_rows", [P, 4 * HD])
        lam_prod = sb("b_lam_prod", [P, 2, HD])
        lam_sum = sb("b_lam_sum", [P, 2])
        lam_exp = sb("b_lam_exp", [P, 2])
        s_ps = [ps(f"b_s{i}") for i in range(SS)]
        turn = [ps(f"b_turn{i}") for i in range(2)]
        o_ps = [ps(f"b_ops{i}") for i in range(2)]

        const_in = sem("b_const_in")
        lam_summed = sem("b_lam_summed")
        lam_exped = sem("b_lam_exped")
        lam_ready = sem("b_lam_ready")
        zeroed = sem("b_zeroed")
        pair_in = [sem(f"b_pair_in{i}") for i in range(2)]
        s_full = sem("b_s_full")
        s_used = sem("b_s_used")
        shift_ready = sem("b_shift_ready")
        exp_done = sem("b_exp_done")
        inv_ready = sem("b_inv_ready")
        w_ready = sem("b_w_ready")
        turned = sem("b_turned")
        copied = [sem("b_copied_scalar"), sem("b_copied_vector")]
        wT_used = sem("b_wT_used")
        o_copied = sem("b_o_copied")
        o_out = [sem(f"b_o_out{i}") for i in range(2)]
        vec = sem("b_vec")
        vec_gate, pool_gate = sem("b_vec_gate"), sem("b_pool_gate")

        class Pass:
            def __init__(self, diff):
                self.diff = diff
                self.maps = (0, 1) if diff else (0,)
                self.units = [(i, m, g) for i in range(2) for m in ((0,) if diff else (0, 1)) for g in range(NU)]
                self.n = len(self.units)
                self.part0 = [sum(NQ * (g + 1) * len(self.maps) for _, _, g in self.units[:n]) for n in range(self.n + 1)]
                self.key0 = [sum(NQ * (g + 1) for _, _, g in self.units[:n]) for n in range(self.n + 1)]
                self.rows = NQ * len(self.maps)
                self.links = sum(self.rows * (g > 0) + 3 * NQ * diff for _, _, g in self.units)

        kinds = (Pass(False), Pass(True))
        COUNTS = ("units", "parts", "keys", "rows", "tiles", "vec")

        def size(kd):
            return dict(units=kd.n, parts=kd.part0[-1], keys=kd.key0[-1], rows=kd.n * kd.rows, tiles=kd.n * NQ, vec=kd.links)

        def passes(eng, body):
            done = dict.fromkeys(COUNTS, 0)
            for kd in kinds:
                n = size(kd)
                with eng.Fori(0, PASSES) as r:
                    body(kd, r, {c: r * n[c] + done[c] for c in COUNTS})
                for c in COUNTS:
                    done[c] += PASSES * n[c]

        with nc.Block() as block:
            @block.sync
            def _(sp):
                for dst, name in ((bias[0], "bias_dilated"), (bias[1], "bias_causal")):
                    sp.dma_start(dst[:], io[name]).then_inc(const_in, 16)
                sp.dma_start(lam_rows[:], io["lambdas"].broadcast_to([P, 4 * HD])).then_inc(const_in, 16)
                sp.wait_ge(zeroed, 2)
                ends = []
                for pair in range(2 * NP):
                    i, kd = pair % 2, kinds[pair // NP]
                    if pair >= 2:
                        sp.wait_ge(wT_used, WS + ends[pair - 2])
                    sp.dma_start(k[i][:], io["kT"][pair]).then_inc(pair_in[i], 16)
                    for m in range(2):
                        h = slice(m * HD, (m + 1) * HD)
                        sp.dma_start(q[i][h, m, :], io["qT"][pair, h]).then_inc(pair_in[i], 16)
                    vs = io["vb_p" if kd.diff else "va_p"].rearrange("(t p) (g n) -> g p t n", p=P, g=NP)
                    sp.dma_start(v[i][:], vs[pair % NP]).then_inc(pair_in[i], 16)
                    ends.append((ends[-1] if ends else 0) + kd.key0[-1] // 2)

            @block.gpsimd
            def _(pool):
                for i in range(2):
                    nc.gpsimd.memset(q[i][:], 0.0).then_inc(zeroed, 1)
                kd = kinds[0]
                with pool.Fori(0, PASSES) as r:
                    for n, (i, m, g) in enumerate(kd.units):
                        for t in range(NQ):
                            pool.wait_ge(inv_ready, r * (kd.n * NQ) + (n * NQ + t + 1))
                            pool.sem_inc(pool_gate, 1)
                            row = w[n % 2][t][:, 0:(NQ * g + t + 1) * P]
                            nc.gpsimd.tensor_scalar(row, row, inv[:, n % 2, 2 * t:2 * t + 1], None,
                                                    ALU.mult).then_inc(w_ready, 1)

            @block.tensor
            def _(pe):
                def body(kd, r, base):
                    def scores(n):
                        i, m, g = kd.units[n]
                        if n % (kd.n // 2) == 0:
                            pe.wait_ge(pair_in[i], r * 64 + (64 * (1 + PASSES * kd.diff)))
                        j = kd.part0[n]
                        for t in range(NQ):
                            for mm in kd.maps:
                                for b in range(g + 1):
                                    pe.wait_ge(s_used, base["parts"] + (j + 1))
                                    lo, hi = b * 512, min((b + 1) * 512, (NQ * g + t + 1) * P)
                                    nc.tensor.matmul(s_ps[j % SS][:, 0:hi - lo],
                                                     q[i][:, m + mm, (NQ * g + t) * P:(NQ * g + t + 1) * P],
                                                     k[i][:, lo:hi], start=True, stop=True).then_inc(s_full, 1)
                                    j += 1

                    def weigh(n):
                        i, m, g = kd.units[n]
                        nk = NQ * (g + 1)
                        pe.wait_ge(w_ready, base["tiles"] + NQ * (n + 1))

                        def turn_keys(kt):
                            e = kd.key0[n] + kt
                            pe.wait_ge(copied[e % 2], base["keys/2"] + (e // 2 + 1))
                            for t in range(max(0, kt - NQ * g), NQ):
                                last = nc.tensor.transpose(turn[e % 2][:, t * P:(t + 1) * P],
                                                           w[n % 2][t][:, kt * P:(kt + 1) * P], keep["ident"][:])
                            last.then_inc(turned, 1)

                        turn_keys(0)
                        turn_keys(1)
                        pe.wait_ge(o_copied, base["units"] + (n + 1))
                        rows, lo = (P, 0) if kd.diff else (HD, m * HD)
                        for kt in range(nk):
                            e = kd.key0[n] + kt
                            c0 = max(0, kt - NQ * g) * P
                            pe.wait_ge(copied[e % 2], base["keys/2"] + (e // 2 + 2))
                            nc.tensor.matmul(o_ps[n % 2][0:rows, c0:512], v[i][:, kt, lo:lo + rows],
                                             wT[e % WS][:, c0:512], start=(kt == 0),
                                             stop=(kt == nk - 1)).then_inc(wT_used, 1)
                            if kt + 2 < nk:
                                turn_keys(kt + 2)

                    base["keys/2"] = r * (kd.key0[-1] // 2) + (PASSES * kinds[0].key0[-1] // 2 * kd.diff)
                    scores(0)
                    for n in range(kd.n):
                        if n + 1 < kd.n:
                            scores(n + 1)
                        weigh(n)

                pe.sem_inc(turned, 1)
                pe.sem_inc(wT_used, WS)
                passes(pe, body)

            def copy_turned(eng, copy, kd, base, n, which):
                i, m, g = kd.units[n]
                for kt in range(NQ * (g + 1)):
                    e = kd.key0[n] + kt
                    if e % 2 != which:
                        continue
                    c0 = max(0, kt - NQ * g) * P
                    eng.wait_ge(turned, base["keys"] + (e + 2))
                    eng.wait_ge(wT_used, base["keys"] + (e + 1))
                    copy(wT[e % WS][:, c0:512], turn[e % 2][:, c0:512]).then_inc(copied[which], 1)

            @block.scalar
            def _(act):
                act.sem_inc(copied[0], 1)
                act.sem_inc(o_copied, OS)
                for i in range(2):
                    act.sem_inc(o_out[i], 1)
                act.wait_ge(lam_summed, 1)
                nc.scalar.activation(lam_exp[:], lam_sum[:], ACT.Exp).then_inc(lam_exped, 1)

                def body(kd, r, base):
                    def exps(n):
                        i, m, g = kd.units[n]
                        for t in range(NQ):
                            for mm in kd.maps:
                                act.wait_ge(shift_ready, base["rows"] + (n * kd.rows + t * len(kd.maps) + mm + 1))
                                row = (w1[t % 2] if mm else w[n % 2][t])[:, 0:(NQ * g + t + 1) * P]
                                c = 2 * t + mm
                                nc.scalar.activation(row, row, ACT.Exp, bias=shift[:, n % 2, c:c + 1], scale=SCALE,
                                                     accum_out=total[:, n % 2, c:c + 1]).then_inc(exp_done, 1)

                    def put(n):
                        i, m, g = kd.units[n]
                        rows, lo = (P, 0) if kd.diff else (HD, m * HD)
                        act.wait_ge(wT_used, base["keys"] + (WS + kd.key0[n + 1]))
                        act.wait_ge(o_out[n % 2], base["units"] * 8 + (1 + n // 2 * 16))
                        nc.scalar.copy(o[n % 2][0:rows], o_ps[n % 2][0:rows]).then_inc(o_copied, 1)
                        pair = r * 2 + (NP * kd.diff + i)
                        act.wait_ge(o_copied, base["units"] + (OS + n + 1))
                        dst = io["mixT"][bass.ds(pair, 1), lo:lo + rows, g * 512:(g + 1) * 512]
                        act.dma_start(dst.rearrange("o p n -> (o p) n"), o[n % 2][0:rows]).then_inc(o_out[n % 2], 16)

                    exps(0)
                    for n in range(kd.n):
                        if n + 1 < kd.n:
                            exps(n + 1)
                        copy_turned(act, nc.scalar.copy, kd, base, n, 0)
                        put(n)

                passes(act, body)
                for i in range(2):
                    act.wait_ge(o_out[i], 1 + 8 * PASSES * (kinds[0].n + kinds[1].n))

            @block.vector
            def _(dve):
                link = linker(dve, vec, Count(0))
                dve.wait_ge(const_in, 48)
                link(nc.vector.tensor_tensor(lam_prod[:].rearrange("p a n -> p (a n)"), lam_rows[:, 0:2 * HD],
                                             lam_rows[:, 2 * HD:4 * HD], ALU.mult))
                nc.vector.tensor_reduce(lam_sum[:], lam_prod[:], AX.X, ALU.add).then_inc(lam_summed, 1)
                dve.wait_ge(lam_exped, 1)
                link(nc.vector.tensor_scalar(keep["neg_lam"][:], lam_exp[:, 1:2], -LAMBDA_INIT, None, ALU.add))
                link(nc.vector.tensor_tensor(keep["neg_lam"][:], keep["neg_lam"][:], lam_exp[:, 0:1], ALU.subtract))

                def body(kd, r, base):
                    link = linker(dve, vec, Count(base["vec"] + 3))

                    def biased(n, t, mm, j):
                        i, m, g = kd.units[n]
                        tile = NQ * g + t
                        row = w1[t % 2] if mm else w[n % 2][t]
                        rb = n * kd.rows + t * len(kd.maps) + mm
                        for b in range(g + 1):
                            lo, hi = b * 512, min((b + 1) * 512, (tile + 1) * P)
                            at = (NT - 1 - tile) * P + lo
                            dve.wait_ge(s_full, base["parts"] + (j + 1))
                            dve.sem_inc(vec_gate, 1)
                            nc.vector.tensor_tensor_reduce(
                                out=row[:, lo:hi], in0=s_ps[j % SS][:, 0:hi - lo],
                                in1=bias[kd.diff][:, at:at + hi - lo], scale=1.0, scalar=-BIG, op0=ALU.add,
                                op1=ALU.max, accum_out=(part[:, rb % 2, b:b + 1])).then_inc(s_used, 1)
                            j += 1
                        dve.wait_ge(s_used, base["parts"] + (SS + j))
                        src = part[:, rb % 2, 0:1]
                        if g:
                            link(nc.vector.tensor_reduce(top[:, rb % 2:rb % 2 + 1], part[:, rb % 2, 0:g + 1],
                                                         AX.X, ALU.max))
                            src = top[:, rb % 2:rb % 2 + 1]
                        c = 2 * t + mm
                        nc.vector.tensor_scalar(shift[:, n % 2, c:c + 1], src, -SCALE, None,
                                                ALU.mult).then_inc(shift_ready, 1)
                        return j

                    def normed(n, t):
                        i, m, g = kd.units[n]
                        c = 2 * t
                        dve.wait_ge(exp_done, base["rows"] + (n * kd.rows + (t + 1) * len(kd.maps)))
                        rec = nc.vector.reciprocal(inv[:, n % 2, c:c + len(kd.maps)],
                                                   total[:, n % 2, c:c + len(kd.maps)])
                        if not kd.diff:
                            rec.then_inc(inv_ready, 1)
                            return
                        link(rec)
                        cols = (NQ * g + t + 1) * P
                        link(nc.vector.tensor_scalar(inv[:, n % 2, c + 1:c + 2], inv[:, n % 2, c + 1:c + 2],
                                                     keep["neg_lam"][:, 0:1], None, ALU.mult))
                        row = w[n % 2][t][:, 0:cols]
                        link(nc.vector.tensor_scalar(row, row, inv[:, n % 2, c:c + 1], None, ALU.mult))
                        nc.vector.scalar_tensor_tensor(out=row, in0=w1[t % 2][:, 0:cols],
                                                       scalar=inv[:, n % 2, c + 1:c + 2], in1=row,
                                                       op0=ALU.mult, op1=ALU.add).then_inc(w_ready, 1)

                    def score_rows(n):
                        dve.wait_ge(turned, base["keys"] + (1 + (kd.key0[n - 1] if n >= 2 else 0)))
                        j = kd.part0[n]
                        for t in range(NQ):
                            for mm in kd.maps:
                                j = biased(n, t, mm, j)
                            if t >= 1:
                                normed(n, t - 1)

                    score_rows(0)
                    normed(0, NQ - 1)
                    for n in range(kd.n):
                        if n + 1 < kd.n:
                            score_rows(n + 1)
                        copy_turned(dve, nc.vector.tensor_copy, kd, base, n, 1)
                        if n + 1 < kd.n:
                            normed(n + 1, NQ - 1)

                dve.sem_inc(copied[1], 1)
                dve.sem_inc(s_used, SS)
                passes(dve, body)


CH = 8
SL = 4
ROWS = 32
NC = PAGES // CH + 1


def attend_decode(nc, io, keep):
    RG = 3
    with ExitStack() as ctx:
        sb = lambda n, s, d=F32: ctx.enter_context(nc.sbuf_tensor(n, s, d))
        ps = lambda n: ctx.enter_context(nc.psum_tensor(n, [P, 512], F32))
        sem = lambda n: ctx.enter_context(nc.semaphore(n))
        table = sb("c_table", [1, ND * PAGES], I32)
        k = [sb(f"c_k{i}", [P, CH, GW]) for i in range(RG)]
        v = [sb(f"c_v{i}", [P, CH, GW]) for i in range(RG)]
        kT = [sb(f"c_kT{i}", [P, NP, CH * P]) for i in range(RG)]
        q_rows = sb("c_q_rows", [P, 2, NP, SL * ROWS])
        v_new = sb("c_v_new", [TD, 2, ND, GW])
        bias_new = sb("c_bias_new", [P, 2, TD])
        bias_win = sb("c_bias_win", [P, 2 * P])
        own_head = sb("c_own_head", [P, 2, GW])
        same_row = sb("c_same_row", [P, P])
        token = sb("c_token", [P, TD])
        map_of = sb("c_map_of", [P, 2])
        sign = sb("c_sign", [P, 2])
        s_new = sb("c_s_new", [P, 2, TD])
        p_new = sb("c_p_new", [P, 2, TD])
        pT_new = sb("c_pT_new", [TD, 2, P])
        s_win = sb("c_s_win", [P, 2 * P])
        m = sb("c_m", [P, 2, 2])
        chunk_max = sb("c_chunk_max", [P, 1])
        shift = sb("c_shift", [P, RG])
        shift_new = sb("c_shift_new", [P, 2])
        alpha = sb("c_alpha", [P, RG])
        l_new = sb("c_l_new", [P, 2])
        l_chunk = sb("c_l_chunk", [P, RG])
        l = sb("c_l", [P, 2])
        prob = [sb(f"c_prob{i}", [P, 2 * P]) for i in range(RG)]
        pT = [sb(f"c_pT{i}", [P, 2 * P]) for i in range(RG)]
        acc = sb("c_acc", [P, 2, GW])
        m_row = sb("c_m_row", [2, ROWS])
        m_rows = sb("c_m_rows", [2, SL, ROWS])
        below = sb("c_below", [P, 2])
        weight = sb("c_weight", [P, 2])
        lw = sb("c_lw", [P, 2])
        coef = sb("c_coef", [P, 2])
        comb = sb("c_comb", [P, 2, TD])
        turn = [ps(f"c_turn{i}") for i in range(2)]
        s_ps = [ps(f"c_s{i}") for i in range(RG)]
        pT_ps, o_ps, x_ps = ps("c_pT_ps"), ps("c_o_ps"), ps("c_x_ps")

        const_in, table_in = sem("c_const_in"), sem("c_table_in")
        q_zero, q_ready = sem("c_q_zero"), sem("c_q_ready")
        k_in = [sem(f"c_k_in{i}") for i in range(RG)]
        v_in = [sem(f"c_v_in{i}") for i in range(RG)]
        turned = sem("c_turned")
        copied = [sem("c_copied_scalar"), sem("c_copied_vector")]
        s_full, shift_ready, exp_done = sem("c_s_full"), sem("c_shift_ready"), sem("c_exp_done")
        p_turned, pT_ready = sem("c_p_turned"), sem("c_pT_ready")
        o_full, o_added, l_added = sem("c_o_full"), sem("c_o_added"), sem("c_l_added")
        new_scored, new_shifted, new_exped = sem("c_new_scored"), sem("c_new_shifted"), sem("c_new_exped")
        new_turned, new_pT, new_full, new_taken = (sem("c_new_turned"), sem("c_new_pT"), sem("c_new_full"),
                                                   sem("c_new_taken"))
        m_turned, m_spread_ready, m_spread = sem("c_m_turned"), sem("c_m_spread_ready"), sem("c_m_spread")
        below_ready, weight_ready = sem("c_below_ready"), sem("c_weight_ready")
        lw_ready, l_summed, comb_ready = sem("c_lw_ready"), sem("c_l_summed"), sem("c_comb_ready")
        mixed, mix_kept = sem("c_mixed"), sem("c_mix_kept")
        vec = sem("c_vec")
        vec_gate, sp_gate, pool_gate = sem("c_vec_gate"), sem("c_sp_gate"), sem("c_pool_gate")

        kind = lambda c: 1 if c < NC - 1 else 0
        EV = NP * CH // 4
        LINKS = 3 + 2 * NC + 4
        FIRST_LINKS = 3
        X_M, X_L, X_O = P, P + 4, P + 8
        X_S = X_O + 2 * NP * TD
        X_P = X_S + 2 * TD

        def samples(eng, chunks, between):
            between(None, 0)
            with eng.Fori(0, ND - 1) as n:
                chunks(n)
                between(n, n + 1)
            chunks(ND - 1)
            between(ND - 1, None)

        with nc.Block() as block:
            def load(eng, n, c, dst, src, landed):
                i = c % RG
                if kind(c):
                    for g in range(CH):
                        page = eng.value_load(table[0:1, bass.ds(n * PAGES + (c * CH + g), 1)],
                                             min_val=0, max_val=NPHYS - 1)
                        eng.dma_start(dst[i][:, g, :], io[src[0]][bass.ds(page, 1)].rearrange(
                            "o p d -> (o p) d")).then_inc(landed[i], 16)
                    return
                rows = io[src[1]][bass.ds(n, 1)].rearrange("o t d -> (o t) d")
                for g in range(3):
                    by = rows[g * 512:(g + 1) * 512].rearrange("(a r) d -> a r d", r=16)[:, 0:TD, :]
                    eng.dma_start(dst[i][:, g, :], by).then_inc(landed[i], 16)
                near = rows[1536:2048].rearrange("(g p) d -> p g d", p=P)
                eng.dma_start(dst[i][:, 3:7, :], near).then_inc(landed[i], 16)
                eng.dma_start(dst[i][:, 7, :], rows[1920:2048]).then_inc(landed[i], 16)

            @block.sync
            def _(sp):
                sp.dma_start(table[:], io["page_table"]).then_inc(table_in, 16)
                consts = (("bias_new", bias_new), ("bias_win", bias_win), ("own_head", own_head),
                          ("same_row", same_row), ("token", token), ("map_of", map_of))
                for name, dst in consts:
                    sp.dma_start(dst[:], io[name]).then_inc(const_in, 16)
                sp.dma_start(v_new[:, 0], io["va_win"][:, WIN - TD:WIN, :].rearrange("n t d -> t n d")).then_inc(const_in, 16)
                sp.dma_start(v_new[:, 1], io["vb_s"].rearrange("(n t) d -> t n d", t=TD)).then_inc(const_in, 16)
                sp.wait_ge(table_in, 16)

                with sp.Fori(0, ND) as n:
                    for c in range(NC):
                        sp.wait_ge(turned, n * (NC * EV) + (c + 1) * EV)
                        sp.sem_inc(sp_gate, 1)
                        load(sp, n, c, k, ("k_cache", "ka_state"), k_in)

            @block.gpsimd
            def _(pool):
                pool.wait_ge(table_in, 16)
                with pool.Fori(0, ND) as n:
                    for c in range(NC):
                        pool.wait_ge(o_full, n * NC + (c + 1))
                        pool.sem_inc(pool_gate, 1)
                        load(pool, n, c, v, ("v_cache", "va_state"), v_in)

            def landed(c, n):
                count = lambda cc: 16 * (CH if kind(cc) else 5)
                mine = [cc for cc in range(NC) if cc % RG == c % RG]
                return n * sum(map(count, mine)) + sum(count(cc) for cc in mine if cc <= c)

            @block.tensor
            def _(pe):
                pe.sem_inc(turned, RG * EV)
                pe.sem_inc(o_full, RG)
                pe.sem_inc(s_full, RG)
                pe.wait_ge(const_in, 16 * 8)

                def turn_keys(n, c, part=range(EV)):
                    i = c % RG
                    if part[0] == 0:
                        pe.wait_ge(k_in[i], landed(c, n))
                    for e in part:
                        p, half = e // 2, e % 2
                        pe.wait_ge(copied[e % 2], n * (NC * EV // 2) + ((c * EV + e) // 2 + 1))
                        for g in range(4):
                            last = nc.tensor.transpose(turn[e % 2][:, g * P:(g + 1) * P],
                                                       k[i][:, half * 4 + g, p * P:(p + 1) * P], keep["ident"][:])
                        last.then_inc(turned, 1)

                def scores(n, c):
                    i = c % RG
                    for e in range(2):
                        pe.wait_ge(copied[e], n * (NC * EV // 2) + ((c + 1) * EV // 2 + 1))
                    pe.wait_ge(exp_done, n * NC + (c + 1))
                    for p in range(NP):
                        for j in range(SL):
                            last = nc.tensor.matmul(
                                s_ps[i][ROWS * j:ROWS * (j + 1), 0:2 * P],
                                q_rows[:, kind(c), p, ROWS * j:ROWS * (j + 1)],
                                kT[i][:, p, j * 2 * P:(j + 1) * 2 * P], start=(p == 0), stop=(p == NP - 1))
                    last.then_inc(s_full, 1)

                def weigh(n, c):
                    i = c % RG
                    pe.wait_ge(exp_done, n * NC + (RG + c + 1))
                    pe.wait_ge(pT_ready, n * NC + (c + 1))
                    for a in range(2):
                        last = nc.tensor.transpose(pT_ps[:, a * P:(a + 1) * P],
                                                   prob[i][:, a * P:(a + 1) * P], keep["ident"][:])
                    last.then_inc(p_turned, 1)
                    pe.wait_ge(v_in[i], landed(c, n))
                    pe.wait_ge(pT_ready, n * NC + (c + 2))
                    if c:
                        pe.wait_ge(o_added, n * NC + c)
                    else:
                        pe.wait_ge(new_taken, n * 2 + 3)
                    for a in range(2):
                        for j in range(SL):
                            last = nc.tensor.matmul(
                                o_ps[ROWS * j:ROWS * (j + 1), :],
                                pT[i][:, a * P + ROWS * j:a * P + ROWS * (j + 1)],
                                v[i][:, 2 * j + a, :], start=(a == 0), stop=(a == 1))
                    last.then_inc(o_full, 1)

                def new_scores(n):
                    pe.wait_ge(q_ready, n * 2 + 2)
                    for kd in range(2):
                        for p in range(NP):
                            rhs = keep["ksT"][:, kd * NP + p, bass.ds(n * TD, TD)]
                            last = nc.tensor.matmul(x_ps[:, X_S + kd * TD:X_S + (kd + 1) * TD], q_rows[:, kd, p, :],
                                                    rhs, start=(p == 0), stop=(p == NP - 1))
                    last.then_inc(new_scored, 1)

                def new_values(n):
                    pe.wait_ge(new_exped, n * 2 + 2)
                    pe.wait_ge(mix_kept, n + 1)
                    for kd in range(2):
                        last = nc.tensor.transpose(x_ps[0:TD, X_P + kd * P:X_P + (kd + 1) * P], p_new[:, kd, :],
                                                   keep["ident"][:])
                    last.then_inc(new_turned, 1)
                    pe.wait_ge(new_pT, n + 1)
                    for kd in range(2):
                        pe.wait_ge(new_taken, n * 2 + (kd + 1))
                        nc.tensor.matmul(o_ps[:, :], pT_new[:, kd, :],
                                         v_new[:, kd, bass.ds(n, 1), :].rearrange("t o d -> t (o d)"),
                                         start=True, stop=True).then_inc(new_full, 1)

                def between(n, new):
                    if n is not None:
                        nc.tensor.transpose(x_ps[0:2, 0:P], m[:, 0, :], keep["ident"][:]).then_inc(m_turned, 1)
                    if new is not None:
                        turn_keys(new, 0, range(EV // 2))
                    if n is not None:
                        pe.wait_ge(m_spread_ready, n + 1)
                        nc.tensor.matmul(x_ps[:, X_M:X_M + 2], m_rows[:, :, :].rearrange("k j r -> k (j r)"),
                                         keep["ident"][0:2, 0:2], start=True, stop=True).then_inc(m_spread, 1)
                    if new is not None:
                        turn_keys(new, 0, range(EV // 2, EV))
                        if n is not None:
                            pe.wait_ge(below_ready, n + 1)
                        new_scores(new)
                    if n is not None:
                        pe.wait_ge(lw_ready, n + 1)
                        if new is not None:
                            pe.wait_ge(new_shifted, new + 1)
                        nc.tensor.matmul(x_ps[:, X_L:X_L + 2], same_row[:], lw[:], start=True,
                                         stop=True).then_inc(l_summed, 1)
                    if new is not None:
                        turn_keys(new, 1)
                    if n is not None:
                        pe.wait_ge(comb_ready, n + 1)
                        for kd in range(2):
                            for p in range(NP):
                                at = X_O + (kd * NP + p) * TD
                                last = nc.tensor.matmul(x_ps[:, at:at + TD], acc[:, kd, p * P:(p + 1) * P],
                                                        comb[:, kd, :], start=True, stop=True)
                        last.then_inc(mixed, 1)
                    if new is not None:
                        new_values(new)

                def chunks(n):
                    for c in range(NC):
                        if 1 <= c < NC - 1:
                            turn_keys(n, c + 1)
                        scores(n, c)
                        if c:
                            weigh(n, c - 1)
                    weigh(n, NC - 1)

                samples(pe, chunks, between)

            @block.scalar
            def _(act):
                act.sem_inc(copied[0], 1)
                act.sem_inc(exp_done, RG)
                act.sem_inc(pT_ready, 1)

                def copy_keys(n, c, part=range(0, EV, 2)):
                    i = c % RG
                    for e in part:
                        act.wait_ge(turned, n * (NC * EV) + ((RG + c) * EV + e + 1))
                        act.wait_ge(s_full, n * NC + (c + 1))
                        nc.scalar.copy(kT[i][:, e // 2, 0:512], turn[0][:]).then_inc(copied[0], 1)

                def exps(n, c):
                    i = c % RG
                    act.wait_ge(shift_ready, n * NC + (c + 1))
                    old = m[:, c % 2 if kind(c) else 1, kind(c):kind(c) + 1]
                    nc.scalar.activation(alpha[:, i:i + 1], old, ACT.Exp, bias=shift[:, i:i + 1], scale=SCALE)
                    src = s_ps[i][:, 0:2 * P] if kind(c) else s_win[:]
                    nc.scalar.activation(prob[i][:], src, ACT.Exp, bias=shift[:, i:i + 1], scale=SCALE,
                                         accum_out=l_chunk[:, i:i + 1]).then_inc(exp_done, 1)

                def copy_pT(n, c):
                    act.wait_ge(p_turned, n * NC + (c + 1))
                    nc.scalar.copy(pT[c % RG][:], pT_ps[:, 0:2 * P]).then_inc(pT_ready, 1)

                def between(n, new):
                    if new is not None:
                        copy_keys(new, 0, range(0, EV // 2, 2))
                    if n is not None:
                        act.wait_ge(below_ready, n + 1)
                        nc.scalar.activation(weight[:], below[:], ACT.Exp, scale=SCALE).then_inc(weight_ready, 1)
                    if new is not None:
                        copy_keys(new, 0, range(EV // 2, EV, 2))
                    if new is not None:
                        act.wait_ge(new_shifted, new + 1)
                        for kd in range(2):
                            nc.scalar.activation(p_new[:, kd, :], s_new[:, kd, :], ACT.Exp,
                                                 bias=shift_new[:, kd:kd + 1], scale=SCALE,
                                                 accum_out=l_new[:, kd:kd + 1]).then_inc(new_exped, 1)
                        copy_keys(new, 1)

                def chunks(n):
                    for c in range(NC):
                        if 1 <= c < NC - 1:
                            copy_keys(n, c + 1)
                        if c:
                            copy_pT(n, c - 1)
                        exps(n, c)
                    copy_pT(n, NC - 1)

                samples(act, chunks, between)

            @block.vector
            def _(dve):
                dve.wait_ge(const_in, 16 * 8)
                nc.vector.memset(q_rows[:].rearrange("p a b c -> p (a b c)"), 0.0).then_inc(q_zero, 1)
                nc.vector.tensor_scalar(sign[:], map_of[:], keep["neg_lam"][:, 0:1], None, ALU.mult).then_inc(q_zero, 1)
                dve.wait_ge(q_zero, 2)
                nc.vector.tensor_tensor(sign[:, 0:1], sign[:, 0:1], map_of[:, 1:2], ALU.add).then_inc(q_zero, 1)
                dve.wait_ge(q_zero, 3)
                dve.sem_inc(copied[1], 1)
                dve.sem_inc(new_taken, 1)
                dve.sem_inc(l_added, 1)
                dve.sem_inc(mix_kept, 1)

                def copy_keys(n, c, part=range(1, EV, 2)):
                    i = c % RG
                    for e in part:
                        dve.wait_ge(turned, n * (NC * EV) + ((RG + c) * EV + e + 1))
                        dve.wait_ge(s_full, n * NC + (c + 1))
                        nc.vector.tensor_copy(kT[i][:, e // 2, 512:1024], turn[1][:]).then_inc(copied[1], 1)

                def maxima(n, c, link):
                    i, kd = c % RG, kind(c)
                    dve.wait_ge(s_full, n * NC + (RG + c + 1))
                    if kd:
                        link(nc.vector.tensor_reduce(chunk_max[:], s_ps[i][:, 0:2 * P], AX.X, ALU.max))
                    else:
                        dve.sem_inc(vec_gate, 1)
                        link(nc.vector.tensor_tensor_reduce(
                            out=s_win[:], in0=s_ps[i][:, 0:2 * P], in1=bias_win[:], scale=1.0, scalar=-BIG,
                            op0=ALU.add, op1=ALU.max, accum_out=chunk_max[:]))
                    old, new = (c % 2, (c + 1) % 2) if kd else (1, 0)
                    link(nc.vector.tensor_tensor(m[:, new, kd:kd + 1], m[:, old, kd:kd + 1], chunk_max[:], ALU.max))
                    nc.vector.tensor_scalar(shift[:, i:i + 1], m[:, new, kd:kd + 1], -SCALE, None,
                                            ALU.mult).then_inc(shift_ready, 1)

                def add(n, c):
                    i, kd = c % RG, kind(c)
                    dve.wait_ge(exp_done, n * NC + (RG + c + 1))
                    dve.wait_ge(l_added, n * NC + (c + 1))
                    nc.vector.scalar_tensor_tensor(out=l[:, kd:kd + 1], in0=l[:, kd:kd + 1],
                                                   scalar=alpha[:, i:i + 1], in1=l_chunk[:, i:i + 1],
                                                   op0=ALU.mult, op1=ALU.add).then_inc(l_added, 1)
                    dve.wait_ge(o_full, n * NC + (RG + c + 1))
                    nc.vector.scalar_tensor_tensor(out=acc[:, kd, :], in0=acc[:, kd, :],
                                                   scalar=alpha[:, i:i + 1], in1=o_ps[:, :],
                                                   op0=ALU.mult, op1=ALU.add).then_inc(o_added, 1)

                def queries(n):
                    dve.wait_ge(s_full, n * NC + RG)
                    for c in range(2):
                        h = slice(c * HD, (c + 1) * HD)
                        for kd in range(2):
                            for g in range(NP):
                                src = keep["qsT"][h, kd * NP + g, bass.ds(n * TD, TD)]
                                at = g * 2 * TD + c * TD
                                dst = q_rows[h, kd, g, :].rearrange("p (j r) -> p j r", j=SL)[:, :, at:at + TD]
                                last = nc.vector.tensor_copy(dst, src.unsqueeze(1).broadcast_to([HD, SL, TD]))
                        last.then_inc(q_ready, 1)

                def between(n, new, link):
                    if n is not None:
                        add(n, NC - 1)
                        dve.wait_ge(m_turned, n + 1)
                        link(nc.vector.tensor_reduce(m_row[:], x_ps[0:2, 0:P].rearrange("k (j r) -> k r j", j=SL),
                                                     AX.X, ALU.max))
                        nc.vector.tensor_copy(m_rows[:], m_row[:].unsqueeze(1).broadcast_to([2, SL, ROWS])).then_inc(
                            m_spread_ready, 1)
                    if new is not None:
                        copy_keys(new, 0, range(1, EV // 2, 2))
                    if n is not None:
                        dve.wait_ge(m_spread, n + 1)
                        nc.vector.tensor_tensor(below[:], m[:, 0, :], x_ps[:, X_M:X_M + 2],
                                                ALU.subtract).then_inc(below_ready, 1)
                    if new is not None:
                        copy_keys(new, 0, range(EV // 2 + 1, EV, 2))
                    if n is not None:
                        dve.wait_ge(o_added, n * NC + NC)
                        nc.vector.tensor_tensor(acc[:], acc[:], own_head[:], ALU.mult)
                        dve.wait_ge(weight_ready, n + 1)
                        dve.wait_ge(l_added, n * NC + (NC + 1))
                        nc.vector.tensor_tensor(lw[:], l[:], weight[:], ALU.mult).then_inc(lw_ready, 1)
                    if new is not None:
                        dve.wait_ge(new_scored, new + 1)
                        link(nc.vector.tensor_tensor(s_new[:], x_ps[:, X_S:X_S + 2 * TD].rearrange(
                            "p (a b) -> p a b", a=2), bias_new[:], ALU.add))
                        if n is not None:
                            dve.wait_ge(below_ready, n + 1)
                        nc.vector.tensor_reduce(m[:, 1, 0:1], s_new[:, 0, :], AX.X, ALU.max)
                        link(nc.vector.tensor_reduce(m[:, 0, 1:2], s_new[:, 1, :], AX.X, ALU.max))
                        nc.vector.tensor_scalar(shift_new[:, 0:1], m[:, 1, 0:1], -SCALE, None, ALU.mult)
                        nc.vector.tensor_scalar(shift_new[:, 1:2], m[:, 0, 1:2], -SCALE, None,
                                                ALU.mult).then_inc(new_shifted, 1)
                    if n is not None:
                        dve.wait_ge(l_summed, n + 1)
                        link(nc.vector.reciprocal(coef[:], x_ps[:, X_L:X_L + 2]))
                        link(nc.vector.tensor_tensor(coef[:], coef[:], weight[:], ALU.mult))
                        link(nc.vector.tensor_tensor(coef[:, 1:2], coef[:, 1:2], sign[:, 0:1], ALU.mult))
                        for kd in range(2):
                            ins = nc.vector.tensor_scalar(comb[:, kd, :], token[:], coef[:, kd:kd + 1], None, ALU.mult)
                        ins.then_inc(comb_ready, 1)
                    if new is not None:
                        copy_keys(new, 1)
                    if n is not None:
                        dve.wait_ge(mixed, n + 1)
                        nc.vector.tensor_copy(keep["mixsT"][:, :, bass.ds(n * TD, TD)],
                                              x_ps[:, X_O:X_O + 2 * NP * TD].rearrange("p (g t) -> p g t", t=TD)
                                              ).then_inc(mix_kept, 1)
                    if new is not None:
                        dve.wait_ge(new_exped, new * 2 + 2)
                        link(nc.vector.tensor_scalar(l[:], l_new[:], 1.0 / SL, None, ALU.mult))
                        dve.wait_ge(new_turned, new + 1)
                        nc.vector.tensor_scalar(pT_new[:], x_ps[0:TD, X_P:X_P + 2 * P].rearrange(
                            "t (a b) -> t a b", a=2), 1.0 / SL, None, ALU.mult).then_inc(new_pT, 1)
                        for kd in range(2):
                            dve.wait_ge(new_full, new * 2 + kd + 1)
                            nc.vector.tensor_copy(acc[:, kd, :], o_ps[:, :]).then_inc(new_taken, 1)
                        dve.wait_ge(new_taken, new * 2 + 3)

                def chunks(n, new, link):
                    for c in range(NC):
                        if 1 <= c < NC - 1:
                            copy_keys(n, c + 1)
                        maxima(n, c, link)
                        if c:
                            add(n, c - 1)
                    if new is not None:
                        queries(new)

                queries(0)
                between(None, 0, linker(dve, vec, Count(0)))
                with dve.Fori(0, ND - 1) as n:
                    count = Count(n * LINKS + FIRST_LINKS)
                    link = linker(dve, vec, count)
                    chunks(n, n + 1, link)
                    between(n, n + 1, link)
                    assert count.n == LINKS, count.n
                link = linker(dve, vec, Count((ND - 1) * LINKS + FIRST_LINKS))
                chunks(ND - 1, None, link)
                between(ND - 1, None, link)


def mlp(nc, io, keep):
    TB = 4
    NB = NT // TB
    DB = 4
    DP = 2 * TB
    NF = 4
    NH = NP
    with ExitStack() as ctx:
        sb = lambda n, s, d=F32: ctx.enter_context(nc.sbuf_tensor(n, s, d))
        ps = lambda n: ctx.enter_context(nc.psum_tensor(n, [P, 512], F32))
        sem = lambda n: ctx.enter_context(nc.semaphore(n))
        w_out = sb("d_w_out", [P, KC, D])
        w_up = [sb(f"d_w_up{i}", [P, KC, 512]) for i in range(2)]
        w_down = [sb(f"d_w_down{i}", [P, NF, D]) for i in range(2)]
        mix = sb("d_mix", [P, KC, 512])
        y = [sb(f"d_y{i}", [P, TB, D]) for i in range(2)]
        hs = [sb(f"d_hs{i}", [P, D]) for i in range(2)]
        hT = sb("d_hT", [P, KC, 512])
        uT = [sb(f"d_uT{i}", [P, NF, 512]) for i in range(2)]
        square = sb("d_square", [P, 512])
        root = sb("d_root", [P, 512])
        gain_mlp = sb("d_gain_mlp", [P, KC])
        gain_head = sb("d_gain_head", [P, 1])
        gain_last = sb("d_gain_last", [P, D])
        ones = sb("d_ones", [P, P])
        fold = sb("d_fold", [P, P])
        stat = sb("d_stat", [P, 4])
        d_ps = [ps(f"d_dps{i}") for i in range(DB)]
        u_ps = [ps(f"d_ups{i}") for i in range(2)]
        t_ps = [ps(f"d_tps{i}") for i in range(2)]

        const_in, out_in = sem("d_const_in"), sem("d_out_in")
        up_in = [sem(f"d_up_in{i}") for i in range(2)]
        down_in = [sem(f"d_down_in{i}") for i in range(2)]
        mix_in, y_in = sem("d_mix_in"), sem("d_y_in")
        ones_ready, gain_ready = sem("d_ones_ready"), sem("d_gain_ready")
        squared, summed = sem("d_squared"), sem("d_summed")
        var_ready, rooted = sem("d_var_ready"), sem("d_rooted")
        mix_ready = sem("d_mix_ready")
        d_full, d_used = sem("d_d_full"), sem("d_d_used")
        u_full, u_relued, u_used = sem("d_u_full"), sem("d_u_relued"), sem("d_u_used")
        row_squared, row_var, row_rooted = sem("d_row_squared"), sem("d_row_var"), sem("d_row_rooted")
        hs_ready, h_turned, hT_ready = sem("d_hs_ready"), sem("d_h_turned"), sem("d_hT_ready")
        y_ready = sem("d_y_ready")
        stored = [sem(f"d_stored{i}") for i in range(2)]
        vec = sem("d_vec")
        sp_gate = sem("d_sp_gate")
        u4_ready, f_full, f_used = sem("d_u4_ready"), sem("d_f_full"), sem("d_f_used")

        BLOCK_D = DP * (1 + FG)
        BLOCK_U = NF * FG

        with nc.Block() as block:
            def load_up(sp, g, i):
                src = io["w_up"].rearrange("(c p) (g n) -> g p c n", p=P, g=FG)[bass.ds(g, 1)]
                sp.dma_start(w_up[i][:], src.rearrange("o p c n -> (o p) c n")).then_inc(up_in[i], 16)

            def load_down(sp, g, i):
                src = io["w_down"].rearrange("(g f p) n -> g p f n", p=P, f=NF)[bass.ds(g, 1)]
                sp.dma_start(w_down[i][:], src.rearrange("o p f n -> (o p) f n")).then_inc(down_in[i], 16)

            @block.sync
            def _(sp):
                def load_mix(blk):
                    src = io["mixT"].rearrange("c p n -> p c n")[:, :, blk * 512:(blk + 1) * 512]
                    sp.dma_start(mix[:], src).then_inc(mix_in, 16)

                def load_x(blk):
                    if blk < NB:
                        src = io["x_prompt"].rearrange("(b t p) d -> b p t d", p=P, t=TB)[blk]
                        sp.dma_start(y[blk % 2][:], src).then_inc(y_in, 16)
                    else:
                        sp.dma_start(y[blk % 2][0:NS, 0, :], io["x_sample"]).then_inc(y_in, 16)

                load_mix(0)
                sp.dma_start(gain_mlp[:], io["norm_mlp"]).then_inc(const_in, 16)
                sp.dma_start(gain_head[:], io["subln_gain"]).then_inc(const_in, 16)
                sp.dma_start(gain_last[:], io["final_norm"].broadcast_to([P, D])).then_inc(const_in, 16)
                sp.dma_start(fold[:], io["same_row"]).then_inc(const_in, 16)
                sp.dma_start(w_out[:], io["w_out"].rearrange("(c p) n -> p c n", p=P)).then_inc(out_in, 16)
                load_x(0)
                for g in range(2):
                    load_up(sp, g, g)
                    load_down(sp, g, g)
                for blk in range(NB + 1):
                    if blk < NB:
                        sp.wait_ge(d_full, 1 + blk * BLOCK_D + DP)
                        if blk + 1 < NB:
                            load_mix(blk + 1)
                        if blk >= 1:
                            sp.wait_ge(stored[(blk + 1) % 2], 16 * TB * ((blk + 1) // 2))
                        load_x(blk + 1)
                    group_u, group_d = (NF, DP) if blk < NB else (1, 2)
                    base_d = blk * BLOCK_D + (DP if blk < NB else 2)

                    def reload(gg, i):
                        sp.wait_ge(u_full, gg * (2 * group_u) + (blk * BLOCK_U + (i + 1) * group_u))
                        sp.sem_inc(sp_gate, 1)
                        g = (2 * gg + 2 + i) % FG if isinstance(gg, int) else gg * 2 + (2 + i)
                        load_up(sp, g, i)
                        sp.wait_ge(d_full, 1 + gg * (2 * group_d) + (base_d + (i + 1) * group_d))
                        sp.sem_inc(sp_gate, 1)
                        load_down(sp, g, i)

                    with sp.Fori(0, FG // 2 - 1) as gg:
                        for i in range(2):
                            reload(gg, i)
                    if blk < NB:
                        for i in range(2):
                            reload(FG // 2 - 1, i)

            @block.gpsimd
            def _(pool):
                for blk in range(NB):
                    for t in range(TB):
                        pool.wait_ge(y_ready, blk * TB + t + 1)
                        dst = io["y_p"].rearrange("(b t p) d -> b t p d", p=P, t=TB)[blk, t]
                        pool.dma_start(dst, y[blk % 2][:, t, :]).then_inc(stored[blk % 2], 16)
                pool.wait_ge(y_ready, NB * TB + 1)
                pool.dma_start(io["y_s"], y[NB % 2][0:NS, 0, :]).then_inc(stored[NB % 2], 16)
                for i in range(2):
                    pool.wait_ge(stored[i], 16 * TB * (NB // 2) + 16 * (NB % 2 == i))

            @block.tensor
            def _(pe):
                pe.sem_inc(d_full, 1)
                pe.sem_inc(f_full, 1)
                pe.wait_ge(const_in, 64)
                pe.wait_ge(ones_ready, 1)
                turns = Count()

                def bank():
                    n = turns.n
                    turns.up()
                    if n >= 2:
                        pe.wait_ge(hT_ready, n - 1)
                    return t_ps[n % 2]

                def head_sums(blk):
                    heads, cols = (NH, 512) if blk < NB else (1, NH * NS)
                    for h in range(heads):
                        pe.wait_ge(squared, blk * NH + h + 1)
                        dst = bank()
                        nc.tensor.matmul(dst[:, 0:cols], ones[:], square[:, 0:cols], start=True,
                                         stop=True).then_inc(summed, 1)

                def project_out(blk, t):
                    rows = P if blk < NB else NS
                    if t == 0:
                        pe.wait_ge(mix_ready, min(blk, NB) * NH + (NH if blk < NB else 1))
                    for half in range(2):
                        n = blk * BLOCK_D + 2 * t + half
                        if n >= DB:
                            pe.wait_ge(d_used, n - DB + 1)
                        for c in range(KC):
                            lhs = mix[:, c, t * P:(t + 1) * P] if blk < NB else keep["mixsT"][:, c, :]
                            last = nc.tensor.matmul(d_ps[n % DB][0:rows, :], lhs,
                                                    w_out[:, c, half * 512:(half + 1) * 512],
                                                    start=(c == 0), stop=(c == KC - 1))
                        last.then_inc(d_full, 1)

                def turn_h(blk, t):
                    rows = P if blk < NB else NS
                    pe.wait_ge(hs_ready, blk * TB + t + 1)
                    for half in range(2):
                        dst = bank()
                        for c in range(4):
                            last = nc.tensor.transpose(dst[:, c * P:c * P + rows],
                                                       hs[t % 2][0:rows, (4 * half + c) * P:(4 * half + c + 1) * P],
                                                       keep["ident"][0:rows, 0:rows])
                        last.then_inc(h_turned, 1)

                pe.wait_ge(mix_in, 16)
                head_sums(0)
                pe.wait_ge(out_in, 16)
                for blk in range(NB):
                    project_out(blk, 0)
                    for t in range(TB):
                        if t + 1 < TB:
                            project_out(blk, t + 1)
                        turn_h(blk, t)
                    pe.wait_ge(hT_ready, turns.n)
                    with pe.Fori(0, FG // 2) as gg:
                        for i in range(2):
                            pe.wait_ge(up_in[i], gg * 16 + (blk * (FG // 2) + 1) * 16)
                            for f in range(NF):
                                n = blk * BLOCK_U + i * NF + f
                                pe.wait_ge(u_used, gg * (2 * NF) + (n + 1))
                                for c in range(KC):
                                    last = nc.tensor.matmul(u_ps[f % 2][:, :], w_up[i][:, c, f * P:(f + 1) * P],
                                                            hT[:, c, :], start=(c == 0), stop=(c == KC - 1))
                                last.then_inc(u_full, 1)
                            pe.wait_ge(down_in[i], gg * 16 + (blk * (FG // 2) + 1) * 16)
                            for t in range(TB):
                                for half in range(2):
                                    n = blk * BLOCK_D + DP + i * DP + 2 * t + half
                                    pe.wait_ge(d_used, gg * (2 * DP) + (n - DB + 1))
                                    for f in range(NF):
                                        if t == 0 and half == 0:
                                            pe.wait_ge(u_used, 2 + gg * (2 * NF) + (blk * BLOCK_U + i * NF + f + 1))
                                        last = nc.tensor.matmul(d_ps[n % DB][:, :], uT[i][:, f, t * P:(t + 1) * P],
                                                                w_down[i][:, f, half * 512:(half + 1) * 512],
                                                                start=(f == 0), stop=(f == NF - 1))
                                    last.then_inc(d_full, 1)
                    head_sums(blk + 1)
                d0 = NB * BLOCK_D
                project_out(NB, 0)
                turn_h(NB, 0)
                pe.wait_ge(hT_ready, turns.n)
                with pe.Fori(0, FG // 2) as gg:
                    for i in range(2):
                        pe.wait_ge(up_in[i], gg * 16 + (NB * (FG // 2) + 1) * 16)
                        n = NB * BLOCK_U + i
                        pe.wait_ge(u_used, 2 + gg * 2 + n)
                        for c in range(KC):
                            j = c % 4
                            last = nc.tensor.matmul(u_ps[0][NS * j:NS * (j + 1), :], hT[:, c, 0:NS], w_up[i][:, c, :],
                                                    start=(c < 4), stop=(c >= 4))
                        last.then_inc(u_full, 1)
                        pe.wait_ge(u4_ready, gg * 2 + (i + 1))
                        for f in range(NF):
                            last = nc.tensor.matmul(u_ps[1][:, f * NS:(f + 1) * NS], square[:, f * P:(f + 1) * P],
                                                    fold[:, 0:NS], start=True, stop=True)
                        last.then_inc(f_full, 1)
                        pe.wait_ge(u_used, 2 + gg * 2 + (n + 1))
                        pe.wait_ge(down_in[i], gg * 16 + (NB * (FG // 2) + 1) * 16)
                        pe.wait_ge(d_used, gg * 4 + (d0 + 2 + 2 * i))
                        for f in range(NF):
                            for half in range(2):
                                last = nc.tensor.matmul(d_ps[half][NS * f:NS * (f + 1), :], uT[i][:, f, 0:NS],
                                                        w_down[i][:, f, half * 512:(half + 1) * 512],
                                                        start=True, stop=True)
                            if f >= NF - 1:
                                last.then_inc(d_full, 2)
                pe.wait_ge(d_used, d0 + 2 + 2 * FG)
                for half in range(2):
                    nc.tensor.matmul(d_ps[2 + half][0:NS, :], fold[:, 0:NS], hs[1][:, half * 512:(half + 1) * 512],
                                     start=True, stop=True).then_inc(d_full, 1)

            @block.scalar
            def _(act):
                row_events = Count()

                def head_roots(blk):
                    if blk < NB:
                        act.wait_ge(mix_in, 16 * (blk + 1))
                    heads, cols = (NH, 512) if blk < NB else (1, NH * NS)
                    for h in range(heads):
                        n = blk * NH + h
                        src = mix[:, NP + h, :] if blk < NB else keep["mixsT"][:, NP:2 * NP, :]
                        dst = square[:, 0:cols] if blk < NB else square[:, 0:cols].rearrange("p (a b) -> p a b", a=NH)
                        if n:
                            act.wait_ge(summed, n)
                        nc.scalar.activation(dst, src, ACT.Square).then_inc(squared, 1)
                        act.wait_ge(var_ready, n + 1)
                        nc.scalar.activation(root[:, 0:cols], root[:, 0:cols], ACT.Sqrt).then_inc(rooted, 1)

                def row_root(rows, src, junk, ready):
                    ready()
                    nc.scalar.activation(junk, src, ACT.Square, accum_out=stat[0:rows, 0:1]).then_inc(row_squared, 1)
                    act.wait_ge(row_var, row_events.up())
                    nc.scalar.activation(stat[0:rows, 2:3], stat[0:rows, 1:2], ACT.Sqrt).then_inc(row_rooted, 1)

                def early(blk, t):
                    rows = P if blk < NB else NS

                    def ready():
                        act.wait_ge(d_used, blk * BLOCK_D + 2 * (t + 1))
                        if blk * TB + t >= 2:
                            act.wait_ge(h_turned, 2 * (blk * TB + t - 1))

                    row_root(rows, y[blk % 2][0:rows, t, :], hs[t % 2][0:rows], ready)

                def late(blk, t):
                    rows = P if blk < NB else NS

                    def ready():
                        act.wait_ge(d_used, (blk + 1) * BLOCK_D if blk < NB else NB * BLOCK_D + 2 + 2 * FG + 2)
                        if blk < NB:
                            act.wait_ge(h_turned, 2 * TB * (blk + 1))

                    row_root(rows, y[blk % 2][0:rows, t, :], hs[0][0:rows], ready)

                head_roots(0)
                for blk in range(NB):
                    for t in range(TB):
                        early(blk, t)
                    with act.Fori(0, FG // 2) as gg:
                        for i in range(2):
                            for f in range(NF):
                                n = blk * BLOCK_U + i * NF + f
                                act.wait_ge(u_full, gg * (2 * NF) + (n + 1))
                                act.wait_ge(d_full, 1 + gg * (2 * DP) + (blk * BLOCK_D + i * DP))
                                nc.scalar.activation(uT[i][:, f, :], u_ps[f % 2][:], ACT.Relu).then_inc(u_relued, 1)
                    head_roots(blk + 1)
                    for t in range(TB):
                        late(blk, t)
                early(NB, 0)
                with act.Fori(0, FG // 2) as gg:
                    for i in range(2):
                        act.wait_ge(u_full, gg * 2 + (NB * BLOCK_U + i + 1))
                        act.wait_ge(f_full, gg * 2 + 1 + i)
                        nc.scalar.copy(square[:], u_ps[0][:]).then_inc(u4_ready, 1)
                        act.wait_ge(f_full, gg * 2 + 1 + (i + 1))
                        act.wait_ge(d_full, 1 + gg * 4 + (NB * BLOCK_D + 2 * i))
                        nc.scalar.activation(uT[i][:, :, 0:NS], u_ps[1][:, 0:NF * NS].rearrange(
                            "p (f n) -> p f n", f=NF), ACT.Relu).then_inc(u_relued, 1)
                late(NB, 0)

            @block.vector
            def _(dve):
                link = linker(dve, vec, Count())
                row_events = Count()
                dve.wait_ge(const_in, 64)
                nc.vector.memset(ones[:], 1.0).then_inc(ones_ready, 1)
                dve.sem_inc(u_used, 2)
                link(nc.vector.tensor_scalar(gain_head[:], gain_head[:], 1.0 - LAMBDA_INIT, None, ALU.mult))

                def head_norms(blk):
                    heads, cols = (NH, 512) if blk < NB else (1, NH * NS)
                    for h in range(heads):
                        n = blk * NH + h
                        dve.wait_ge(summed, n + 1)
                        nc.vector.tensor_scalar(root[:, 0:cols], t_ps[sum_bank[n] % 2][:, 0:cols], 1.0 / P, SUB_EPS,
                                                ALU.mult, ALU.add).then_inc(var_ready, 1)
                        dve.wait_ge(var_ready, n + 1)
                        dve.sem_inc(hT_ready, 1)
                        dve.wait_ge(rooted, n + 1)
                        link(nc.vector.reciprocal(root[:, 0:cols], root[:, 0:cols]))
                        if blk < NB:
                            m, r = mix[:, NP + h, :], root[:, 0:cols]
                        else:
                            m, r = keep["mixsT"][:, NP:2 * NP, :], root[:, 0:cols].rearrange("p (a b) -> p a b", a=NH)
                        nc.vector.scalar_tensor_tensor(out=m, in0=m, scalar=gain_head[:, 0:1], in1=r,
                                                       op0=ALU.mult, op1=ALU.mult).then_inc(mix_ready, 1)
                        dve.wait_ge(mix_ready, n + 1)

                def row_norm(rows):
                    n = row_events.up()
                    dve.wait_ge(row_squared, n)
                    nc.vector.tensor_scalar(stat[0:rows, 1:2], stat[0:rows, 0:1], 1.0 / D, EPS,
                                            ALU.mult, ALU.add).then_inc(row_var, 1)
                    dve.wait_ge(row_rooted, n)
                    link(nc.vector.reciprocal(stat[0:rows, 3:4], stat[0:rows, 2:3]))

                def residual(blk, t):
                    rows = P if blk < NB else NS
                    if t == 0:
                        dve.wait_ge(y_in, 16 * (blk + 1))
                    for half in range(2):
                        n = blk * BLOCK_D + 2 * t + half
                        part = y[blk % 2][0:rows, t, half * 512:(half + 1) * 512]
                        dve.wait_ge(d_full, 1 + n + 1)
                        nc.vector.tensor_tensor(part, part, d_ps[n % DB][0:rows, :], ALU.add).then_inc(d_used, 1)

                def normed(blk, t):
                    rows = P if blk < NB else NS
                    row_norm(rows)
                    nc.vector.tensor_scalar(hs[t % 2][0:rows], y[blk % 2][0:rows, t, :], stat[0:rows, 3:4], None,
                                            ALU.mult).then_inc(hs_ready, 1)

                def spread(blk, t):
                    rows = P if blk < NB else NS
                    if t == 0 and blk:
                        dve.wait_ge(u_full, blk * BLOCK_U)
                    for half in range(2):
                        dve.wait_ge(h_turned, 2 * (blk * TB + t) + half + 1)
                        src = t_ps[turn_bank[blk * TB + t] % 2 ^ half][:].rearrange("p (c n) -> p c n", c=4)[:, :, 0:rows]
                        g = gain_mlp[:, 4 * half:4 * half + 4].unsqueeze(2).broadcast_to([P, 4, rows])
                        nc.vector.tensor_tensor(hT[:, 4 * half:4 * half + 4, t * P:t * P + rows], src, g,
                                                ALU.mult).then_inc(hT_ready, 1)

                def last_norm(blk, t):
                    rows = P if blk < NB else NS
                    row_norm(rows)
                    part = y[blk % 2][0:rows, t, :]
                    nc.vector.scalar_tensor_tensor(out=part, in0=part, scalar=stat[0:rows, 3:4],
                                                   in1=gain_last[0:rows], op0=ALU.mult,
                                                   op1=ALU.mult).then_inc(y_ready, 1)

                sum_bank, turn_bank, at = {}, {}, 0
                for blk in range(NB + 1):
                    for h in range(NH if blk < NB else 1):
                        sum_bank[blk * NH + h] = at
                        at += 1
                    for t in range(TB if blk < NB else 1):
                        turn_bank[blk * TB + t] = at
                        at += 2

                head_norms(0)
                for blk in range(NB):
                    residual(blk, 0)
                    for t in range(TB):
                        normed(blk, t)
                        if t + 1 < TB:
                            residual(blk, t + 1)
                        spread(blk, t)
                    with dve.Fori(0, FG // 2) as gg:
                        for i in range(2):
                            for f in range(NF):
                                n = blk * BLOCK_U + i * NF + f
                                dve.wait_ge(u_relued, gg * (2 * NF) + (n + 1))
                                nc.vector.tensor_tensor(uT[i][:, f, :], uT[i][:, f, :], u_ps[f % 2][:],
                                                        ALU.mult).then_inc(u_used, 1)
                            for t in range(TB):
                                for half in range(2):
                                    n = blk * BLOCK_D + DP + i * DP + 2 * t + half
                                    part = y[blk % 2][:, t, half * 512:(half + 1) * 512]
                                    dve.wait_ge(d_full, 1 + gg * (2 * DP) + (n + 1))
                                    nc.vector.tensor_tensor(part, part, d_ps[n % DB][:], ALU.add).then_inc(d_used, 1)
                    head_norms(blk + 1)
                    for t in range(TB):
                        last_norm(blk, t)
                d0 = NB * BLOCK_D
                residual(NB, 0)
                normed(NB, 0)
                spread(NB, 0)
                link(nc.vector.memset(hs[1][:], 0.0))
                with dve.Fori(0, FG // 2) as gg:
                    for i in range(2):
                        dve.wait_ge(u_relued, gg * 2 + (NB * BLOCK_U + i + 1))
                        nc.vector.tensor_tensor(uT[i][:, :, 0:NS], uT[i][:, :, 0:NS],
                                                u_ps[1][:, 0:NF * NS].rearrange("p (f n) -> p f n", f=NF),
                                                ALU.mult).then_inc(u_used, 1)
                        dve.wait_ge(d_full, 1 + gg * 4 + (d0 + 2 + 2 * (i + 1)))
                        for half in range(2):
                            part = hs[1][:, half * 512:(half + 1) * 512]
                            nc.vector.tensor_tensor(part, part, d_ps[half][:], ALU.add).then_inc(d_used, 1)
                for half in range(2):
                    dve.wait_ge(d_full, 1 + d0 + 2 + 2 * FG + half + 1)
                    part = y[NB % 2][0:NS, 0, half * 512:(half + 1) * 512]
                    nc.vector.tensor_tensor(part, part, d_ps[2 + half][0:NS, :], ALU.add).then_inc(d_used, 1)
                last_norm(NB, 0)


def build(nc, io):
    with ExitStack() as ctx:
        sb = lambda n, s: ctx.enter_context(nc.sbuf_tensor(n, s, F32))
        keep = {"ident": sb("ident", [P, P]), "qsT": sb("qsT", [P, 2 * NP, NS]), "ksT": sb("ksT", [P, 2 * NP, NS]),
                "mixsT": sb("mixsT", [P, 2 * NP, NS]), "neg_lam": sb("neg_lam", [P, 1])}
        for name, dt in (("qT", F32), ("kT", F32), ("mixT", F32)):
            io[name] = nc.dram_tensor(name, [2 * NP, P, S], dt, kind="Internal").ap()
        project(nc, io, keep)
        attend_prompt(nc, io, keep)
        attend_decode(nc, io, keep)
        mlp(nc, io, keep)


def rope_tables():
    half = ROT // 2
    inv = np.float32(THETA) ** (-np.arange(half, dtype=np.float32) * np.float32(2.0) / np.float32(ROT))
    pos = np.zeros((NT + 1, P), np.float32)
    pos[:NT] = np.arange(S).reshape(NT, P)
    pos[NT, :NS] = PAGES * PAGE + np.arange(NS) % TD
    ang = (pos[:, :, None] * inv).astype(np.float32).astype(np.float64)
    cos, sin = np.cos(ang), np.sin(ang)
    lay = lambda a: np.ascontiguousarray(a.transpose(1, 0, 2).astype(np.float32))
    return lay(np.concatenate([cos, cos], -1)), lay(np.concatenate([-sin, sin], -1))


def log_reads(dist):
    reads = sum(((dist >= 0) & (dist <= w) & (dist % d == 0)).astype(np.float64) for w, d in BRANCHES)
    return np.where(reads > 0, np.log(np.maximum(reads, 1)) / SCALE, NEG).astype(np.float32)


def decode_constants():
    row = np.arange(SL * ROWS)
    slot, pair, which, t = row // ROWS, row % ROWS // (2 * TD), row % (2 * TD) // TD, row % TD
    key = np.arange(P)
    pos = np.stack([16 * (g * 32 + key // TD) + key % TD for g in range(3)]
                   + [1536 + g * P + key for g in range(4)] + [np.full(P, 2 * WIN)])
    pos = pos.reshape(SL, 2 * P)[slot]
    win = log_reads(np.where(pos < WIN, WIN + t[:, None] - pos, -1))
    ago = t[:, None] - np.arange(TD)[None, :]
    new = np.stack([log_reads(ago), np.where(ago >= 0, 0, NEG).astype(np.float32)], 1)
    col = np.arange(GW)
    same_pair = pair[:, None] == col[None, :] // P
    own = np.stack([same_pair & (which[:, None] == col[None, :] % P // HD), same_pair], 1)
    f = lambda a: np.ascontiguousarray(a.astype(np.float32))
    return {"bias_win": f(win), "bias_new": f(new), "own_head": f(own),
            "same_row": f(row[:, None] % ROWS == row[None, :] % ROWS),
            "token": f(t[:, None] == np.arange(TD)[None, :]), "map_of": f(np.stack([which == 1, which == 0], 1))}


def constants():
    cos, sin = rope_tables()
    dist = (NT - 1) * P + np.arange(P)[:, None] - np.arange(S)[None, :]
    return {"ident": np.eye(P, dtype=np.float32), "cos": cos, "sin": sin,
            "bias_dilated": log_reads(dist), "bias_causal": np.where(dist >= 0, 0, NEG).astype(np.float32),
            **decode_constants()}


OUTPUTS = (("y_p", (1, S, D)), ("y_s", (ND, TD, D)), ("kb_p", (1, 1, S, 4, 2 * HD)), ("vb_p", (1, 1, S, 4, 2 * HD)),
           ("ka_p", (1, 1, S, 8, HD)), ("va_p", (1, 1, S, 8, HD)),
           ("kb_s", (1, ND, TD, 4, 2 * HD)), ("vb_s", (1, ND, TD, 4, 2 * HD)),
           ("ka_win", (1, ND, WIN, 8, HD)), ("va_win", (1, ND, WIN, 8, HD)))
SHAPES = {"y_p": (S, D), "y_s": (NS, D), "kb_p": (S, GW), "vb_p": (S, GW), "ka_p": (S, GW), "va_p": (S, GW),
          "kb_s": (NS, GW), "vb_s": (NS, GW), "ka_win": (ND, WIN, GW), "va_win": (ND, WIN, GW)}


def lay_out(inputs):
    a = {k: np.asarray(v) for k, v in inputs.items()}
    by_chunk = lambda v: np.ascontiguousarray(v.reshape(-1, P).T)
    out = {
        "x_prompt": a["x_prompt"].reshape(S, D), "x_sample": a["x_sample"].reshape(NS, D),
        "ka_state": a["state_win_k"].reshape(ND, WIN, GW), "va_state": a["state_win_v"].reshape(ND, WIN, GW),
        "k_cache": a["cache_diff_k"].reshape(NPHYS, PAGE, GW), "v_cache": a["cache_diff_v"].reshape(NPHYS, PAGE, GW),
        "page_table": a["page_table"].reshape(1, ND * PAGES),
        "norm_attn": by_chunk(a["norm_attn"]), "norm_mlp": by_chunk(a["norm_mlp"]),
        "final_norm": a["final_norm"].reshape(1, D), "subln_gain": a["subln_gain"].reshape(P, 1),
        "lambdas": np.stack([a[k].reshape(HD) for k in ("lambda_q1", "lambda_q2", "lambda_k1", "lambda_k2")]).reshape(1, 4 * HD),
        "w_in": a["w_in"][0], "w_out": a["w_out"][0], "w_up": a["w_up"][0], "w_down": a["w_down"][0],
    }
    out.update(constants())
    return {k: np.ascontiguousarray(v) for k, v in out.items()}


def kernel(**inputs):
    import concourse.bacc as bacc
    from concourse.bass_utils import run_bass_kernel_spmd

    nc = bacc.Bacc("TRN2", target_bir_lowering=False, num_devices=1)
    arrays = lay_out(inputs)
    io = {k: nc.dram_tensor("in_" + k, v.shape, mybir.dt.from_np(v.dtype), kind="ExternalInput").ap()
          for k, v in arrays.items()}
    for k, _ in OUTPUTS:
        io[k] = nc.dram_tensor("out_" + k, SHAPES[k], F32, kind="ExternalOutput").ap()
    build(nc, io)
    r = run_bass_kernel_spmd(nc, [{"in_" + k: v for k, v in arrays.items()}], core_ids=[0])
    return tuple(np.asarray(r.results[0]["out_" + k]).reshape(s) for k, s in OUTPUTS)
```

```python
import math
from contextlib import ExitStack

import numpy as np

import concourse.bass as bass
import concourse.mybir as mybir

F32 = mybir.dt.float32
I32 = mybir.dt.int32
ALU = mybir.AluOpType
ACT = mybir.ActivationFunctionType
AX = mybir.AxisListType

P = 128
D = 1024
S = 2048
ND, TD = 8, 4
NS = ND * TD
HD = 64
GW = 512
NP = GW // P
FF = 4096
WIN = 2048
PAGES, PAGE = 64, 128
NPHYS = 640
BRANCHES = ((128, 1), (512, 4), (2048, 16))
KC = D // P
NT = S // P
ROT = HD // 4
THETA = 500000.0
SCALE = HD ** -0.5
LAMBDA_INIT = 0.8 - 0.6 * math.exp(0.0)
NEG = -1.0e30
BIG = 3.0e38
EPS, SUB_EPS = 1e-6, 1e-5


class Count:

    def __init__(self, base=0):
        self.base, self.n = base, 0

    def up(self, k=1):
        self.n += k
        return self.base + self.n


def linker(eng, sem, count):
    def link(ins):
        ins.then_inc(sem, 1)
        eng.wait_ge(sem, count.up())
    return link


def project(nc, io, keep):
    F32R = mybir.dt.float32r
    GROUPS = ("q", "k", "v")
    NG, NR = 3, 2
    NTT = NT + 1
    ZB = 3
    with ExitStack() as ctx:
        sb = lambda n, s, d=F32: ctx.enter_context(nc.sbuf_tensor(n, s, d))
        ps = lambda n: ctx.enter_context(nc.psum_tensor(n, [P, 512], F32))
        sem = lambda n: ctx.enter_context(nc.semaphore(n))
        w_raw = [sb(f"a_w_raw{i}", [P, KC, GW]) for i in range(2)]
        w_hi = [sb(f"a_w_hi{i}", [P, KC, GW], F32R) for i in range(NG)]
        w_lo = [sb(f"a_w_lo{i}", [P, KC, GW], F32R) for i in range(NG)]
        gain = sb("a_gain", [P, KC])
        cos = sb("a_cos", [P, NTT, ROT])
        sin = sb("a_sin", [P, NTT, ROT])
        x = [sb(f"a_x{b}", [P, D]) for b in range(2)]
        xs = sb("a_xs", [P, D])
        xT = sb("a_xT", [P, KC, P])
        xT_hi = [sb(f"a_xT_hi{b}", [P, KC, P], F32R) for b in range(2)]
        xT_lo = [sb(f"a_xT_lo{b}", [P, KC, P], F32R) for b in range(2)]
        stat = sb("a_stat", [P, 4])
        z = [sb(f"a_z{b}", [P, NG, GW]) for b in range(2)]
        rot = sb("a_rot", [P, 2, GW // HD, ROT])
        zT = [sb(f"a_zT{b}", [P, NR, NP, P]) for b in range(2)]
        x_turn = [ps(f"a_turn{i}") for i in range(2)]
        z_ps = [ps(f"a_zps{i}") for i in range(ZB)]
        z_turn = [ps(f"a_zturn{i}") for i in range(2)]

        const_in = sem("a_const_in")
        w_landed = [sem(f"a_w_landed{i}") for i in range(2)]
        w_hi_ready = sem("a_w_hi_ready")
        w_ready = [sem(f"a_w_ready{i}") for i in range(2)]
        x_landed = [sem(f"a_x_landed{b}") for b in range(2)]
        squared = sem("a_squared")
        var_ready = sem("a_var_ready")
        root_ready = sem("a_root_ready")
        xs_ready = sem("a_xs_ready")
        x_turned = sem("a_x_turned")
        xT_read = sem("a_xT_read")
        xT_ready = sem("a_xT_ready")
        z_summed = sem("a_z_summed")
        z_free = sem("a_z_free")
        rotated = sem("a_rotated")
        z_turned = sem("a_z_turned")
        zT_ready = sem("a_zT_ready")
        stored = [sem(f"a_stored{b}") for b in range(2)]
        vec = sem("a_vec")
        VEC = 2 * NR + 1 + 2
        copied = sem("a_copied")

        w_cols = io["w_in"].rearrange("(c p) (g n) -> g p c n", p=P, n=GW)
        name = lambda h, i: GROUPS[i] + "ab"[h]
        extra = 16 * (2 * ND - 4)

        def rows_of(it):
            return NS if isinstance(it, int) and it == NT else P

        def last(n):
            return isinstance(n, int) and n == 2 * NTT - 1

        def phase(prologue, step):
            def run(eng):
                prologue()
                for h in range(2):
                    with eng.Fori(0, (NT - 2) // 2) as p:
                        for i in range(2):
                            step(h, p * 2 + i, p * 2 + (i + h * NTT), (i + h) % 2)
                    for it in range(NT - 2, NTT):
                        step(h, it, it + h * NTT, (it + h) % 2)
            return run

        def after(it):
            return 0 if isinstance(it, int) and it == NT else it + 1

        with nc.Block() as block:
            @block.sync
            def _(sp):
                def load(it, b):
                    src = io["x_sample"] if rows_of(it) == NS else io["x_prompt"].rearrange(
                        "(t p) d -> t p d", p=P)[bass.ds(it, 1)].rearrange("o p d -> (o p) d")
                    sp.dma_start(x[b][0:rows_of(it)], src).then_inc(x_landed[b], 16)

                def load_w(k):
                    if k >= 2:
                        sp.wait_ge(w_ready[(k - 2) // NG], (k - 2) % NG + 1)
                    sp.dma_start(w_raw[k % 2][:], w_cols[k]).then_inc(w_landed[k % 2], 16)

                def prologue():
                    for b in range(2):
                        sp.sem_inc(stored[b], 1)
                    load(0, 0)
                    load_w(0)
                    for source, dst in (("norm_attn", gain), ("cos", cos), ("sin", sin), ("ident", keep["ident"])):
                        sp.dma_start(dst[:], io[source]).then_inc(const_in, 16)
                    load_w(1)
                    load(1, 1)
                    load_w(2)

                def step(h, it, n, b):
                    r = rows_of(it)
                    if not (isinstance(it, int) and h and it >= NT - 1):
                        sp.wait_ge(xs_ready, n + 1)
                        load(after(after(it)), b)
                    for i in range(NG):
                        if GROUPS[i] == "q":
                            continue
                        if i < NR:
                            sp.wait_ge(rotated, n * NR + (i + 1))
                        else:
                            sp.wait_ge(z_free, n * NG + (ZB + i + 1))
                        g = name(h, i)
                        if r == P:
                            dst = io[g + "_p"].rearrange("(t p) n -> t p n", p=P)[bass.ds(it, 1)]
                            sp.dma_start(dst.rearrange("o p n -> (o p) n"), z[b][:, i, :]).then_inc(stored[b], 16)
                        elif h:
                            sp.dma_start(io[g + "_s"], z[b][0:NS, i, :]).then_inc(stored[b], 16)
                        else:
                            for s in range(ND):
                                sp.dma_start(io[g + "_win"][s, WIN - TD:WIN, :],
                                             z[b][s * TD:(s + 1) * TD, i, :]).then_inc(stored[b], 16)
                    if r == P:
                        for i in range(NR):
                            sp.wait_ge(zT_ready, n * NR + (2 + i + 1))
                            dst = io[GROUPS[i] + "T"].rearrange("g p (t n) -> t p g n", n=P)[bass.ds(it, 1)]
                            sp.dma_start(dst[:, :, h * NP:(h + 1) * NP].rearrange("o p g n -> (o p) g n"),
                                         zT[b][:, i]).then_inc(stored[b], 16)
                    if isinstance(it, int) and h == 0:
                        load_w(NG + it - (NT - 2))
                    if last(n):
                        for p, mine in ((0, 2 * ND * 16), (1, 2 * 16)):
                            sp.wait_ge(stored[p], 1 + 64 * NT + mine)

                phase(prologue, step)(sp)

            @block.gpsimd
            def _(pool):
                body = (WIN - TD) // 16 * 16
                pool.wait_ge(w_ready[0], NG)

                def copy_window(n):
                    pool.wait_ge(xs_ready, n * 3 + 5)
                    for k in ("ka", "va"):
                        src = io[k + "_state"][bass.ds(n, 1)].rearrange("o t n -> (o t) n")
                        dst = io[k + "_win"][bass.ds(n, 1)].rearrange("o t n -> (o t) n")
                        pool.dma_start(dst[0:body].rearrange("(a b) n -> a b n", a=16),
                                       src[TD:TD + body].rearrange("(a b) n -> a b n", a=16)).then_inc(copied, 16)
                        pool.dma_start(dst[body:WIN - TD], src[TD + body:WIN]).then_inc(copied, 16)

                with pool.Fori(0, ND // 2) as n:
                    copy_window(n)
                for i in range(NG):
                    pool.wait_ge(w_hi_ready, NG + i + 1)
                    nc.gpsimd.tensor_tensor(w_lo[i][:], w_raw[(NG + i) % 2][:], w_hi[i][:].bitcast(F32),
                                            ALU.subtract).then_inc(w_ready[1], 1)
                with pool.Fori(ND // 2, ND) as n:
                    copy_window(n)
                pool.wait_ge(copied, 16 * 4 * ND)

            @block.scalar
            def _(act):
                def norm(it, n, b):
                    r = rows_of(it)
                    act.wait_ge(x_landed[b], (n - b) * 8 + 16)
                    if not isinstance(n, int) or n:
                        act.wait_ge(x_turned, n * 2)
                    nc.scalar.activation(xs[0:r], x[b][0:r], ACT.Square,
                                         accum_out=stat[0:r, 0:1]).then_inc(squared, 1)
                    act.wait_ge(var_ready, n + 1)
                    nc.scalar.activation(stat[0:r, 2:3], stat[0:r, 1:2], ACT.Sqrt).then_inc(root_ready, 1)

                def split(k):
                    act.wait_ge(w_landed[k % 2], 16 * (k // 2 + 1))
                    if k >= NG:
                        act.wait_ge(z_summed, NT * NG + (k - NG) + 2)
                    nc.scalar.copy(w_hi[k % NG][:], w_raw[k % 2][:]).then_inc(w_hi_ready, 1)

                def prologue():
                    act.sem_inc(z_free, ZB)
                    act.sem_inc(zT_ready, 2)
                    norm(0, 0, 0)
                    for k in range(NG):
                        split(k)

                def step(h, it, n, b):
                    r = rows_of(it)
                    act.wait_ge(stored[b], (n - b) * 32 + (1 + (extra if h and b == 0 else 0)))
                    if not last(n):
                        norm(after(it), n + 1, 1 - b)
                    for i in range(NG):
                        act.wait_ge(z_summed, n * NG + (i + 2))
                        nc.scalar.copy(z[b][0:r, i, :], z_ps[i][0:r, :]).then_inc(z_free, 1)
                        if r == NS and h == 0:
                            split(NG + i)
                    for i in range(NR):
                        act.wait_ge(z_turned, n * NR + (i + 1))
                        dst = zT[b][:, i, :, 0:r] if r == P else keep[GROUPS[i] + "sT"][:, h * NP:(h + 1) * NP, :]
                        src = z_turn[i % 2][:, :].rearrange("p (g n) -> p g n", g=NP)[:, :, 0:r]
                        nc.scalar.copy(dst, src).then_inc(zT_ready, 1)

                phase(prologue, step)(act)

            @block.vector
            def _(dve):
                def norm(it, n, b, link):
                    r = rows_of(it)
                    dve.wait_ge(squared, n + 1)
                    nc.vector.tensor_scalar(stat[0:r, 1:2], stat[0:r, 0:1], 1.0 / D, EPS,
                                            ALU.mult, ALU.add).then_inc(var_ready, 1)
                    dve.wait_ge(root_ready, n + 1)
                    link(nc.vector.reciprocal(stat[0:r, 3:4], stat[0:r, 2:3]))
                    nc.vector.tensor_scalar(xs[0:r], x[b][0:r], stat[0:r, 3:4], None,
                                            ALU.mult).then_inc(xs_ready, 1)

                def spread(it, n, b, link):
                    r = rows_of(it)
                    if not (isinstance(n, int) and n < 2):
                        dve.wait_ge(z_summed, (n - 1) * NG + 1)
                    for h in range(2):
                        dve.wait_ge(x_turned, n * 2 + (h + 1))
                        part = lambda t: t[:, 4 * h:4 * h + 4, 0:r]
                        src = x_turn[h][:, :].rearrange("p (c n) -> p c n", c=4)[:, :, 0:r]
                        g = gain[:, 4 * h:4 * h + 4].unsqueeze(2).broadcast_to([P, 4, r])
                        nc.vector.tensor_tensor(part(xT), src, g, ALU.mult).then_inc(xT_read, 1)
                        dve.wait_ge(xT_read, n * 2 + (h + 1))
                        link(nc.vector.tensor_copy(part(xT_hi[b]), part(xT)))
                        nc.vector.tensor_tensor(part(xT_lo[b]), part(xT), part(xT_hi[b]).bitcast(F32),
                                                ALU.subtract).then_inc(xT_ready, 1)

                def prologue():
                    dve.wait_ge(const_in, 64)
                    link = linker(dve, vec, Count(0))
                    norm(0, 0, 0, link)
                    spread(0, 0, 0, link)
                    for i in range(NG):
                        dve.wait_ge(w_hi_ready, i + 1)
                        nc.vector.tensor_tensor(w_lo[i][:], w_raw[i % 2][:], w_hi[i][:].bitcast(F32),
                                                ALU.subtract).then_inc(w_ready[0], 1)

                def step(h, it, n, b):
                    r = rows_of(it)
                    link = linker(dve, vec, Count(n * VEC + (1 + 2)))
                    if not last(n):
                        norm(after(it), n + 1, 1 - b, link)
                    for i in range(NR):
                        dve.wait_ge(z_free, n * NG + (ZB + i + 1))
                        head = z[b][0:r, i, :].rearrange("p (u e) -> p u e", e=HD)[:, :, 0:ROT]
                        u = GW // HD
                        tab = lambda t: t[0:r, bass.ds(it, 1), :].broadcast_to([r, u, ROT])
                        link(nc.vector.tensor_tensor(rot[0:r, 0], head, tab(cos), ALU.mult))
                        swap = head.rearrange("p u (h e) -> p u h e", h=2)[:, :, ::-1, :]
                        link(nc.vector.tensor_tensor(
                            rot[0:r, 1].rearrange("p u (h e) -> p u h e", h=2), swap,
                            tab(sin).rearrange("p u (h e) -> p u h e", h=2), ALU.mult))
                        nc.vector.tensor_tensor(head, rot[0:r, 0], rot[0:r, 1], ALU.add).then_inc(rotated, 1)
                        dve.wait_ge(rotated, n * NR + (i + 1))
                    if not last(n):
                        spread(after(it), n + 1, 1 - b, link)

                phase(prologue, step)(dve)

            @block.tensor
            def _(pe):
                def turn(it, n, b):
                    r = rows_of(it)
                    if isinstance(n, int) and n == 0:
                        pe.wait_ge(const_in, 64)
                    pe.wait_ge(xs_ready, n + 1)
                    for h in range(2):
                        if not (isinstance(n, int) and n == 0):
                            pe.wait_ge(xT_read, n * 2 - 1 + h)
                        for c in range(4):
                            m = nc.tensor.transpose(x_turn[h][:, c * P:c * P + r],
                                                    xs[0:r, (4 * h + c) * P:(4 * h + c + 1) * P],
                                                    keep["ident"][0:r, 0:r])
                        m.then_inc(x_turned, 1)

                def prologue():
                    pe.sem_inc(z_summed, 1)
                    turn(0, 0, 0)

                def step(h, it, n, b):
                    r = rows_of(it)
                    pe.wait_ge(xT_ready, n * 2 + 2)
                    for i in range(NG):
                        if not isinstance(it, int):
                            pe.wait_ge(w_ready[h], i + 1)
                        pe.wait_ge(z_free, n * NG + (i + 1))
                        dst = z_ps[i][0:r, :]
                        for c in range(KC):
                            x_hi, x_lo = xT_hi[b][:, c, 0:r], xT_lo[b][:, c, 0:r]
                            nc.tensor.matmul(dst, x_hi, w_hi[i][:, c, :], start=(c == 0), stop=False)
                            nc.tensor.matmul(dst, x_hi, w_lo[i][:, c, :], start=False, stop=False)
                            m = nc.tensor.matmul(dst, x_lo, w_hi[i][:, c, :], start=False, stop=(c == KC - 1))
                        m.then_inc(z_summed, 1)
                        if i == 1 and not last(n):
                            turn(after(it), n + 1, 1 - b)
                    for i in range(NR):
                        pe.wait_ge(rotated, n * NR + (i + 1))
                        pe.wait_ge(zT_ready, n * NR + (i + 1))
                        for g in range(NP):
                            m = nc.tensor.transpose(z_turn[i % 2][:, g * P:g * P + r],
                                                    z[b][0:r, i, g * P:(g + 1) * P], keep["ident"][0:r, 0:r])
                        m.then_inc(z_turned, 1)

                phase(prologue, step)(pe)


def attend_prompt(nc, io, keep):
    NQ = 4
    NU = NT // NQ
    PASSES = NP // 2
    SS, TS, WS = 4, 3, 6
    with ExitStack() as ctx:
        sb = lambda n, s, d=F32: ctx.enter_context(nc.sbuf_tensor(n, s, d))
        ps = lambda n: ctx.enter_context(nc.psum_tensor(n, [P, 512], F32))
        sem = lambda n: ctx.enter_context(nc.semaphore(n))
        q = [sb(f"b_q{i}", [P, 2, S]) for i in range(2)]
        k = [sb(f"b_k{i}", [P, S]) for i in range(2)]
        v = [sb(f"b_v{i}", [P, NT, P]) for i in range(2)]
        bias = [sb("b_bias_dilated", [P, S]), sb("b_bias_causal", [P, S])]
        w = [[sb(f"b_w{i}_{t}", [P, S]) for t in range(NQ)] for i in range(2)]
        w1 = [sb(f"b_second{t}", [P, S]) for t in range(NQ)]
        wT = [sb(f"b_wT{i}", [P, 512]) for i in range(WS)]
        o = [sb(f"b_o{i}", [P, 512]) for i in range(2)]
        part = sb("b_part", [P, 2, NU])
        top = sb("b_top", [P, 2])
        shift = sb("b_shift", [P, 2, 2 * NQ])
        total = sb("b_total", [P, 2, 2 * NQ])
        inv = sb("b_inv", [P, 2, 2 * NQ])
        lam_rows = sb("b_lam_rows", [P, 4 * HD])
        lam_prod = sb("b_lam_prod", [P, 2, HD])
        lam_sum = sb("b_lam_sum", [P, 2])
        lam_exp = sb("b_lam_exp", [P, 2])
        s_ps = [ps(f"b_s{i}") for i in range(SS)]
        turn = [ps(f"b_turn{i}") for i in range(TS)]
        o_ps = ps("b_ops")

        bias_in = [sem(f"b_bias_in{i}") for i in range(2)]
        lam_in = sem("b_lam_in")
        lam_summed = sem("b_lam_summed")
        lam_exped = sem("b_lam_exped")
        zeroed = sem("b_zeroed")
        pair_in = [sem(f"b_pair_in{i}") for i in range(2)]
        s_full = sem("b_s_full")
        s_used = sem("b_s_used")
        shift_ready = sem("b_shift_ready")
        exp_done = sem("b_exp_done")
        w_ready = sem("b_w_ready")
        turned = sem("b_turned")
        copied = sem("b_copied")
        wT_used = sem("b_wT_used")
        o_copied = sem("b_o_copied")
        o_half = sem("b_o_half")
        o_out = [sem(f"b_o_out{i}") for i in range(2)]
        vec = sem("b_vec")
        vec_gate = sem("b_vec_gate")

        class Pass:
            def __init__(self, diff):
                self.diff = diff
                self.maps = (0, 1) if diff else (0,)
                self.units = [(i, m, g) for i in range(2) for m in ((0,) if diff else (0, 1)) for g in range(NU)]
                self.n = len(self.units)
                self.part0 = [sum(NQ * (g + 1) * len(self.maps) for _, _, g in self.units[:n]) for n in range(self.n + 1)]
                self.key0 = [sum(NQ * (g + 1) for _, _, g in self.units[:n]) for n in range(self.n + 1)]
                self.rows = NQ * len(self.maps)
                self.links = sum(self.rows * (g > 0) + (3 if diff else 1) * NQ for _, _, g in self.units)

            def halved(self, g):
                return not self.diff and g > 0

        kinds = (Pass(False), Pass(True))
        COUNTS = ("units", "parts", "keys", "rows", "tiles", "vec", "halves")

        def size(kd):
            return dict(units=kd.n, parts=kd.part0[-1], keys=kd.key0[-1], rows=kd.n * kd.rows, tiles=kd.n * NQ, vec=kd.links,
                        halves=sum(kd.halved(g) for _, _, g in kd.units))

        def passes(eng, body):
            done = dict.fromkeys(COUNTS, 0)
            for kd in kinds:
                n = size(kd)
                with eng.Fori(0, PASSES) as r:
                    body(kd, r, {c: r * n[c] + done[c] for c in COUNTS})
                for c in COUNTS:
                    done[c] += PASSES * n[c]

        with nc.Block() as block:
            @block.sync
            def _(sp):
                ends = []
                for pair in range(2 * NP):
                    i, kd = pair % 2, kinds[pair // NP]
                    if pair >= 2:
                        sp.wait_ge(wT_used, ends[pair - 2])
                    sp.dma_start(k[i][:], io["kT"][pair]).then_inc(pair_in[i], 16)
                    for m in range(2):
                        h = slice(m * HD, (m + 1) * HD)
                        sp.dma_start(q[i][h, m, :], io["qT"][pair, h]).then_inc(pair_in[i], 16)
                    if pair < 2:
                        name = ("bias_dilated", "bias_causal")[pair]
                        sp.dma_start(bias[pair][:], io[name]).then_inc(bias_in[pair], 16)
                        if pair == 0:
                            sp.dma_start(lam_rows[:], io["lambdas"].broadcast_to([P, 4 * HD])).then_inc(lam_in, 16)
                    vs = io["vb_p" if kd.diff else "va_p"].rearrange("(t p) (g n) -> g p t n", p=P, g=NP)
                    sp.dma_start(v[i][:], vs[pair % NP]).then_inc(pair_in[i], 16)
                    ends.append((ends[-1] if ends else 0) + kd.key0[-1] // 2)

            @block.gpsimd
            def _(pool):
                for m in range(2):
                    nc.gpsimd.memset(q[1][(1 - m) * HD:(2 - m) * HD, m, :], 0.0).then_inc(zeroed, 1)

            @block.tensor
            def _(pe):
                def body(kd, r, base):
                    def scores(n):
                        i, m, g = kd.units[n]
                        if n % (kd.n // 2) == 0:
                            pe.wait_ge(pair_in[i], r * 64 + (64 * (1 + PASSES * kd.diff)))
                        j = kd.part0[n]
                        for t in range(NQ):
                            for mm in kd.maps:
                                for b in range(g + 1):
                                    pe.wait_ge(s_used, base["parts"] + (j + 1))
                                    lo, hi = b * 512, min((b + 1) * 512, (NQ * g + t + 1) * P)
                                    nc.tensor.matmul(s_ps[j % SS][:, 0:hi - lo],
                                                     q[i][:, m + mm, (NQ * g + t) * P:(NQ * g + t + 1) * P],
                                                     k[i][:, lo:hi], start=True, stop=True).then_inc(s_full, 1)
                                    j += 1

                    def weigh(n):
                        i, m, g = kd.units[n]
                        nk = NQ * (g + 1)
                        pe.wait_ge(w_ready, base["tiles"] + NQ * (n + 1))

                        def turn_keys(kt):
                            e = kd.key0[n] + kt
                            if kt >= TS:
                                pe.wait_ge(copied, base["keys"] + (e - TS + 1))
                            for t in range(max(0, kt - NQ * g), NQ):
                                last = nc.tensor.transpose(turn[kt % TS][:, t * P:(t + 1) * P],
                                                           w[n % 2][t][:, kt * P:(kt + 1) * P], keep["ident"][:])
                            last.then_inc(turned, 1)

                        def product(kt):
                            up = HD * (kt % 2) if kd.halved(g) else 0
                            e = kd.key0[n] + kt
                            c0 = max(0, kt - NQ * g) * P
                            pe.wait_ge(copied, base["keys"] + (e + 1))
                            nc.tensor.matmul(o_ps[up:up + rows, c0:512], v[i][:, kt, lo:lo + rows],
                                             wT[kt % WS][:, c0:512], start=(kt < 1 + kd.halved(g)),
                                             stop=(kt >= nk - 1 - kd.halved(g))).then_inc(wT_used, 1)

                        rows, lo = (P, 0) if kd.diff else (HD, m * HD)
                        for kt in range(TS):
                            turn_keys(kt)
                        pe.wait_ge(o_copied, base["units"] + (n + 1))
                        for kt in range(0, nk, 2):
                            for ahead in (kt + TS, kt + TS + 1):
                                if ahead < nk:
                                    turn_keys(ahead)
                            product(kt)
                            product(kt + 1)

                    scores(0)
                    for n in range(kd.n):
                        if n + 1 < kd.n:
                            scores(n + 1)
                        weigh(n)

                pe.sem_inc(turned, 1)
                pe.wait_ge(zeroed, 4)
                passes(pe, body)

            @block.scalar
            def _(act):
                act.sem_inc(o_copied, 1)
                for i in range(2):
                    act.sem_inc(o_out[i], 1)
                act.wait_ge(lam_summed, 1)
                nc.scalar.activation(lam_exp[:], lam_sum[:], ACT.Exp).then_inc(lam_exped, 1)

                def body(kd, r, base):
                    def exps(n, tiles):
                        i, m, g = kd.units[n]
                        for t in tiles:
                            for mm in kd.maps:
                                act.wait_ge(shift_ready, base["rows"] + (n * kd.rows + t * len(kd.maps) + mm + 1))
                                row = (w1[t] if mm else w[n % 2][t])[:, 0:(NQ * g + t + 1) * P]
                                c = 2 * t + mm
                                nc.scalar.activation(row, row, ACT.Exp, bias=shift[:, n % 2, c:c + 1], scale=SCALE,
                                                     accum_out=total[:, n % 2, c:c + 1]).then_inc(exp_done, 1)

                    def put(n):
                        i, m, g = kd.units[n]
                        rows, lo = (P, 0) if kd.diff else (HD, m * HD)
                        act.wait_ge(wT_used, base["keys"] + kd.key0[n + 1])
                        act.wait_ge(o_out[n % 2], base["units"] * 8 + (1 + n // 2 * 16))
                        if kd.halved(g):
                            nc.scalar.copy(o[n % 2][0:rows], o_ps[rows:2 * rows]).then_inc(o_half, 1)
                        else:
                            nc.scalar.copy(o[n % 2][0:rows], o_ps[0:rows]).then_inc(o_copied, 1)
                        pair = r * 2 + (NP * kd.diff + i)
                        act.wait_ge(o_copied, base["units"] + (n + 2))
                        dst = io["mixT"][bass.ds(pair, 1), lo:lo + rows, g * 512:(g + 1) * 512]
                        act.dma_start(dst.rearrange("o p n -> (o p) n"), o[n % 2][0:rows]).then_inc(o_out[n % 2], 16)

                    exps(0, range(NQ))
                    for n in range(kd.n):
                        if n + 1 < kd.n:
                            exps(n + 1, (0, 1))

                        i, m, g = kd.units[n]
                        for kt in range(NQ * (g + 1)):
                            e = kd.key0[n] + kt
                            c0 = max(0, kt - NQ * g) * P
                            act.wait_ge(turned, base["keys"] + (e + 2))
                            if kt >= WS:
                                act.wait_ge(wT_used, base["keys"] + (e - WS + 1))
                            nc.scalar.copy(wT[kt % WS][:, c0:512], turn[kt % TS][:, c0:512]).then_inc(copied, 1)
                            if kt in (1, 3) and n + 1 < kd.n:
                                exps(n + 1, (2 + kt // 2,))
                        put(n)

                passes(act, body)
                for i in range(2):
                    act.wait_ge(o_out[i], 1 + 8 * PASSES * (kinds[0].n + kinds[1].n))

            @block.vector
            def _(dve):
                link = linker(dve, vec, Count(0))
                for m in range(2):
                    nc.vector.memset(q[0][(1 - m) * HD:(2 - m) * HD, m, :], 0.0).then_inc(zeroed, 1)
                dve.wait_ge(lam_in, 16)
                link(nc.vector.tensor_tensor(lam_prod[:].rearrange("p a n -> p (a n)"), lam_rows[:, 0:2 * HD],
                                             lam_rows[:, 2 * HD:4 * HD], ALU.mult))
                nc.vector.tensor_reduce(lam_sum[:], lam_prod[:], AX.X, ALU.add).then_inc(lam_summed, 1)
                dve.wait_ge(lam_exped, 1)
                link(nc.vector.tensor_scalar(keep["neg_lam"][:], lam_exp[:, 1:2], -LAMBDA_INIT, None, ALU.add))
                link(nc.vector.tensor_tensor(keep["neg_lam"][:], keep["neg_lam"][:], lam_exp[:, 0:1], ALU.subtract))

                def body(kd, r, base):
                    link = linker(dve, vec, Count(base["vec"] + 3))
                    dve.wait_ge(bias_in[kd.diff], 16)

                    def biased(n, t, mm, j):
                        i, m, g = kd.units[n]
                        tile = NQ * g + t
                        row = w1[t] if mm else w[n % 2][t]
                        rb = n * kd.rows + t * len(kd.maps) + mm
                        for b in range(g + 1):
                            lo, hi = b * 512, min((b + 1) * 512, (tile + 1) * P)
                            at = (NT - 1 - tile) * P + lo
                            dve.wait_ge(s_full, base["parts"] + (j + 1))
                            dve.sem_inc(vec_gate, 1)
                            nc.vector.tensor_tensor_reduce(
                                out=row[:, lo:hi], in0=s_ps[j % SS][:, 0:hi - lo],
                                in1=bias[kd.diff][:, at:at + hi - lo], scale=1.0, scalar=-BIG, op0=ALU.add,
                                op1=ALU.max, accum_out=(part[:, rb % 2, b:b + 1])).then_inc(s_used, 1)
                            j += 1
                        dve.wait_ge(s_used, base["parts"] + (SS + j))
                        src = part[:, rb % 2, 0:1]
                        if g:
                            link(nc.vector.tensor_reduce(top[:, rb % 2:rb % 2 + 1], part[:, rb % 2, 0:g + 1],
                                                         AX.X, ALU.max))
                            src = top[:, rb % 2:rb % 2 + 1]
                        c = 2 * t + mm
                        nc.vector.tensor_scalar(shift[:, n % 2, c:c + 1], src, -SCALE, None,
                                                ALU.mult).then_inc(shift_ready, 1)
                        return j

                    def normed(n, t):
                        i, m, g = kd.units[n]
                        c = 2 * t
                        dve.wait_ge(exp_done, base["rows"] + (n * kd.rows + (t + 1) * len(kd.maps)))
                        link(nc.vector.reciprocal(inv[:, n % 2, c:c + len(kd.maps)],
                                                  total[:, n % 2, c:c + len(kd.maps)]))
                        cols = (NQ * g + t + 1) * P
                        if not kd.diff:
                            row = w[n % 2][t][:, 0:cols]
                            nc.vector.tensor_scalar(row, row, inv[:, n % 2, c:c + 1], None,
                                                    ALU.mult).then_inc(w_ready, 1)
                            return
                        link(nc.vector.tensor_scalar(inv[:, n % 2, c + 1:c + 2], inv[:, n % 2, c + 1:c + 2],
                                                     keep["neg_lam"][:, 0:1], None, ALU.mult))
                        row = w[n % 2][t][:, 0:cols]
                        link(nc.vector.tensor_scalar(row, row, inv[:, n % 2, c:c + 1], None, ALU.mult))
                        nc.vector.scalar_tensor_tensor(out=row, in0=w1[t][:, 0:cols],
                                                       scalar=inv[:, n % 2, c + 1:c + 2], in1=row,
                                                       op0=ALU.mult, op1=ALU.add).then_inc(w_ready, 1)

                    def score_rows(n):
                        dve.wait_ge(turned, base["keys"] + (1 + (kd.key0[n - 1] if n >= 2 else 0)))
                        j = kd.part0[n]
                        for t in range(NQ):
                            for mm in kd.maps:
                                j = biased(n, t, mm, j)

                    def join(n):
                        if not kd.halved(kd.units[n][2]):
                            return
                        dve.wait_ge(o_half, base["halves"] + (sum(kd.halved(g) for _, _, g in kd.units[:n]) + 1))
                        nc.vector.tensor_tensor(o[n % 2][0:HD], o[n % 2][0:HD], o_ps[0:HD],
                                                ALU.add).then_inc(o_copied, 1)

                    for n in range(kd.n):
                        score_rows(n)
                        for t in range(NQ):
                            normed(n, t)
                        if n:
                            join(n - 1)
                    join(kd.n - 1)

                dve.sem_inc(s_used, SS)
                passes(dve, body)


CH = 8
SL = 4
ROWS = 32
NC = PAGES // CH + 1


def attend_decode(nc, io, keep):
    RG = 3
    with ExitStack() as ctx:
        sb = lambda n, s, d=F32: ctx.enter_context(nc.sbuf_tensor(n, s, d))
        ps = lambda n: ctx.enter_context(nc.psum_tensor(n, [P, 512], F32))
        sem = lambda n: ctx.enter_context(nc.semaphore(n))
        table = sb("c_table", [1, ND * PAGES], I32)
        k = [sb(f"c_k{i}", [P, CH, GW]) for i in range(RG)]
        v = [sb(f"c_v{i}", [P, CH, GW]) for i in range(RG)]
        kT = [sb(f"c_kT{i}", [P, NP, CH * P]) for i in range(RG)]
        q_rows = sb("c_q_rows", [P, 2, NP, SL * ROWS])
        v_new = sb("c_v_new", [TD, 2, ND, GW])
        bias_new = sb("c_bias_new", [P, 2, TD])
        bias_win = sb("c_bias_win", [P, 2 * P])
        own_head = sb("c_own_head", [P, 2, GW])
        same_row = sb("c_same_row", [P, P])
        token = sb("c_token", [P, TD])
        map_of = sb("c_map_of", [P, 2])
        sign = sb("c_sign", [P, 2])
        s_new = sb("c_s_new", [P, 2, TD])
        p_new = sb("c_p_new", [P, 2, TD])
        pT_new = sb("c_pT_new", [TD, 2, P])
        s_win = sb("c_s_win", [P, 2 * P])
        m = sb("c_m", [P, 2, 2])
        chunk_max = sb("c_chunk_max", [P, 1])
        shift = sb("c_shift", [P, RG])
        shift_new = sb("c_shift_new", [P, 2])
        alpha = sb("c_alpha", [P, RG])
        l_new = sb("c_l_new", [P, 2])
        l_chunk = sb("c_l_chunk", [P, RG])
        l = sb("c_l", [P, 2])
        prob = [sb(f"c_prob{i}", [P, 2 * P]) for i in range(RG)]
        pT = [sb(f"c_pT{i}", [P, 2 * P]) for i in range(RG)]
        acc = sb("c_acc", [P, 2, GW])
        m_row = sb("c_m_row", [2, ROWS])
        m_rows = sb("c_m_rows", [2, SL, ROWS])
        below = sb("c_below", [P, 2])
        weight = sb("c_weight", [P, 2])
        lw = sb("c_lw", [P, 2])
        coef = sb("c_coef", [P, 2])
        comb = sb("c_comb", [P, 2, TD])
        turn = [ps(f"c_turn{i}") for i in range(2)]
        s_ps = [ps(f"c_s{i}") for i in range(RG)]
        pT_ps, o_ps, x_ps = ps("c_pT_ps"), ps("c_o_ps"), ps("c_x_ps")

        const_in, table_in = sem("c_const_in"), sem("c_table_in")
        q_zero, q_ready = sem("c_q_zero"), sem("c_q_ready")
        k_in = [sem(f"c_k_in{i}") for i in range(RG)]
        v_in = [sem(f"c_v_in{i}") for i in range(RG)]
        turned = sem("c_turned")
        copied = [sem("c_copied_scalar"), sem("c_copied_vector")]
        s_full, shift_ready, exp_done = sem("c_s_full"), sem("c_shift_ready"), sem("c_exp_done")
        p_turned, pT_ready = sem("c_p_turned"), sem("c_pT_ready")
        o_full, o_added, l_added = sem("c_o_full"), sem("c_o_added"), sem("c_l_added")
        new_scored, new_shifted, new_exped = sem("c_new_scored"), sem("c_new_shifted"), sem("c_new_exped")
        new_turned, new_pT, new_full, new_taken = (sem("c_new_turned"), sem("c_new_pT"), sem("c_new_full"),
                                                   sem("c_new_taken"))
        m_turned, m_spread_ready, m_spread = sem("c_m_turned"), sem("c_m_spread_ready"), sem("c_m_spread")
        below_ready, weight_ready = sem("c_below_ready"), sem("c_weight_ready")
        lw_ready, l_summed, comb_ready = sem("c_lw_ready"), sem("c_l_summed"), sem("c_comb_ready")
        mixed, mix_kept = sem("c_mixed"), sem("c_mix_kept")
        vec = sem("c_vec")
        vec_gate, sp_gate, pool_gate = sem("c_vec_gate"), sem("c_sp_gate"), sem("c_pool_gate")

        kind = lambda c: 1 if c < NC - 1 else 0
        EV = NP * CH // 4
        LINKS = 3 + 2 * NC + 4
        FIRST_LINKS = 3
        X_M, X_L, X_O = P, P + 4, P + 8
        X_S = X_O + 2 * NP * TD
        X_P = X_S + 2 * TD

        def samples(eng, chunks, between):
            between(None, 0)
            with eng.Fori(0, ND - 1) as n:
                chunks(n)
                between(n, n + 1)
            chunks(ND - 1)
            between(ND - 1, None)

        with nc.Block() as block:
            def load(eng, n, c, dst, src, landed):
                i = c % RG
                if kind(c):
                    for g in range(CH):
                        page = eng.value_load(table[0:1, bass.ds(n * PAGES + (c * CH + g), 1)],
                                             min_val=0, max_val=NPHYS - 1)
                        eng.dma_start(dst[i][:, g, :], io[src[0]][bass.ds(page, 1)].rearrange(
                            "o p d -> (o p) d")).then_inc(landed[i], 16)
                    return
                rows = io[src[1]][bass.ds(n, 1)].rearrange("o t d -> (o t) d")
                for g in range(3):
                    by = rows[g * 512:(g + 1) * 512].rearrange("(a r) d -> a r d", r=16)[:, 0:TD, :]
                    eng.dma_start(dst[i][:, g, :], by).then_inc(landed[i], 16)
                near = rows[1536:2048].rearrange("(g p) d -> p g d", p=P)
                eng.dma_start(dst[i][:, 3:7, :], near).then_inc(landed[i], 16)
                eng.dma_start(dst[i][:, 7, :], rows[1920:2048]).then_inc(landed[i], 16)

            @block.sync
            def _(sp):
                sp.dma_start(table[:], io["page_table"]).then_inc(table_in, 16)
                sp.wait_ge(table_in, 16)

                with sp.Fori(0, ND) as n:
                    for c in range(NC):
                        sp.wait_ge(turned, n * (NC * EV) + (c + 1) * EV)
                        sp.sem_inc(sp_gate, 1)
                        load(sp, n, c, k, ("k_cache", "ka_state"), k_in)

            @block.gpsimd
            def _(pool):
                pool.wait_ge(table_in, 16)
                pool.wait_ge(k_in[0], 16 * CH)
                with pool.Fori(0, ND) as n:
                    for c in range(NC):
                        pool.wait_ge(o_full, n * NC + (c + 1))
                        pool.sem_inc(pool_gate, 1)
                        load(pool, n, c, v, ("v_cache", "va_state"), v_in)

            def landed(c, n):
                count = lambda cc: 16 * (CH if kind(cc) else 5)
                mine = [cc for cc in range(NC) if cc % RG == c % RG]
                return n * sum(map(count, mine)) + sum(count(cc) for cc in mine if cc <= c)

            @block.tensor
            def _(pe):
                pe.sem_inc(turned, RG * EV)
                pe.sem_inc(o_full, RG)
                pe.sem_inc(s_full, RG)
                pe.wait_ge(const_in, 16 * 8)

                def turn_keys(n, c, part=range(EV)):
                    i = c % RG
                    if part[0] == 0:
                        pe.wait_ge(k_in[i], landed(c, n))
                    for e in part:
                        p, half = e // 2, e % 2
                        pe.wait_ge(copied[e % 2], n * (NC * EV // 2) + ((c * EV + e) // 2 + 1))
                        for g in range(4):
                            last = nc.tensor.transpose(turn[e % 2][:, g * P:(g + 1) * P],
                                                       k[i][:, half * 4 + g, p * P:(p + 1) * P], keep["ident"][:])
                        last.then_inc(turned, 1)

                def scores(n, c):
                    i = c % RG
                    for e in range(2):
                        pe.wait_ge(copied[e], n * (NC * EV // 2) + ((c + 1) * EV // 2 + 1))
                    pe.wait_ge(exp_done, n * NC + (c + 1))
                    for p in range(NP):
                        for j in range(SL):
                            last = nc.tensor.matmul(
                                s_ps[i][ROWS * j:ROWS * (j + 1), 0:2 * P],
                                q_rows[:, kind(c), p, ROWS * j:ROWS * (j + 1)],
                                kT[i][:, p, j * 2 * P:(j + 1) * 2 * P], start=(p == 0), stop=(p == NP - 1))
                    last.then_inc(s_full, 1)

                def weigh(n, c):
                    i = c % RG
                    pe.wait_ge(exp_done, n * NC + (RG + c + 1))
                    pe.wait_ge(pT_ready, n * NC + (c + 1))
                    for a in range(2):
                        last = nc.tensor.transpose(pT_ps[:, a * P:(a + 1) * P],
                                                   prob[i][:, a * P:(a + 1) * P], keep["ident"][:])
                    last.then_inc(p_turned, 1)
                    pe.wait_ge(v_in[i], landed(c, n))
                    pe.wait_ge(pT_ready, n * NC + (c + 2))
                    if c:
                        pe.wait_ge(o_added, n * NC + c)
                    else:
                        pe.wait_ge(new_taken, n * 2 + 3)
                    for a in range(2):
                        for j in range(SL):
                            last = nc.tensor.matmul(
                                o_ps[ROWS * j:ROWS * (j + 1), :],
                                pT[i][:, a * P + ROWS * j:a * P + ROWS * (j + 1)],
                                v[i][:, 2 * j + a, :], start=(a == 0), stop=(a == 1))
                    last.then_inc(o_full, 1)

                def new_scores(n):
                    pe.wait_ge(q_ready, n * 2 + 2)
                    for kd in range(2):
                        for p in range(NP):
                            rhs = keep["ksT"][:, kd * NP + p, bass.ds(n * TD, TD)]
                            last = nc.tensor.matmul(x_ps[:, X_S + kd * TD:X_S + (kd + 1) * TD], q_rows[:, kd, p, :],
                                                    rhs, start=(p == 0), stop=(p == NP - 1))
                    last.then_inc(new_scored, 1)

                def new_values(n):
                    pe.wait_ge(new_exped, n * 2 + 2)
                    pe.wait_ge(mix_kept, n + 1)
                    for kd in range(2):
                        last = nc.tensor.transpose(x_ps[0:TD, X_P + kd * P:X_P + (kd + 1) * P], p_new[:, kd, :],
                                                   keep["ident"][:])
                    last.then_inc(new_turned, 1)
                    pe.wait_ge(new_pT, n + 1)
                    for kd in range(2):
                        pe.wait_ge(new_taken, n * 2 + (kd + 1))
                        nc.tensor.matmul(o_ps[:, :], pT_new[:, kd, :],
                                         v_new[:, kd, bass.ds(n, 1), :].rearrange("t o d -> t (o d)"),
                                         start=True, stop=True).then_inc(new_full, 1)

                def between(n, new):
                    if n is not None:
                        nc.tensor.transpose(x_ps[0:2, 0:P], m[:, 0, :], keep["ident"][:]).then_inc(m_turned, 1)
                    if new is not None:
                        turn_keys(new, 0, range(EV // 2))
                    if n is not None:
                        pe.wait_ge(m_spread_ready, n + 1)
                        nc.tensor.matmul(x_ps[:, X_M:X_M + 2], m_rows[:, :, :].rearrange("k j r -> k (j r)"),
                                         keep["ident"][0:2, 0:2], start=True, stop=True).then_inc(m_spread, 1)
                    if new is not None:
                        turn_keys(new, 0, range(EV // 2, EV))
                        if n is not None:
                            pe.wait_ge(below_ready, n + 1)
                        new_scores(new)
                    if n is not None:
                        pe.wait_ge(lw_ready, n + 1)
                        if new is not None:
                            pe.wait_ge(new_shifted, new + 1)
                        nc.tensor.matmul(x_ps[:, X_L:X_L + 2], same_row[:], lw[:], start=True,
                                         stop=True).then_inc(l_summed, 1)
                    if new is not None:
                        turn_keys(new, 1)
                    if n is not None:
                        pe.wait_ge(comb_ready, n + 1)
                        for kd in range(2):
                            for p in range(NP):
                                at = X_O + (kd * NP + p) * TD
                                last = nc.tensor.matmul(x_ps[:, at:at + TD], acc[:, kd, p * P:(p + 1) * P],
                                                        comb[:, kd, :], start=True, stop=True)
                        last.then_inc(mixed, 1)
                    if new is not None:
                        new_values(new)

                def chunks(n):
                    for c in range(NC):
                        if 1 <= c < NC - 1:
                            turn_keys(n, c + 1)
                        scores(n, c)
                        if c:
                            weigh(n, c - 1)
                    weigh(n, NC - 1)

                samples(pe, chunks, between)

            @block.scalar
            def _(act):
                consts = (("bias_new", bias_new), ("bias_win", bias_win), ("own_head", own_head),
                          ("same_row", same_row), ("token", token), ("map_of", map_of))
                for name, dst in consts:
                    act.dma_start(dst[:], io[name]).then_inc(const_in, 16)
                act.dma_start(v_new[:, 0], io["va_win"][:, WIN - TD:WIN, :].rearrange("n t d -> t n d")).then_inc(const_in, 16)
                act.dma_start(v_new[:, 1], io["vb_s"].rearrange("(n t) d -> t n d", t=TD)).then_inc(const_in, 16)
                act.sem_inc(copied[0], 1)
                act.sem_inc(exp_done, RG)
                act.sem_inc(pT_ready, 1)

                def copy_keys(n, c, part=range(0, EV, 2)):
                    i = c % RG
                    for e in part:
                        act.wait_ge(turned, n * (NC * EV) + ((RG + c) * EV + e + 1))
                        act.wait_ge(s_full, n * NC + (c + 1))
                        nc.scalar.copy(kT[i][:, e // 2, 0:512], turn[0][:]).then_inc(copied[0], 1)

                def exps(n, c):
                    i = c % RG
                    act.wait_ge(shift_ready, n * NC + (c + 1))
                    old = m[:, c % 2 if kind(c) else 1, kind(c):kind(c) + 1]
                    nc.scalar.activation(alpha[:, i:i + 1], old, ACT.Exp, bias=shift[:, i:i + 1], scale=SCALE)
                    src = s_ps[i][:, 0:2 * P] if kind(c) else s_win[:]
                    nc.scalar.activation(prob[i][:], src, ACT.Exp, bias=shift[:, i:i + 1], scale=SCALE,
                                         accum_out=l_chunk[:, i:i + 1]).then_inc(exp_done, 1)

                def copy_pT(n, c):
                    act.wait_ge(p_turned, n * NC + (c + 1))
                    nc.scalar.copy(pT[c % RG][:], pT_ps[:, 0:2 * P]).then_inc(pT_ready, 1)

                def between(n, new):
                    if new is not None:
                        copy_keys(new, 0, range(0, EV // 2, 2))
                    if n is not None:
                        act.wait_ge(below_ready, n + 1)
                        nc.scalar.activation(weight[:], below[:], ACT.Exp, scale=SCALE).then_inc(weight_ready, 1)
                    if new is not None:
                        copy_keys(new, 0, range(EV // 2, EV, 2))
                    if new is not None:
                        act.wait_ge(new_shifted, new + 1)
                        for kd in range(2):
                            nc.scalar.activation(p_new[:, kd, :], s_new[:, kd, :], ACT.Exp,
                                                 bias=shift_new[:, kd:kd + 1], scale=SCALE,
                                                 accum_out=l_new[:, kd:kd + 1]).then_inc(new_exped, 1)
                        copy_keys(new, 1)

                def chunks(n):
                    for c in range(NC):
                        if 1 <= c < NC - 1:
                            copy_keys(n, c + 1)
                        if c:
                            copy_pT(n, c - 1)
                        exps(n, c)
                    copy_pT(n, NC - 1)

                samples(act, chunks, between)

            @block.vector
            def _(dve):
                dve.wait_ge(const_in, 16 * 8)
                nc.vector.memset(q_rows[:].rearrange("p a b c -> p (a b c)"), 0.0).then_inc(q_zero, 1)
                nc.vector.tensor_scalar(sign[:], map_of[:], keep["neg_lam"][:, 0:1], None, ALU.mult).then_inc(q_zero, 1)
                dve.wait_ge(q_zero, 2)
                nc.vector.tensor_tensor(sign[:, 0:1], sign[:, 0:1], map_of[:, 1:2], ALU.add).then_inc(q_zero, 1)
                dve.wait_ge(q_zero, 3)
                dve.sem_inc(copied[1], 1)
                dve.sem_inc(new_taken, 1)
                dve.sem_inc(l_added, 1)
                dve.sem_inc(mix_kept, 1)

                def copy_keys(n, c, part=range(1, EV, 2)):
                    i = c % RG
                    for e in part:
                        dve.wait_ge(turned, n * (NC * EV) + ((RG + c) * EV + e + 1))
                        dve.wait_ge(s_full, n * NC + (c + 1))
                        nc.vector.tensor_copy(kT[i][:, e // 2, 512:1024], turn[1][:]).then_inc(copied[1], 1)

                def maxima(n, c, link):
                    i, kd = c % RG, kind(c)
                    dve.wait_ge(s_full, n * NC + (RG + c + 1))
                    if kd:
                        link(nc.vector.tensor_reduce(chunk_max[:], s_ps[i][:, 0:2 * P], AX.X, ALU.max))
                    else:
                        dve.sem_inc(vec_gate, 1)
                        link(nc.vector.tensor_tensor_reduce(
                            out=s_win[:], in0=s_ps[i][:, 0:2 * P], in1=bias_win[:], scale=1.0, scalar=-BIG,
                            op0=ALU.add, op1=ALU.max, accum_out=chunk_max[:]))
                    old, new = (c % 2, (c + 1) % 2) if kd else (1, 0)
                    link(nc.vector.tensor_tensor(m[:, new, kd:kd + 1], m[:, old, kd:kd + 1], chunk_max[:], ALU.max))
                    nc.vector.tensor_scalar(shift[:, i:i + 1], m[:, new, kd:kd + 1], -SCALE, None,
                                            ALU.mult).then_inc(shift_ready, 1)

                def add(n, c):
                    i, kd = c % RG, kind(c)
                    dve.wait_ge(exp_done, n * NC + (RG + c + 1))
                    dve.wait_ge(l_added, n * NC + (c + 1))
                    nc.vector.scalar_tensor_tensor(out=l[:, kd:kd + 1], in0=l[:, kd:kd + 1],
                                                   scalar=alpha[:, i:i + 1], in1=l_chunk[:, i:i + 1],
                                                   op0=ALU.mult, op1=ALU.add).then_inc(l_added, 1)
                    dve.wait_ge(o_full, n * NC + (RG + c + 1))
                    nc.vector.scalar_tensor_tensor(out=acc[:, kd, :], in0=acc[:, kd, :],
                                                   scalar=alpha[:, i:i + 1], in1=o_ps[:, :],
                                                   op0=ALU.mult, op1=ALU.add).then_inc(o_added, 1)

                def queries(n):
                    dve.wait_ge(s_full, n * NC + RG)
                    for c in range(2):
                        h = slice(c * HD, (c + 1) * HD)
                        for kd in range(2):
                            for g in range(NP):
                                src = keep["qsT"][h, kd * NP + g, bass.ds(n * TD, TD)]
                                at = g * 2 * TD + c * TD
                                dst = q_rows[h, kd, g, :].rearrange("p (j r) -> p j r", j=SL)[:, :, at:at + TD]
                                last = nc.vector.tensor_copy(dst, src.unsqueeze(1).broadcast_to([HD, SL, TD]))
                        last.then_inc(q_ready, 1)

                def between(n, new, link):
                    if n is not None:
                        add(n, NC - 1)
                        dve.wait_ge(m_turned, n + 1)
                        link(nc.vector.tensor_reduce(m_row[:], x_ps[0:2, 0:P].rearrange("k (j r) -> k r j", j=SL),
                                                     AX.X, ALU.max))
                        nc.vector.tensor_copy(m_rows[:], m_row[:].unsqueeze(1).broadcast_to([2, SL, ROWS])).then_inc(
                            m_spread_ready, 1)
                    if new is not None:
                        copy_keys(new, 0, range(1, EV // 2, 2))
                    if n is not None:
                        dve.wait_ge(m_spread, n + 1)
                        nc.vector.tensor_tensor(below[:], m[:, 0, :], x_ps[:, X_M:X_M + 2],
                                                ALU.subtract).then_inc(below_ready, 1)
                    if new is not None:
                        copy_keys(new, 0, range(EV // 2 + 1, EV, 2))
                    if n is not None:
                        dve.wait_ge(o_added, n * NC + NC)
                        nc.vector.tensor_tensor(acc[:], acc[:], own_head[:], ALU.mult)
                        dve.wait_ge(weight_ready, n + 1)
                        dve.wait_ge(l_added, n * NC + (NC + 1))
                        nc.vector.tensor_tensor(lw[:], l[:], weight[:], ALU.mult).then_inc(lw_ready, 1)
                    if new is not None:
                        dve.wait_ge(new_scored, new + 1)
                        link(nc.vector.tensor_tensor(s_new[:], x_ps[:, X_S:X_S + 2 * TD].rearrange(
                            "p (a b) -> p a b", a=2), bias_new[:], ALU.add))
                        if n is not None:
                            dve.wait_ge(below_ready, n + 1)
                        nc.vector.tensor_reduce(m[:, 1, 0:1], s_new[:, 0, :], AX.X, ALU.max)
                        link(nc.vector.tensor_reduce(m[:, 0, 1:2], s_new[:, 1, :], AX.X, ALU.max))
                        nc.vector.tensor_scalar(shift_new[:, 0:1], m[:, 1, 0:1], -SCALE, None, ALU.mult)
                        nc.vector.tensor_scalar(shift_new[:, 1:2], m[:, 0, 1:2], -SCALE, None,
                                                ALU.mult).then_inc(new_shifted, 1)
                    if n is not None:
                        dve.wait_ge(l_summed, n + 1)
                        link(nc.vector.reciprocal(coef[:], x_ps[:, X_L:X_L + 2]))
                        link(nc.vector.tensor_tensor(coef[:], coef[:], weight[:], ALU.mult))
                        link(nc.vector.tensor_tensor(coef[:, 1:2], coef[:, 1:2], sign[:, 0:1], ALU.mult))
                        for kd in range(2):
                            ins = nc.vector.tensor_scalar(comb[:, kd, :], token[:], coef[:, kd:kd + 1], None, ALU.mult)
                        ins.then_inc(comb_ready, 1)
                    if new is not None:
                        copy_keys(new, 1)
                    if n is not None:
                        dve.wait_ge(mixed, n + 1)
                        nc.vector.tensor_copy(keep["mixsT"][:, :, bass.ds(n * TD, TD)],
                                              x_ps[:, X_O:X_O + 2 * NP * TD].rearrange("p (g t) -> p g t", t=TD)
                                              ).then_inc(mix_kept, 1)
                    if new is not None:
                        dve.wait_ge(new_exped, new * 2 + 2)
                        link(nc.vector.tensor_scalar(l[:], l_new[:], 1.0 / SL, None, ALU.mult))
                        dve.wait_ge(new_turned, new + 1)
                        nc.vector.tensor_scalar(pT_new[:], x_ps[0:TD, X_P:X_P + 2 * P].rearrange(
                            "t (a b) -> t a b", a=2), 1.0 / SL, None, ALU.mult).then_inc(new_pT, 1)
                        for kd in range(2):
                            dve.wait_ge(new_full, new * 2 + kd + 1)
                            nc.vector.tensor_copy(acc[:, kd, :], o_ps[:, :]).then_inc(new_taken, 1)
                        dve.wait_ge(new_taken, new * 2 + 3)

                def chunks(n, new, link):
                    for c in range(NC):
                        if 1 <= c < NC - 1:
                            copy_keys(n, c + 1)
                        maxima(n, c, link)
                        if c:
                            add(n, c - 1)
                    if new is not None:
                        queries(new)

                queries(0)
                between(None, 0, linker(dve, vec, Count(0)))
                with dve.Fori(0, ND - 1) as n:
                    count = Count(n * LINKS + FIRST_LINKS)
                    link = linker(dve, vec, count)
                    chunks(n, n + 1, link)
                    between(n, n + 1, link)
                    assert count.n == LINKS, count.n
                link = linker(dve, vec, Count((ND - 1) * LINKS + FIRST_LINKS))
                chunks(ND - 1, None, link)
                between(ND - 1, None, link)


def mlp(nc, io, keep):
    F32R = mybir.dt.float32r
    W = 416
    NB = (S + NS) // W
    TB = 4
    TT = W // TB
    GC = 256
    NF = GC // P
    OG, UG = D // GC, FF // GC
    SG = OG + UG
    NH = NP
    DB = 3
    with ExitStack() as ctx:
        sb = lambda n, s, d=F32: ctx.enter_context(nc.sbuf_tensor(n, s, d))
        ps = lambda n: ctx.enter_context(nc.psum_tensor(n, [P, 512], F32))
        sem = lambda n: ctx.enter_context(nc.semaphore(n))
        up_raw = [sb(f"d_up_raw{i}", [P, KC, GC]) for i in range(2)]
        up_hi = [sb(f"d_up_hi{i}", [P, KC, GC], F32R) for i in range(2)]
        up_lo = [sb(f"d_up_lo{i}", [P, KC, GC], F32R) for i in range(2)]
        down_raw = sb("d_down_raw", [P, NF, D])
        down_hi = [sb(f"d_down_hi{i}", [P, NF, D], F32R) for i in range(2)]
        down_lo = [sb(f"d_down_lo{i}", [P, NF, D], F32R) for i in range(2)]
        a_hi = sb("d_a_hi", [P, KC, W], F32R)
        a_lo = sb("d_a_lo", [P, KC, W], F32R)
        u_hi = [sb(f"d_u_hi{i}", [P, NF, W], F32R) for i in range(2)]
        u_lo = [sb(f"d_u_lo{i}", [P, NF, W], F32R) for i in range(2)]
        mix = sb("d_mix", [P, KC, W])
        y = [sb(f"d_y{i}", [P, KC, W]) for i in range(2)]
        x_in = sb("d_x", [TT, TB, D])
        out = [sb(f"d_out{i}", [TT, D]) for i in range(2)]
        relu = sb("d_relu", [P, NF, W])
        u = sb("d_u", [P, NF, W])
        h = u
        square = sb("d_square", [P, 2, W])
        root = sb("d_root", [P, 2, W])
        gain_mlp, gain_last = sb("d_gain_mlp", [P, KC]), sb("d_gain_last", [P, KC])
        gain_head = sb("d_gain_head", [P, 1])
        ones = sb("d_ones", [P, P])
        eps = sb("d_eps", [P, 2])
        u_ps = [ps(f"d_ups{i}") for i in range(NF)]
        d_ps = [ps(f"d_dps{i}") for i in range(DB)]
        t_ps = [ps(f"d_tps{i}") for i in range(2)]
        s_ps = ps("d_sps")

        const_in, set_up = sem("d_const_in"), sem("d_set_up")
        up_in = [sem(f"d_up_in{i}") for i in range(2)]
        down_in = sem("d_down_in")
        up_hi_ready, up_lo_ready = sem("d_up_hi_ready"), sem("d_up_lo_ready")
        down_hi_ready, down_lo_ready = sem("d_down_hi_ready"), sem("d_down_lo_ready")
        mix_in, x_landed = sem("d_mix_in"), sem("d_x_landed")
        headed = sem("d_headed")
        h_ready = sem("d_h_ready")
        a_hi_ready, a_ready = sem("d_a_hi_ready"), sem("d_a_ready")
        u_full, out_added, relued = sem("d_u_full"), sem("d_out_added"), sem("d_relued")
        u_ready, u_hi_ready, u_split = sem("d_u_ready"), sem("d_u_hi_ready"), sem("d_u_split")
        d_full, d_used = sem("d_d_full"), sem("d_d_used")
        t_full, t_used = sem("d_t_full"), sem("d_t_used")
        square_ready, square_used = sem("d_square_ready"), sem("d_square_used")
        s_full, rooted = sem("d_s_full"), sem("d_rooted")
        inverted, root_used = sem("d_inverted"), sem("d_root_used")
        y_ready = sem("d_y_ready")
        stored = [sem(f"d_stored{i}") for i in range(2)]
        sp_gate, pool_gate = sem("d_sp_gate"), sem("d_pool_gate")

        col_group = lambda b, s: s + b * SG
        row_group = lambda b, g: g + b * UG
        turn_no = lambda b: b * KC + max(0, b - 1) * 2 * TB

        def wait(eng, sem, value):
            if not isinstance(value, int) or value > 0:
                eng.wait_ge(sem, value)

        def groups(eng, step):
            with eng.Fori(0, (UG - 4) // 2) as q:
                for i in range(2):
                    step(q * 2 + (2 + i), i)

        with nc.Block() as block:
            @block.sync
            def _(sp):
                def load_cols(b, s, i):
                    wait(sp, up_lo_ready, col_group(b, s) - 1)
                    sp.sem_inc(sp_gate, 1)
                    if isinstance(s, int):
                        name, g = ("w_out", s) if s < OG else ("w_up", s - OG)
                    else:
                        name, g = "w_up", s - OG
                    src = io[name].rearrange("(c p) (g n) -> g p c n", p=P, n=GC)[bass.ds(g, 1)]
                    sp.dma_start(up_raw[i][:], src.rearrange("o p c n -> (o p) c n")).then_inc(up_in[i], 16)

                def load_rows(b, g):
                    wait(sp, down_lo_ready, row_group(b, g))
                    sp.sem_inc(sp_gate, 1)
                    src = io["w_down"].rearrange("(g f p) n -> g p f n", p=P, f=NF)[bass.ds(g, 1)]
                    sp.dma_start(down_raw[:], src.rearrange("o p f n -> (o p) f n")).then_inc(down_in, 16)

                def load_mix(b):
                    mine = min(W, S - b * W)
                    sp.dma_start(mix[:, :, 0:mine], io["mixT"].rearrange("c p n -> p c n")[
                        :, :, b * W:b * W + mine]).then_inc(mix_in, 16)
                    if mine < W:
                        sp.dma_start(mix[:, :, mine:W], keep["mixsT"][:]).then_inc(mix_in, 16)

                def load_x(b):
                    if (b + 1) * W <= S:
                        src = io["x_prompt"][b * W:(b + 1) * W].rearrange("(t p) d -> p t d", p=TT)
                        sp.dma_start(x_in[:], src).then_inc(x_landed, 16)
                        return
                    whole, rest = (S - b * W) // TT, (S - b * W) % TT
                    src = io["x_prompt"][b * W:b * W + whole * TT].rearrange("(t p) d -> p t d", p=TT)
                    sp.dma_start(x_in[:, 0:whole], src).then_inc(x_landed, 16)
                    sp.dma_start(x_in[0:rest, whole], io["x_prompt"][S - rest:S]).then_inc(x_landed, 16)
                    sp.dma_start(x_in[rest:TT, whole], io["x_sample"]).then_inc(x_landed, 16)

                load_mix(0)
                load_cols(0, 0, 0)
                for name, dst in (("norm_mlp", gain_mlp), ("subln_gain", gain_head), ("final_norm", gain_last)):
                    sp.dma_start(dst[:], io[name]).then_inc(const_in, 16)
                load_x(0)
                load_cols(0, 1, 1)
                load_rows(0, 0)
                for b in range(NB):
                    for s in range(2, OG + 2):
                        load_cols(b, s, s % 2)
                    if b + 1 < NB:
                        sp.wait_ge(a_ready, b * 2 * KC + KC)
                        load_mix(b + 1)
                        sp.wait_ge(t_full, turn_no(b) + KC)
                        load_x(b + 1)

                    def step(g, i):
                        if not isinstance(g, int) or g + 1 < UG:
                            load_rows(b, g + 1)
                        elif b + 1 < NB:
                            load_rows(b + 1, 0)
                        if not isinstance(g, int) or g + 2 < UG:
                            load_cols(b, g + (OG + 2), i)
                        elif b + 1 < NB:
                            load_cols(b + 1, g + 2 - UG, i)

                    step(0, 0)
                    step(1, 1)
                    groups(sp, step)
                    step(UG - 2, 0)
                    step(UG - 1, 1)

            @block.gpsimd
            def _(pool):
                with pool.Fori(0, NB * SG // 2) as q:
                    for i in range(2):
                        pool.wait_ge(up_hi_ready, q * 2 + (i + 1))
                        pool.sem_inc(pool_gate, 1)
                        nc.gpsimd.tensor_tensor(up_lo[i][:], up_raw[i][:], up_hi[i][:].bitcast(F32),
                                                ALU.subtract).then_inc(up_lo_ready, 1)

            def three(dst, w_hi, w_lo, x_hi, x_lo, first, last):
                nc.tensor.matmul(dst, w_hi, x_hi, start=first, stop=False)
                nc.tensor.matmul(dst, w_hi, x_lo, start=False, stop=False)
                return nc.tensor.matmul(dst, w_lo, x_hi, start=False, stop=last)

            @block.tensor
            def _(pe):
                squares, sums = Count(), Count()

                def columns(b, s, i, f, ready):
                    if f == 0:
                        pe.wait_ge(up_lo_ready, col_group(b, s) + 1)
                    for c in range(KC):
                        if ready is not None:
                            pe.wait_ge(a_ready, ready + c + 1)
                        at = slice(f * P, (f + 1) * P)
                        last = three(u_ps[f][:, 0:W], up_hi[i][:, c, at], up_lo[i][:, c, at], a_hi[:, c, :],
                                     a_lo[:, c, :], c == 0, c == KC - 1)
                    last.then_inc(u_full, 1)

                def project_out(b, c):
                    s, f = c // NF, c % NF
                    if s == 0:
                        wait(pe, relued, b * UG * NF + f - 1)
                    else:
                        pe.wait_ge(out_added, b * KC + c - 1)
                    columns(b, s, s % 2, f, b * 2 * KC if c == 0 else None)

                def up(b, g, i):
                    for f in range(NF):
                        if isinstance(g, int) and g == 0:
                            pe.wait_ge(out_added, b * KC + KC - NF + f + 1)
                        else:
                            pe.wait_ge(relued, g * NF + (b * UG * NF + f - 1))
                        first = isinstance(g, int) and g == 0 and f == 0
                        columns(b, g + OG, i, f, b * 2 * KC + KC if first else None)

                def down(b, g, i, between=lambda c: None):
                    pe.wait_ge(down_lo_ready, row_group(b, g) + 1)
                    for c in range(KC):
                        before = c - DB if c >= DB else max(e for e in range(KC) if e % DB == c) - KC
                        wait(pe, d_used, row_group(b, g) * KC + (before + 1))
                        for f in range(NF):
                            if c == 0:
                                pe.wait_ge(u_split, row_group(b, g) * NF + (f + 1))
                            at = slice(c * P, (c + 1) * P)
                            last = three(d_ps[c % DB][:, 0:W], down_hi[i][:, f, at], down_lo[i][:, f, at],
                                         u_hi[i][:, f, :], u_lo[i][:, f, :], f == 0, f == NF - 1)
                        last.then_inc(d_full, 1)
                        between(c)

                def turn_bank(n):
                    wait(pe, t_used, n - 1)
                    return t_ps[n % 2]

                def turn_x(b, c):
                    if c == 0:
                        pe.wait_ge(x_landed, 16 * (b + 1) + (32 if b == NB - 1 else 0))
                    dst = turn_bank(turn_no(b) + c)
                    for t in range(TB):
                        last = nc.tensor.transpose(dst[:, t * TT:(t + 1) * TT], x_in[:, t, c * P:(c + 1) * P],
                                                   keep["ident"][0:TT, 0:TT])
                    last.then_inc(t_full, 1)

                def turn_y(b, j):
                    if j < 2:
                        pe.wait_ge(y_ready, b * KC + 4 * (j + 1))
                    dst = turn_bank(turn_no(b + 1) + (KC if b + 1 < NB else 0) + j)
                    t, half = j // 2, j % 2
                    for c in range(4):
                        last = nc.tensor.transpose(dst[0:TT, c * P:(c + 1) * P],
                                                   y[b % 2][:, 4 * half + c, t * TT:(t + 1) * TT], keep["ident"][:])
                    last.then_inc(t_full, 1)

                def add_square(first, last):
                    if first:
                        wait(pe, rooted, sums.n)
                        sums.up()
                    n = squares.up()
                    pe.wait_ge(square_ready, n)
                    ins = nc.tensor.matmul(s_ps[:, 0:W], ones[:], square[:, (n - 1) % 2, :], start=first, stop=last)
                    ins.then_inc(square_used, 1)
                    if last:
                        pe.wait_ge(square_used, n)
                        pe.sem_inc(s_full, 1)

                pe.wait_ge(set_up, 4)
                for _ in range(NH):
                    add_square(True, True)
                for b in range(NB):
                    for c in range(KC):
                        turn_x(b, c)
                        project_out(b, c)
                        if c >= 2:
                            add_square(c == 2, False)
                    add_square(False, False)
                    add_square(False, True)
                    if b:
                        for c in range(KC):
                            add_square(c == 0, c == KC - 1)
                    up(b, 0, 0)
                    up(b, 1, 1)
                    down(b, 0, 0)
                    up(b, 2, 0)
                    down(b, 1, 1, (lambda c: turn_y(b - 1, c)) if b else lambda c: None)

                    def step(g, i):
                        up(b, g + 1, (i + 1) % 2)
                        down(b, g, i)

                    groups(pe, step)
                    up(b, UG - 1, 1)
                    down(b, UG - 2, 0, (lambda c: c % 2 and add_square(True, True)) if b + 1 < NB else lambda c: None)
                    down(b, UG - 1, 1)
                for c in range(KC):
                    add_square(c == 0, c == KC - 1)
                for c in range(KC):
                    turn_y(NB - 1, c)

            @block.scalar
            def _(act):
                squares, sums, stores = Count(), Count(), [Count(), Count()]

                def cols_hi(b, s, i):
                    n = col_group(b, s)
                    half = b * (SG // 2) + s // 2 + 1 if isinstance(s, int) else None
                    act.wait_ge(up_in[i], 16 * half if half else s * 8 + (b * SG * 8 - 8 * i + 16))
                    wait(act, u_full, n * NF - NF)
                    nc.scalar.copy(up_hi[i][:], up_raw[i][:]).then_inc(up_hi_ready, 1)

                def rows_hi(b, g, i):
                    n = row_group(b, g)
                    act.wait_ge(down_in, n * 16 + 16)
                    wait(act, d_full, n * KC - KC)
                    nc.scalar.copy(down_hi[i][:], down_raw[:]).then_inc(down_hi_ready, 1)

                def squared(src):
                    n = squares.up()
                    wait(act, square_used, n - 2)
                    nc.scalar.activation(square[:, (n - 1) % 2, :], src, ACT.Square).then_inc(square_ready, 1)

                def take_root(scale, which):
                    n = sums.up()
                    act.wait_ge(s_full, n)
                    wait(act, root_used, n - 2)
                    nc.scalar.activation(root[:, (n - 1) % 2, :], s_ps[:, 0:W], ACT.Sqrt, bias=eps[:, which:which + 1],
                                         scale=scale).then_inc(rooted, 1)

                def heads(b, between=lambda: None):
                    act.wait_ge(mix_in, 16 * (b + 1) + (16 if b == NB - 1 else 0))
                    squared(mix[:, NP, :])
                    for hd in range(NH):
                        if hd + 1 < NH:
                            squared(mix[:, NP + hd + 1, :])
                        if hd == 0:
                            between()
                        take_root(1.0 / P, 1)

                def mix_hi(b, c):
                    if c >= NP:
                        act.wait_ge(headed, b * NH + c - NP + 1)
                    nc.scalar.copy(a_hi[:, c, :], mix[:, c, :]).then_inc(a_hi_ready, 1)

                def relus(b, g):
                    for f in range(NF):
                        act.wait_ge(u_full, (g + (b * SG + OG)) * NF + (f + 1))
                        wait(act, u_ready, row_group(b, g) * NF + (f - 1))
                        nc.scalar.activation(relu[:, f, :], u_ps[f][:, 0:W], ACT.Relu).then_inc(relued, 1)

                def put(b, j):
                    n = turn_no(b + 1) + (KC if b + 1 < NB else 0) + j
                    t, half = j // 2, j % 2
                    act.wait_ge(t_full, n + 1)
                    if half == 0:
                        wait(act, stored[t % 2], stores[t % 2].n)
                    nc.scalar.copy(out[t % 2][:, half * 512:(half + 1) * 512], t_ps[n % 2][0:TT, :]).then_inc(t_used, 1)
                    if half:
                        act.wait_ge(t_used, n + 1)
                        at = b * W + t * TT
                        rest = min(TT, S - at)
                        act.dma_start(io["y_p"][at:at + rest], out[t % 2][0:rest]).then_inc(stored[t % 2], 16)
                        stores[t % 2].up(16)
                        if rest < TT:
                            act.dma_start(io["y_s"], out[t % 2][rest:TT]).then_inc(stored[t % 2], 16)
                            stores[t % 2].up(16)

                act.wait_ge(set_up, 4)
                heads(0, lambda: cols_hi(0, 0, 0))
                for c in range(KC):
                    mix_hi(0, c)
                cols_hi(0, 1, 1)
                rows_hi(0, 0, 0)
                for b in range(NB):
                    for c in range(KC):
                        act.wait_ge(t_full, turn_no(b) + c + 1)
                        nc.scalar.copy(y[b % 2][:, c, :], t_ps[(turn_no(b) + c) % 2][:, 0:W]).then_inc(t_used, 1)
                        if c:
                            act.wait_ge(out_added, b * KC + c)
                            squared(y[b % 2][:, c - 1, :])
                        if c % 2:
                            cols_hi(b, c // 2 + 2, c // 2 % 2)
                    act.wait_ge(out_added, b * KC + KC)
                    squared(y[b % 2][:, KC - 1, :])
                    take_root(1.0 / D, 0)
                    if b:
                        act.wait_ge(d_used, b * UG * KC)
                    for c in range(KC):
                        if b:
                            squared(y[(b - 1) % 2][:, c, :])
                        act.wait_ge(h_ready, b * KC + c + 1)
                        nc.scalar.copy(a_hi[:, c, :], h[:, c % 2, :]).then_inc(a_hi_ready, 1)
                    if b:
                        take_root(1.0 / D, 0)
                    relus(b, 0)
                    rows_hi(b, 1, 1)
                    relus(b, 1)
                    cols_hi(b, OG + 2, 0)
                    rows_hi(b, 2, 0)
                    relus(b, 2)
                    cols_hi(b, OG + 3, 1)
                    if b:
                        for j in range(2 * TB):
                            put(b - 1, j)

                    def step(g, i):
                        rows_hi(b, g + 1, (i + 1) % 2)
                        relus(b, g + 1)
                        cols_hi(b, g + (OG + 2), i)

                    groups(act, step)
                    rows_hi(b, UG - 1, 1)
                    relus(b, UG - 1)
                    if b + 1 < NB:
                        heads(b + 1)
                        cols_hi(b + 1, 0, 0)
                        act.wait_ge(u_full, (b + 1) * SG * NF)
                        for c in range(KC):
                            mix_hi(b + 1, c)
                        cols_hi(b + 1, 1, 1)
                        rows_hi(b + 1, 0, 0)
                act.wait_ge(d_used, NB * UG * KC)
                for c in range(KC):
                    squared(y[(NB - 1) % 2][:, c, :])
                take_root(1.0 / D, 0)
                for j in range(2 * TB):
                    put(NB - 1, j)
                for i in range(2):
                    act.wait_ge(stored[i], stores[i].n)

            @block.vector
            def _(dve):
                sums = Count()
                nc.vector.memset(ones[:], 1.0).then_inc(set_up, 1)
                nc.vector.memset(eps[:, 0:1], EPS).then_inc(set_up, 1)
                nc.vector.memset(eps[:, 1:2], SUB_EPS).then_inc(set_up, 1)
                dve.wait_ge(const_in, 48)
                nc.vector.tensor_scalar(gain_head[:], gain_head[:], 1.0 - LAMBDA_INIT, None, ALU.mult).then_inc(set_up, 1)
                dve.wait_ge(set_up, 4)

                def invert():
                    n = sums.up()
                    r = root[:, (n - 1) % 2, :]
                    dve.wait_ge(rooted, n)
                    nc.vector.reciprocal(r, r).then_inc(inverted, 1)
                    dve.wait_ge(inverted, n)
                    return r

                def scale(dst, src, gain, r):
                    return nc.vector.scalar_tensor_tensor(out=dst, in0=src, scalar=gain, in1=r, op0=ALU.mult, op1=ALU.mult)

                def head(b, hd):
                    r = invert()
                    part = mix[:, NP + hd, :]
                    scale(part, part, gain_head[:, 0:1], r).then_inc(headed, 1)
                    dve.wait_ge(headed, b * NH + hd + 1)
                    dve.sem_inc(root_used, 1)

                def a_low(n, c, src):
                    dve.wait_ge(a_hi_ready, n + c + 1)
                    nc.vector.tensor_tensor(a_lo[:, c, :], src, a_hi[:, c, :].bitcast(F32),
                                            ALU.subtract).then_inc(a_ready, 1)

                def rows_lo(b, g, i):
                    dve.wait_ge(down_hi_ready, row_group(b, g) + 1)
                    nc.vector.tensor_tensor(down_lo[i][:], down_raw[:], down_hi[i][:].bitcast(F32),
                                            ALU.subtract).then_inc(down_lo_ready, 1)

                def split_u(b, g, i):
                    for f in range(NF):
                        n = row_group(b, g) * NF + (f + 1)
                        dve.wait_ge(relued, n)
                        nc.vector.tensor_tensor(u[:, f, :], relu[:, f, :], relu[:, f, :], ALU.mult).then_inc(u_ready, 1)
                        dve.wait_ge(u_ready, n)
                        if not (isinstance(g, int) and b == 0 and g < 2):
                            dve.wait_ge(d_full, row_group(b, g) * KC - KC)
                        nc.vector.tensor_copy(u_hi[i][:, f, :], u[:, f, :]).then_inc(u_hi_ready, 1)
                        dve.wait_ge(u_hi_ready, n)
                        nc.vector.tensor_tensor(u_lo[i][:, f, :], u[:, f, :], u_hi[i][:, f, :].bitcast(F32),
                                                ALU.subtract).then_inc(u_split, 1)

                def add(b, g, c):
                    part = y[b % 2][:, c, :]
                    dve.wait_ge(d_full, row_group(b, g) * KC + (c + 1))
                    nc.vector.tensor_tensor(part, part, d_ps[c % DB][:, 0:W], ALU.add).then_inc(d_used, 1)

                def finish(b, r, before=lambda c: None):
                    for c in range(KC):
                        before(c)
                        part = y[b % 2][:, c, :]
                        scale(part, part, gain_last[:, c:c + 1], r).then_inc(y_ready, 1)
                    dve.wait_ge(y_ready, (b + 1) * KC)
                    dve.sem_inc(root_used, 1)

                for hd in range(NH):
                    head(0, hd)
                for c in range(KC):
                    a_low(0, c, mix[:, c, :])
                rows_lo(0, 0, 0)
                for b in range(NB):
                    for c in range(KC):
                        part = y[b % 2][:, c, :]
                        dve.wait_ge(t_used, turn_no(b) + c + 1)
                        dve.wait_ge(u_full, b * SG * NF + c + 1)
                        nc.vector.tensor_tensor(part, part, u_ps[c % NF][:, 0:W], ALU.add).then_inc(out_added, 1)
                    r = invert()
                    n = b * 2 * KC + KC
                    for c in range(KC + 1):
                        if c < KC:
                            if c >= 2:
                                dve.wait_ge(a_ready, n + c - 1)
                            scale(h[:, c % 2, :], y[b % 2][:, c, :], gain_mlp[:, c:c + 1], r).then_inc(h_ready, 1)
                        if c:
                            a_low(n, c - 1, h[:, (c - 1) % 2, :])
                    dve.sem_inc(root_used, 1)
                    split_u(b, 0, 0)
                    r = invert() if b else None
                    rows_lo(b, 1, 1)
                    split_u(b, 1, 1)
                    if b:
                        finish(b - 1, r, lambda c: add(b, 0, c))
                    else:
                        for c in range(KC):
                            add(b, 0, c)
                    rows_lo(b, 2, 0)
                    split_u(b, 2, 0)
                    for c in range(KC):
                        add(b, 1, c)

                    def step(g, i):
                        rows_lo(b, g + 1, (i + 1) % 2)
                        split_u(b, g + 1, (i + 1) % 2)
                        for c in range(KC):
                            add(b, g, c)

                    groups(dve, step)
                    rows_lo(b, UG - 1, 1)
                    split_u(b, UG - 1, 1)
                    for c in range(KC):
                        add(b, UG - 2, c)
                        if b + 1 < NB and c % 2 and c > 1:
                            head(b + 1, c // 2 - 1)
                    if b + 1 < NB:
                        head(b + 1, NH - 1)
                    for c in range(KC):
                        add(b, UG - 1, c)
                        if b + 1 < NB:
                            a_low((b + 1) * 2 * KC, c, mix[:, c, :])
                    if b + 1 < NB:
                        rows_lo(b + 1, 0, 0)
                dve.wait_ge(d_used, NB * UG * KC)
                finish(NB - 1, invert())


def build(nc, io):
    with ExitStack() as ctx:
        sb = lambda n, s: ctx.enter_context(nc.sbuf_tensor(n, s, F32))
        keep = {"ident": sb("ident", [P, P]), "qsT": sb("qsT", [P, 2 * NP, NS]), "ksT": sb("ksT", [P, 2 * NP, NS]),
                "mixsT": sb("mixsT", [P, 2 * NP, NS]), "neg_lam": sb("neg_lam", [P, 1])}
        for name, dt in (("qT", F32), ("kT", F32), ("mixT", F32)):
            io[name] = nc.dram_tensor(name, [2 * NP, P, S], dt, kind="Internal").ap()
        project(nc, io, keep)
        attend_prompt(nc, io, keep)
        attend_decode(nc, io, keep)
        mlp(nc, io, keep)


def rope_tables():
    half = ROT // 2
    inv = np.float32(THETA) ** (-np.arange(half, dtype=np.float32) * np.float32(2.0) / np.float32(ROT))
    pos = np.zeros((NT + 1, P), np.float32)
    pos[:NT] = np.arange(S).reshape(NT, P)
    pos[NT, :NS] = PAGES * PAGE + np.arange(NS) % TD
    ang = (pos[:, :, None] * inv).astype(np.float32).astype(np.float64)
    cos, sin = np.cos(ang), np.sin(ang)
    lay = lambda a: np.ascontiguousarray(a.transpose(1, 0, 2).astype(np.float32))
    return lay(np.concatenate([cos, cos], -1)), lay(np.concatenate([-sin, sin], -1))


def log_reads(dist):
    reads = sum(((dist >= 0) & (dist <= w) & (dist % d == 0)).astype(np.float64) for w, d in BRANCHES)
    return np.where(reads > 0, np.log(np.maximum(reads, 1)) / SCALE, NEG).astype(np.float32)


def decode_constants():
    row = np.arange(SL * ROWS)
    slot, pair, which, t = row // ROWS, row % ROWS // (2 * TD), row % (2 * TD) // TD, row % TD
    key = np.arange(P)
    pos = np.stack([16 * (g * 32 + key // TD) + key % TD for g in range(3)]
                   + [1536 + g * P + key for g in range(4)] + [np.full(P, 2 * WIN)])
    pos = pos.reshape(SL, 2 * P)[slot]
    win = log_reads(np.where(pos < WIN, WIN + t[:, None] - pos, -1))
    ago = t[:, None] - np.arange(TD)[None, :]
    new = np.stack([log_reads(ago), np.where(ago >= 0, 0, NEG).astype(np.float32)], 1)
    col = np.arange(GW)
    same_pair = pair[:, None] == col[None, :] // P
    own = np.stack([same_pair & (which[:, None] == col[None, :] % P // HD), same_pair], 1)
    f = lambda a: np.ascontiguousarray(a.astype(np.float32))
    return {"bias_win": f(win), "bias_new": f(new), "own_head": f(own),
            "same_row": f(row[:, None] % ROWS == row[None, :] % ROWS),
            "token": f(t[:, None] == np.arange(TD)[None, :]), "map_of": f(np.stack([which == 1, which == 0], 1))}


def constants():
    cos, sin = rope_tables()
    dist = (NT - 1) * P + np.arange(P)[:, None] - np.arange(S)[None, :]
    return {"ident": np.eye(P, dtype=np.float32), "cos": cos, "sin": sin,
            "bias_dilated": log_reads(dist), "bias_causal": np.where(dist >= 0, 0, NEG).astype(np.float32),
            **decode_constants()}


OUTPUTS = (("y_p", (1, S, D)), ("y_s", (ND, TD, D)), ("kb_p", (1, 1, S, 4, 2 * HD)), ("vb_p", (1, 1, S, 4, 2 * HD)),
           ("ka_p", (1, 1, S, 8, HD)), ("va_p", (1, 1, S, 8, HD)),
           ("kb_s", (1, ND, TD, 4, 2 * HD)), ("vb_s", (1, ND, TD, 4, 2 * HD)),
           ("ka_win", (1, ND, WIN, 8, HD)), ("va_win", (1, ND, WIN, 8, HD)))
SHAPES = {"y_p": (S, D), "y_s": (NS, D), "kb_p": (S, GW), "vb_p": (S, GW), "ka_p": (S, GW), "va_p": (S, GW),
          "kb_s": (NS, GW), "vb_s": (NS, GW), "ka_win": (ND, WIN, GW), "va_win": (ND, WIN, GW)}


def lay_out(inputs):
    a = {k: np.asarray(v) for k, v in inputs.items()}
    by_chunk = lambda v: np.ascontiguousarray(v.reshape(-1, P).T)
    out = {
        "x_prompt": a["x_prompt"].reshape(S, D), "x_sample": a["x_sample"].reshape(NS, D),
        "ka_state": a["state_win_k"].reshape(ND, WIN, GW), "va_state": a["state_win_v"].reshape(ND, WIN, GW),
        "k_cache": a["cache_diff_k"].reshape(NPHYS, PAGE, GW), "v_cache": a["cache_diff_v"].reshape(NPHYS, PAGE, GW),
        "page_table": a["page_table"].reshape(1, ND * PAGES),
        "norm_attn": by_chunk(a["norm_attn"]), "norm_mlp": by_chunk(a["norm_mlp"]),
        "final_norm": by_chunk(a["final_norm"]), "subln_gain": a["subln_gain"].reshape(P, 1),
        "lambdas": np.stack([a[k].reshape(HD) for k in ("lambda_q1", "lambda_q2", "lambda_k1", "lambda_k2")]).reshape(1, 4 * HD),
        "w_in": a["w_in"][0], "w_out": a["w_out"][0], "w_up": a["w_up"][0], "w_down": a["w_down"][0],
    }
    out.update(constants())
    return {k: np.ascontiguousarray(v) for k, v in out.items()}


def kernel(**inputs):
    import concourse.bacc as bacc
    from concourse.bass_utils import run_bass_kernel_spmd

    nc = bacc.Bacc("TRN2", target_bir_lowering=False, num_devices=1)
    arrays = lay_out(inputs)
    io = {k: nc.dram_tensor("in_" + k, v.shape, mybir.dt.from_np(v.dtype), kind="ExternalInput").ap()
          for k, v in arrays.items()}
    for k, _ in OUTPUTS:
        io[k] = nc.dram_tensor("out_" + k, SHAPES[k], F32, kind="ExternalOutput").ap()
    build(nc, io)
    r = run_bass_kernel_spmd(nc, [{"in_" + k: v for k, v in arrays.items()}], core_ids=[0])
    return tuple(np.asarray(r.results[0]["out_" + k]).reshape(s) for k, s in OUTPUTS)
```
